# Optimizing a Trainium2 kernel written in Bass

```python
import math
import jax, jax.numpy as jnp
from jax import lax
import numpy as np
import jax
import jax.numpy as jnp

D_MODEL = 1024
BATCH = 1
SEQ = 1024
DEPTH = 2

N_MIXERS = 2
EPS = 1e-6

A_EXPAND = 2
A_WIDTH = A_EXPAND * D_MODEL
A_CHUNK = 128
A_HEADS = 16
A_HEAD_DIM = A_WIDTH // A_HEADS

B_GROUPS = ((128, 1), (512, 4), (2048, 16))
B_N_GROUPS = len(B_GROUPS)
B_HEADS = 16
B_HEAD_DIM = 64
B_WIDTH = B_HEADS * B_HEAD_DIM
B_QKV = B_N_GROUPS * 3 * B_WIDTH
B_TOTAL_HEADS = B_N_GROUPS * B_HEADS

REL_BUCKETS = 32
REL_EXACT = 8
REL_MAX_DISTANCE = 1024

N_A_LAYERS = (DEPTH + 1) // 2
N_B_LAYERS = DEPTH // 2
NEG_INF = -1e30


def rms_norm(x, g):
    xf = x.astype(jnp.float32)
    y = xf * lax.rsqrt(jnp.mean(xf * xf, axis=-1, keepdims=True) + EPS)
    return (y * g.astype(jnp.float32)).astype(x.dtype)

def layer_norm(x, g, b):
    xf = x.astype(jnp.float32)
    mu = jnp.mean(xf, axis=-1, keepdims=True)
    xc = xf - mu
    y = xc * lax.rsqrt(jnp.mean(xc * xc, axis=-1, keepdims=True) + EPS)
    return (y * g.astype(jnp.float32) + b.astype(jnp.float32)).astype(x.dtype)

def t5_bucket(rel):
    half = REL_BUCKETS // 2
    ret = jnp.where(rel > 0, half, 0)
    n = jnp.abs(rel)
    nf = jnp.maximum(n, 1).astype(jnp.float32)
    large = REL_EXACT + (jnp.log(nf / REL_EXACT) / math.log(REL_MAX_DISTANCE / REL_EXACT)
                         * (half - REL_EXACT)).astype(jnp.int32)
    large = jnp.minimum(large, half - 1)
    return ret + jnp.where(n < REL_EXACT, n, large)

def gmlp_mixer(h, w_in, w_s, b_s, vn_g, vn_b, w_out):
    bsz, s, _ = h.shape
    z = h @ w_in
    u, v, g = jnp.split(z, 3, axis=-1)
    u = jax.nn.gelu(u)
    v = layer_norm(jax.nn.gelu(v), vn_g, vn_b)
    nc = s // A_CHUNK
    vc = v.reshape(bsz, nc, A_CHUNK, A_HEADS, A_HEAD_DIM)
    sg = jnp.einsum('hpq,bcqhd->bcphd', w_s, vc) + b_s.T[None, None, :, :, None]
    y = u * sg.reshape(bsz, s, A_WIDTH) * jax.nn.silu(g)
    return y @ w_out

def dilated_window_group(q, k, v, table, dilation, half_w):
    bsz, s, nh, dh = q.shape
    L = s // dilation
    W = half_w
    nb = -(-L // W)
    Lp = nb * W

    def strided(t):
        return t.reshape(bsz, L, dilation, nh, dh).transpose(0, 2, 1, 3, 4)

    qs = jnp.pad(strided(q), ((0, 0), (0, 0), (0, Lp - L), (0, 0), (0, 0)))
    pad_kv = ((0, 0), (0, 0), (W, Lp - L + W), (0, 0), (0, 0))
    kp = jnp.pad(strided(k), pad_kv).reshape(bsz, dilation, nb + 2, W, nh, dh)
    vp = jnp.pad(strided(v), pad_kv).reshape(bsz, dilation, nb + 2, W, nh, dh)

    def band(t):
        return jnp.concatenate([t[:, :, 0:nb], t[:, :, 1:nb + 1], t[:, :, 2:nb + 2]], axis=3)

    kb, vb = band(kp), band(vp)
    qb = qs.reshape(bsz, dilation, nb, W, nh, dh)

    logits = jnp.einsum('bnkqhd,bnkjhd->bnkhqj', qb, kb,
                        preferred_element_type=jnp.float32) * (dh ** -0.5)
    qi = jnp.arange(W, dtype=jnp.int32)[:, None]
    kj = jnp.arange(3 * W, dtype=jnp.int32)[None, :]
    rel = kj - W - qi
    bias = table.astype(jnp.float32)[t5_bucket(rel * dilation)].transpose(2, 0, 1)
    key_pos = jnp.arange(nb, dtype=jnp.int32)[:, None] * W + kj - W
    mask = (jnp.abs(rel) <= W)[None] & ((key_pos >= 0) & (key_pos < L))[:, None, :]
    logits = jnp.where(mask[None, None, :, None], logits + bias, NEG_INF)

    m = jnp.max(logits, axis=-1, keepdims=True)
    p = jnp.exp(logits - m)
    den = jnp.sum(p, axis=-1, keepdims=True)
    o = jnp.einsum('bnkhqj,bnkjhd->bnkqhd', p / den, vb.astype(jnp.float32))
    lse = (m + jnp.log(den))[..., 0]

    o = o.reshape(bsz, dilation, Lp, nh, dh)[:, :, :L].transpose(0, 2, 1, 3, 4).reshape(bsz, s, nh, dh)
    lse = lse.transpose(0, 1, 2, 4, 3).reshape(bsz, dilation, Lp, nh)[:, :, :L]
    lse = lse.transpose(0, 2, 1, 3).reshape(bsz, s, nh)
    return o, lse

def dilated_attention_mixer(h, w_in, w_out, rel_table):
    bsz, s, _ = h.shape
    z = h @ w_in
    qkv = z[..., :B_QKV].reshape(bsz, s, B_N_GROUPS, 3, B_HEADS, B_HEAD_DIM)
    gate = z[..., B_QKV:]
    outs, lses = [], []
    for gi, (window, dil) in enumerate(B_GROUPS):
        o, lse = dilated_window_group(qkv[:, :, gi, 0], qkv[:, :, gi, 1], qkv[:, :, gi, 2],
                                      rel_table[:, gi * B_HEADS:(gi + 1) * B_HEADS],
                                      dil, window // (2 * dil))
        outs.append(o)
        lses.append(lse)
    wts = jax.nn.softmax(jnp.stack(lses), axis=0)
    o = jnp.einsum('gbsh,gbshd->bshd', wts, jnp.stack(outs))
    y = o.reshape(bsz, s, B_WIDTH).astype(h.dtype) * jax.nn.silu(gate)
    return y @ w_out

def first_inputs(seed: int = 0) -> dict:
    key = jax.random.key(seed)
    ks = jax.random.split(key, 16)
    f32 = jnp.float32
    x = jax.random.normal(ks[0], (BATCH, SEQ, D_MODEL), f32)
    norm_pre = 1.0 + 0.1 * jax.random.normal(ks[1], (DEPTH, D_MODEL), f32)
    norm_post = 1.0 + 0.1 * jax.random.normal(ks[2], (DEPTH, D_MODEL), f32)
    a_w_in = jax.random.normal(ks[3], (N_A_LAYERS, D_MODEL, 3 * A_WIDTH), f32) * D_MODEL ** -0.5
    a_w_s = jax.random.normal(ks[4], (N_A_LAYERS, A_HEADS, A_CHUNK, A_CHUNK), f32) * A_CHUNK ** -0.5
    a_b_s = 1.0 + 0.1 * jax.random.normal(ks[5], (N_A_LAYERS, A_HEADS, A_CHUNK), f32)
    a_vnorm_g = 1.0 + 0.1 * jax.random.normal(ks[6], (N_A_LAYERS, A_WIDTH), f32)
    a_vnorm_b = 0.1 * jax.random.normal(ks[7], (N_A_LAYERS, A_WIDTH), f32)
    a_w_out = jax.random.normal(ks[8], (N_A_LAYERS, A_WIDTH, D_MODEL), f32) * A_WIDTH ** -0.5
    b_w_in = jax.random.normal(ks[9], (N_B_LAYERS, D_MODEL, B_QKV + B_WIDTH), f32) * D_MODEL ** -0.5
    b_w_out = jax.random.normal(ks[10], (N_B_LAYERS, B_WIDTH, D_MODEL), f32) * B_WIDTH ** -0.5
    rel_bias = 0.5 * jax.random.normal(ks[11], (REL_BUCKETS, B_TOTAL_HEADS), f32)
    return {"x": x, "norm_pre": norm_pre, "norm_post": norm_post,
            "a_w_in": a_w_in, "a_w_s": a_w_s, "a_b_s": a_b_s,
            "a_vnorm_g": a_vnorm_g, "a_vnorm_b": a_vnorm_b, "a_w_out": a_w_out,
            "b_w_in": b_w_in, "b_w_out": b_w_out, "rel_bias": rel_bias}

def first_block(x, norm_pre, norm_post, a_w_in, a_w_s, a_b_s, a_vnorm_g, a_vnorm_b, a_w_out,
              b_w_in, b_w_out, rel_bias):
    for i in range(DEPTH):
        h = rms_norm(x, norm_pre[i])
        j = i // N_MIXERS
        if i % N_MIXERS == 0:
            y = gmlp_mixer(h, a_w_in[j], a_w_s[j], a_b_s[j], a_vnorm_g[j], a_vnorm_b[j], a_w_out[j])
        else:
            y = dilated_attention_mixer(h, b_w_in[j], b_w_out[j], rel_bias)
        x = x + rms_norm(y, norm_post[i])
    return x


DEPTH_2 = 1

N_META = 16
CHUNK = 128
PAD = CHUNK - N_META
HEAD_DIM = 64
SB_HEADS = 4
SB_W = SB_HEADS * HEAD_DIM
SSD_HEADS = 8
SSD_W = SSD_HEADS * HEAD_DIM
SSD_GROUPS = 2
SSD_STATE = 128
SSD_CONV = 4
SSD_CONV_DIM = SSD_W + 2 * SSD_GROUPS * SSD_STATE
HG_HEADS = 4
HG_DK = 64
HG_DV = 64
HG_W = HG_HEADS * HG_DV
D_MIX = SB_W + SSD_W + HG_W
D_FF = 4 * D_MODEL
TINY = 1e-30
IN_SIZES = (SB_W, SB_W, SB_W,
            SSD_W, SSD_W, SSD_GROUPS * SSD_STATE, SSD_GROUPS * SSD_STATE, SSD_HEADS,
            HG_HEADS * HG_DK, HG_HEADS * HG_DK, HG_W, HG_W)
D_IN = 3 * SB_W + 2 * SSD_W + 2 * SSD_GROUPS * SSD_STATE + SSD_HEADS + 2 * HG_HEADS * HG_DK + 2 * HG_W


def rmsnorm(x, w):
    xf = x.astype(jnp.float32)
    y = xf * lax.rsqrt(jnp.mean(xf * xf, axis=-1, keepdims=True) + EPS)
    return (y * w.astype(jnp.float32)).astype(x.dtype)

def causal_depthwise_conv(u, w, b):
    y = lax.conv_general_dilated(
        u, w[:, None, :].astype(u.dtype), window_strides=(1,), padding=[(w.shape[0] - 1, 0)],
        dimension_numbers=('NWC', 'WIO', 'NWC'), feature_group_count=u.shape[-1])
    return y + b.astype(u.dtype)

def to_chunks(t):
    b, l = t.shape[:2]
    return jnp.moveaxis(t.reshape((b, l // CHUNK, CHUNK) + t.shape[2:]), 1, 0)

def from_chunks(t):
    n, b = t.shape[:2]
    return jnp.moveaxis(t, 0, 1).reshape((b, n * CHUNK) + t.shape[3:])

def masked_decay(seg, mask):
    return jnp.where(mask, jnp.exp(jnp.where(mask, seg, 0.0)), 0.0)

def stick_breaking_attention(q, k, v, valid):
    L, dh = q.shape[2], q.shape[3]
    scale = dh ** -0.5
    pos = jnp.arange(L)
    outs = []
    for blk in range(L // CHUNK):
        start, end = blk * CHUNK, (blk + 1) * CHUNK
        z = jnp.einsum('bhqd,bhkd->bhqk', q[:, :, start:end], k[:, :, :end]).astype(jnp.float32) * scale
        mask = (pos[None, :end] < pos[start:end, None]) & valid[None, :end]
        log_keep = jnp.where(mask, jax.nn.log_sigmoid(-z), 0.0)
        csum = jnp.cumsum(log_keep, axis=-1)
        log_w = jax.nn.log_sigmoid(z) + (csum[..., -1:] - csum)
        w = jnp.where(mask, jnp.exp(jnp.where(mask, log_w, 0.0)), 0.0)
        outs.append(jnp.einsum('bhqk,bhkd->bhqd', w.astype(v.dtype), v[:, :, :end]))
    return jnp.concatenate(outs, axis=2)

def stick_breaking_group(q, k, v, q_norm, k_norm, out_norm, valid):
    bsz, L, _ = q.shape
    shp = (bsz, L, SB_HEADS, HEAD_DIM)
    qh = jnp.transpose(rmsnorm(q.reshape(shp), q_norm), (0, 2, 1, 3))
    kh = jnp.transpose(rmsnorm(k.reshape(shp), k_norm), (0, 2, 1, 3))
    vh = jnp.transpose(v.reshape(shp), (0, 2, 1, 3))
    o = jnp.transpose(stick_breaking_attention(qh, kh, vh, valid), (0, 2, 1, 3))
    return rmsnorm(o, out_norm).reshape(bsz, L, SB_W)

def ssd_chunked(xdt, a, bm, cm):
    bsz = xdt.shape[0]
    rep = SSD_HEADS // SSD_GROUPS
    causal = jnp.tril(jnp.ones((CHUNK, CHUNK), dtype=bool))

    def step(state, inp):
        a_c, x_c, b_c, c_c = inp
        acum = jnp.cumsum(a_c, axis=1)
        seg = acum[:, :, None, :] - acum[:, None, :, :]
        decay = masked_decay(seg, causal[None, :, :, None])
        cb = jnp.repeat(jnp.einsum('btgn,bsgn->btsg', c_c, b_c), rep, axis=-1)
        y_diag = jnp.einsum('btsh,bshp->bthp', cb * decay, x_c)
        c_h = jnp.repeat(c_c, rep, axis=2)
        b_h = jnp.repeat(b_c, rep, axis=2)
        y_off = jnp.einsum('bthn,bhpn->bthp', c_h, state) * jnp.exp(acum)[..., None]
        w_end = jnp.exp(acum[:, -1:, :] - acum)
        state = state * jnp.exp(acum[:, -1, :])[:, :, None, None] + jnp.einsum('bshn,bsh,bshp->bhpn', b_h, w_end, x_c)
        return state, y_diag + y_off

    state0 = jnp.zeros((bsz, SSD_HEADS, HEAD_DIM, SSD_STATE), jnp.float32)
    xs = tuple(to_chunks(t.astype(jnp.float32)) for t in (a, xdt, bm, cm))
    _, y = lax.scan(step, state0, xs)
    return from_chunks(y)

def ssd_group(z, xs, bm, cm, dt_raw, conv_w, conv_b, dt_bias, a_log, d_skip, norm_w, vmask):
    bsz, L, _ = xs.shape
    f32 = jnp.float32
    xbc = jax.nn.silu(causal_depthwise_conv(jnp.concatenate([xs, bm, cm], axis=-1) * vmask, conv_w, conv_b))
    xs, bm, cm = jnp.split(xbc, [SSD_W, SSD_W + SSD_GROUPS * SSD_STATE], axis=-1)
    dt = jax.nn.softplus(dt_raw.astype(f32) + dt_bias.astype(f32)) * vmask.astype(f32)
    a_neg = -jnp.exp(a_log.astype(f32))
    xh = xs.reshape(bsz, L, SSD_HEADS, HEAD_DIM).astype(f32)
    y = ssd_chunked(xh * dt[..., None], dt * a_neg,
                    bm.reshape(bsz, L, SSD_GROUPS, SSD_STATE), cm.reshape(bsz, L, SSD_GROUPS, SSD_STATE))
    y = y + xh * d_skip.astype(f32)[:, None]
    y = y.reshape(bsz, L, SSD_W) * jax.nn.silu(z.astype(f32))
    y = rmsnorm(y.reshape(bsz, L, SSD_GROUPS, SSD_W // SSD_GROUPS), norm_w)
    return y.reshape(bsz, L, SSD_W).astype(z.dtype)

def hgrn2_chunked(q, k, v, log_f):
    bsz = q.shape[0]
    causal = jnp.tril(jnp.ones((CHUNK, CHUNK), dtype=bool))

    def step(S, inp):
        q_c, k_c, v_c, g_c = inp
        gcum = jnp.cumsum(g_c, axis=1)
        seg = gcum[:, :, None] - gcum[:, None, :]
        decay = masked_decay(seg, causal[None, :, :, None, None])
        scores = jnp.einsum('bthk,btshk,bshk->btsh', q_c, decay, k_c)
        o_intra = jnp.einsum('btsh,bshv->bthv', scores, v_c)
        o_inter = jnp.einsum('bthk,bhkv->bthv', q_c * jnp.exp(gcum), S)
        k_end = k_c * jnp.exp(gcum[:, -1:] - gcum)
        S = S * jnp.exp(gcum[:, -1])[..., None] + jnp.einsum('bshk,bshv->bhkv', k_end, v_c)
        return S, o_intra + o_inter

    S0 = jnp.zeros((bsz, HG_HEADS, HG_DK, HG_DV), jnp.float32)
    _, o = lax.scan(step, S0, tuple(to_chunks(t) for t in (q, k, v, log_f)))
    return from_chunks(o)

def hgrn2_group(q, f_logit, i_in, g, lb, out_norm, valid):
    bsz, L, _ = q.shape
    f32 = jnp.float32
    fl = f_logit.astype(f32)
    keep = valid[None, :, None]
    f = lb + (1.0 - lb) * jax.nn.sigmoid(fl)
    log_f = jnp.where(keep, jnp.log(jnp.maximum(f, TINY)), 0.0)
    k = jnp.where(keep, (1.0 - lb) * jax.nn.sigmoid(-fl), 0.0)
    v = jnp.where(keep, i_in.astype(f32), 0.0)
    qf = jax.nn.silu(q.astype(f32))
    shp = (bsz, L, HG_HEADS, HG_DK)
    o = hgrn2_chunked(qf.reshape(shp), k.reshape(shp), v.reshape(bsz, L, HG_HEADS, HG_DV), log_f.reshape(shp))
    o = rmsnorm(o, out_norm) * jax.nn.silu(g.astype(f32)).reshape(bsz, L, HG_HEADS, HG_DV)
    return o.reshape(bsz, L, HG_W).astype(q.dtype)

def second_inputs(seed: int = 0) -> dict:
    key = jax.random.key(seed)
    ks = jax.random.split(key, 19)
    f32 = jnp.float32

    def normal(k, shape, scale):
        return scale * jax.random.normal(k, shape, f32)

    def gain(k, shape):
        return 1.0 + 0.01 * jax.random.normal(k, shape, f32)

    dt_init = jnp.exp(jax.random.uniform(ks[10], (DEPTH_2, SSD_HEADS), f32,
                                         minval=math.log(1e-3), maxval=math.log(1e-1)))
    return {
        'x': normal(ks[0], (BATCH, SEQ, D_MODEL), 1.0),
        'meta_tokens': normal(ks[1], (N_META, D_MODEL), 1.0),
        'hg_lb_logits': normal(ks[2], (DEPTH_2, HG_HEADS * HG_DK), 0.5),
        'norm_mix_w': gain(ks[3], (DEPTH_2, D_MODEL)),
        'w_in': normal(ks[4], (DEPTH_2, D_MODEL, D_IN), D_MODEL ** -0.5),
        'sb_q_norm': gain(ks[5], (DEPTH_2, HEAD_DIM)),
        'sb_k_norm': gain(ks[6], (DEPTH_2, HEAD_DIM)),
        'sb_out_norm': gain(ks[7], (DEPTH_2, SB_HEADS, HEAD_DIM)),
        'ssd_conv_w': normal(ks[8], (DEPTH_2, SSD_CONV, SSD_CONV_DIM), SSD_CONV ** -0.5),
        'ssd_conv_b': normal(ks[9], (DEPTH_2, SSD_CONV_DIM), 0.01),
        'ssd_dt_bias': dt_init + jnp.log(-jnp.expm1(-dt_init)),
        'ssd_A_log': jnp.log(jax.random.uniform(ks[11], (DEPTH_2, SSD_HEADS), f32, minval=1.0, maxval=16.0)),
        'ssd_D': gain(ks[12], (DEPTH_2, SSD_HEADS)),
        'ssd_norm_w': gain(ks[13], (DEPTH_2, SSD_GROUPS, SSD_W // SSD_GROUPS)),
        'hg_out_norm': gain(ks[14], (DEPTH_2, HG_HEADS, HG_DV)),
        'w_out': normal(ks[15], (DEPTH_2, D_MIX, D_MODEL), D_MIX ** -0.5),
        'norm_mlp_w': gain(ks[16], (DEPTH_2, D_MODEL)),
        'w_up': normal(ks[17], (DEPTH_2, D_MODEL, D_FF), D_MODEL ** -0.5),
        'w_down': normal(ks[18], (DEPTH_2, D_FF, D_MODEL), D_FF ** -0.5),
    }

def second_block(x, meta_tokens, hg_lb_logits, norm_mix_w, w_in, sb_q_norm, sb_k_norm, sb_out_norm,
              ssd_conv_w, ssd_conv_b, ssd_dt_bias, ssd_A_log, ssd_D, ssd_norm_w, hg_out_norm,
              w_out, norm_mlp_w, w_up, w_down):
    bsz = x.shape[0]
    dtype = x.dtype
    lead = jnp.concatenate([jnp.zeros((PAD, D_MODEL), dtype), meta_tokens.astype(dtype)], axis=0)
    h = jnp.concatenate([jnp.broadcast_to(lead[None], (bsz, CHUNK, D_MODEL)), x], axis=1)
    L = h.shape[1]
    valid = jnp.arange(L) >= PAD
    vmask = valid[None, :, None].astype(dtype)
    probs = jax.nn.softmax(hg_lb_logits.astype(jnp.float32), axis=0)
    lbs = jnp.concatenate([jnp.zeros_like(probs[0:1]), jnp.cumsum(probs, axis=0)[:-1]], axis=0)
    split_at = np.cumsum(IN_SIZES)[:-1].tolist()
    for l in range(DEPTH_2):
        hn = rmsnorm(h, norm_mix_w[l])
        proj = hn @ w_in[l]
        (q_sb, k_sb, v_sb, z_ssd, x_ssd, b_ssd, c_ssd, dt_ssd,
         q_hg, f_hg, i_hg, g_hg) = jnp.split(proj, split_at, axis=-1)
        o_sb = stick_breaking_group(q_sb, k_sb, v_sb, sb_q_norm[l], sb_k_norm[l], sb_out_norm[l], valid)
        o_ssd = ssd_group(z_ssd, x_ssd, b_ssd, c_ssd, dt_ssd, ssd_conv_w[l], ssd_conv_b[l], ssd_dt_bias[l],
                          ssd_A_log[l], ssd_D[l], ssd_norm_w[l], vmask)
        o_hg = hgrn2_group(q_hg, f_hg, i_hg, g_hg, lbs[l], hg_out_norm[l], valid)
        h = h + jnp.concatenate([o_sb, o_ssd, o_hg], axis=-1) @ w_out[l]
        hn = rmsnorm(h, norm_mlp_w[l])
        h = h + jnp.square(jax.nn.relu(hn @ w_up[l])) @ w_down[l]
    return h[:, CHUNK:]


_first_inputs = second_inputs


def second_inputs(seed=0):
    import zlib

    import numpy as np

    out = dict(_first_inputs(seed))
    spreads = {}
    factors = {'norm_mix_w': 5.819,
     'sb_q_norm': 30.956,
     'sb_k_norm': 29.336,
     'sb_out_norm': 64.0,
     'ssd_conv_b': 58.048,
     'ssd_D': 64.0,
     'ssd_norm_w': 64.0,
     'hg_out_norm': 45.586,
     'norm_mlp_w': 37.86}
    for name, (base, spread) in spreads.items():
        noise = np.random.default_rng([zlib.crc32(name.encode()), seed]).standard_normal(out[name].shape)
        drawn = base * np.exp(spread * noise) if base else spread * noise
        out[name] = jnp.asarray(drawn.astype(out[name].dtype))
    for name, factor in factors.items():
        out[name] = (out[name] * factor).astype(out[name].dtype)
    return out


_narrow_inputs = second_inputs


def second_inputs(seed=0):

    out = dict(_narrow_inputs(seed))
    wider = {'sb_out_norm': 12.0,
     'ssd_D': 12.0,
     'ssd_norm_w': 12.0,
     'hg_out_norm': 6.81,
     'norm_mlp_w': 5.59}
    for name, times in wider.items():
        mean = out[name].mean()
        out[name] = (mean + times * (out[name] - mean)).astype(out[name].dtype)
    return out


def setup_inputs(seed=0):
    out = dict(first_inputs(seed))
    for name, value in second_inputs(seed + 1).items():
        if name != "x":
            out[name + "_2"] = value
    return out


def reference(
    x, norm_pre, norm_post, a_w_in, a_w_s, a_b_s, a_vnorm_g, a_vnorm_b, a_w_out, b_w_in,
    b_w_out, rel_bias, meta_tokens_2, hg_lb_logits_2, norm_mix_w_2, w_in_2, sb_q_norm_2,
    sb_k_norm_2, sb_out_norm_2, ssd_conv_w_2, ssd_conv_b_2, ssd_dt_bias_2, ssd_A_log_2, ssd_D_2,
    ssd_norm_w_2, hg_out_norm_2, w_out_2, norm_mlp_w_2, w_up_2, w_down_2,
):
    x = first_block(
        x, norm_pre, norm_post, a_w_in, a_w_s, a_b_s, a_vnorm_g, a_vnorm_b, a_w_out, b_w_in,
        b_w_out, rel_bias,
    )
    return second_block(
        x, meta_tokens_2, hg_lb_logits_2, norm_mix_w_2, w_in_2, sb_q_norm_2, sb_k_norm_2,
        sb_out_norm_2, ssd_conv_w_2, ssd_conv_b_2, ssd_dt_bias_2, ssd_A_log_2, ssd_D_2,
        ssd_norm_w_2, hg_out_norm_2, w_out_2, norm_mlp_w_2, w_up_2, w_down_2,
    )


_drawn_inputs = setup_inputs


def setup_inputs(seed=0):
    import zlib

    import numpy as np

    out = dict(_drawn_inputs(seed))
    spreads = {}
    factors = {'ssd_D_2': 29.437}
    for name, (base, spread) in spreads.items():
        noise = np.random.default_rng([zlib.crc32(name.encode()), seed]).standard_normal(out[name].shape)
        drawn = base * np.exp(spread * noise) if base else spread * noise
        out[name] = jnp.asarray(drawn.astype(out[name].dtype))
    for name, factor in factors.items():
        out[name] = (out[name] * factor).astype(out[name].dtype)
    return out
```

```python
from contextlib import ExitStack

import numpy as np
import concourse.bass as bass
import concourse.mybir as mybir

F32 = mybir.dt.float32
F32R = mybir.dt.float32r
ACT = mybir.ActivationFunctionType
ALU = mybir.AluOpType
AX = mybir.AxisListType

P = 128
T = 1024
D = 1024
KT = D // P
EPS = 1e-6
HALF = 512


class Stage:

    def __init__(self, nc, name):
        self.nc, self.name, self.stack, self.used = nc, name, ExitStack(), []

    def __enter__(self):
        self.stack.__enter__()
        return self

    def __exit__(self, *a):
        self.stack.__exit__(*a)
        if self.used and a[0] is None:
            self.nc.clear_and_free_semaphores(self.used)
            self.nc.all_engine_barrier()

    def sb(self, name, shape, dt=F32):
        return self.stack.enter_context(self.nc.sbuf_tensor(f"{self.name}_{name}", shape, dt))

    def ps(self, name, shape):
        return self.stack.enter_context(self.nc.psum_tensor(f"{self.name}_{name}", shape, F32))

    def sem(self, name):
        self.used.append(self.nc.alloc_semaphore(f"{self.name}_{name}"))
        return self.used[-1]

    def sems(self, name, n):
        return [self.sem(f"{name}{i}") for i in range(n)]

    def block(self):
        return self.stack.enter_context(self.nc.Block())


def wait(eng, sem, value):
    if isinstance(value, int) and value <= 0:
        return
    eng.wait_ge(sem, value)


def repeat(eng, n, body):
    body(0)
    if n > 2:
        with eng.Fori(1, n - 1) as i:
            body(i)
    if n > 1:
        body(n - 1)


class Chain:

    def __init__(self, eng, sem):
        self.eng, self.sem, self.base, self.n = eng, sem, 0, 0

    def start(self, i, per):
        if self.n:
            assert self.per == self.n, (self.sem, self.per, self.n)
        self.base, self.n, self.per = i * per, 0, per

    def link(self, ins):
        ins.then_inc(self.sem, 1)
        self.n += 1
        self.eng.wait_ge(self.sem, self.base + self.n)


class Weights:

    def __init__(self, st, dram, buffers=2):
        self.nc, self.dram, self.nb = st.nc, dram, buffers
        self.raw = [st.sb(f"w_raw{b}", [P, KT * P]) for b in range(buffers)]
        self.hi = [st.sb(f"w_hi{b}", [P, KT * P], F32R) for b in range(buffers)]
        self.lo = [st.sb(f"w_lo{b}", [P, KT * P], F32R) for b in range(buffers)]
        self.loaded = st.sems("w_loaded", buffers)
        self.hi_done = st.sems("w_hi_done", buffers)
        self.lo_done = st.sems("w_lo_done", buffers)
        self.multiplied = st.sems("w_multiplied", buffers)

    def load(self, sp, b, n, unit):
        wait(sp, self.lo_done[b], n)
        sp.dma_start(self.raw[b][:, :], self.dram[bass.ds(unit, 1), :, :].rearrange("a p n -> p (a n)")
                     ).then_inc(self.loaded[b], 16)

    def split_hi(self, act, b, n, free=None):
        act.wait_ge(self.loaded[b], 16 * n + 16)
        wait(act, *(free or (self.multiplied[b], n)))
        self.nc.scalar.activation(self.hi[b][:, :], self.raw[b][:, :], ACT.Copy).then_inc(self.hi_done[b], 1)

    def split_lo(self, dve, b, n):
        dve.wait_ge(self.hi_done[b], n + 1)
        self.nc.vector.tensor_tensor(self.lo[b][:, :], self.raw[b][:, :], self.hi[b][:, :].bitcast(F32),
                                     ALU.subtract).then_inc(self.lo_done[b], 1)

    def products(self, out, b, act_hi, act_lo, cols):
        for k in range(KT):
            w = slice(k * P, k * P + P)
            for m, (wp, ap) in enumerate(((self.hi, act_hi), (self.lo, act_hi), (self.hi, act_lo))):
                last = self.nc.tensor.matmul(out, wp[b][:, w], ap[:, k, cols],
                                             start=(k == 0 and m == 0), stop=(k == KT - 1 and m == 2))
        return last


def norm_stage(nc, name, x, gain, ones, hi, lo, tokens, post=None, post_gain=None, col0=0, store=None):
    chunks = [(c, min(c + HALF, tokens)) for c in range(0, tokens, HALF)]
    jobs = ([("post", post, post_gain)] if post is not None else []) + [("pre", x, gain)]
    if hi is None:
        jobs = jobs[:1]
    with Stage(nc, name) as st:
        sq = [st.sb(f"sq{b}", [P, tokens]) for b in range(2)]
        acc = st.sb("acc", [P, tokens])
        rms = st.sb("rms", [P, tokens])
        inv = st.sb("inv", [P, tokens])
        h = [st.sb(f"h{b}", [P, tokens]) for b in range(2)]
        eps = st.sb("eps", [P, 1])
        gains = [st.sb(f"gain{j}", [P, KT]) for j in range(len(jobs))]
        total = [st.ps(f"total{c}", [P, HALF]) for c in range(len(chunks))]
        s_gain, s_eps, s_sq, s_acc, s_tot, s_rms, s_inv = (st.sem(n) for n in ("gain_s", "eps_s", "sq_s", "acc_s", "tot_s", "rms_s", "inv_s"))
        s_h, s_hi, s_lo, s_x, s_c = (st.sem(n) for n in ("h_s", "hi_s", "lo_s", "x_s", "chain"))
        block = st.block()

        @block.sync
        def _(sp):
            for j, (_, _, g) in enumerate(jobs):
                sp.dma_start(gains[j][:, :], g).then_inc(s_gain, 16)

        @block.scalar
        def _(act):
            act.wait_ge(s_eps, 1)
            for j, (kind, src, _) in enumerate(jobs):
                if j:
                    act.wait_ge(s_x, KT)
                for k in range(KT):
                    n = j * KT + k
                    wait(act, s_acc, n - 1)
                    nc.scalar.activation(sq[k % 2][:, :], src[:, k, 0:tokens], ACT.Square).then_inc(s_sq, 1)
                act.wait_ge(s_tot, j + 1)
                for c, (a, b) in enumerate(chunks):
                    nc.scalar.activation(rms[:, a:b], total[c][:, 0:b - a], ACT.Sqrt, bias=eps[:, :],
                                         scale=1.0 / D).then_inc(s_rms, 1)
                if kind == "pre":
                    for k in range(KT):
                        act.wait_ge(s_h, k + 1)
                        nc.scalar.activation(hi[:, k, col0:col0 + tokens], h[k % 2][:, :], ACT.Copy).then_inc(s_hi, 1)

        @block.tensor
        def _(pe):
            for j in range(len(jobs)):
                pe.wait_ge(s_acc, (j + 1) * KT)
                for c, (a, b) in enumerate(chunks):
                    last = nc.tensor.matmul(total[c][:, 0:b - a], ones, acc[:, a:b], start=True, stop=True)
                last.then_inc(s_tot, 1)

        @block.vector
        def _(dve):
            chain = Chain(dve, s_c)
            nc.vector.memset(eps[:, :], EPS).then_inc(s_eps, 1)
            dve.wait_ge(s_gain, 16 * len(jobs))
            for j, (kind, src, _) in enumerate(jobs):
                for k in range(KT):
                    dve.wait_ge(s_sq, j * KT + k + 1)
                    if k == 0:
                        wait(dve, s_tot, j)
                        nc.vector.tensor_copy(acc[:, :], sq[0][:, :]).then_inc(s_acc, 1)
                    else:
                        dve.wait_ge(s_acc, j * KT + k)
                        nc.vector.tensor_tensor(acc[:, :], acc[:, :], sq[k % 2][:, :], ALU.add).then_inc(s_acc, 1)
                dve.wait_ge(s_rms, (j + 1) * len(chunks))
                chain.link(nc.vector.reciprocal(inv[:, :], rms[:, :]))
                for k in range(KT):
                    if kind == "post":
                        chain.link(nc.vector.scalar_tensor_tensor(h[k % 2][:, :], src[:, k, 0:tokens], gains[j][:, k:k + 1],
                                                                  inv[:, :], ALU.mult, ALU.mult))
                        nc.vector.tensor_tensor(x[:, k, 0:tokens], x[:, k, 0:tokens], h[k % 2][:, :], ALU.add).then_inc(s_x, 1)
                    else:
                        wait(dve, s_hi, k - 1)
                        wait(dve, s_lo, k - 1)
                        if post is not None and k == 0:
                            dve.wait_ge(s_x, KT)
                        nc.vector.scalar_tensor_tensor(h[k % 2][:, :], src[:, k, 0:tokens], gains[j][:, k:k + 1],
                                                       inv[:, :], ALU.mult, ALU.mult).then_inc(s_h, 1)
                        dve.wait_ge(s_hi, k + 1)
                        nc.vector.tensor_tensor(lo[:, k, col0:col0 + tokens], h[k % 2][:, :],
                                                hi[:, k, col0:col0 + tokens].bitcast(F32), ALU.subtract).then_inc(s_lo, 1)


A_HEADS = 16


def gmlp_values(nc, hi, lo, w_v, vhat, ident):
    units = A_HEADS
    pairs = units // 2
    with Stage(nc, "av") as st:
        w = Weights(st, w_v)
        gelu = [st.sb(f"gelu{b}", [P, T]) for b in range(2)]
        v = st.sb("v", [P, KT, units * P])
        stats = st.sb("stats", [P, KT * 4, 6])
        mv = st.sb("mv", [P, KT, 2])
        sd = st.sb("sd", [P, KT])
        rstd = st.sb("rstd", [P, KT])
        shift = st.sb("shift", [P, KT])
        eps = st.sb("eps", [P, 1])
        z = [[st.ps(f"z{b}{h}", [P, HALF]) for h in range(2)] for b in range(2)]
        tr = [st.ps(f"tr{h}", [P, HALF]) for h in range(2)]
        s_gelu, s_tr = st.sems("gelu_s", 2), st.sems("tr_s", 2)
        s_copied = st.sems("copied", 2)
        s_eps, s_mv, s_sd, s_shift, s_vhat, s_out, s_c = (st.sem(n) for n in ("eps_s", "mv_s", "sd_s", "shift_s", "vhat_s", "out_s", "chain"))
        block = st.block()

        @block.sync
        def _(sp):
            def load_pair(i):
                for b in range(2):
                    w.load(sp, b, i, 2 * i + b)
            repeat(sp, pairs, load_pair)
            for m in range(KT):
                sp.wait_ge(s_vhat, m + 1)
                sp.dma_start(vhat[:, :, m, :].rearrange("j q d -> q j d"),
                             v[:, m, :].rearrange("p (j d) -> p j d", d=P)).then_inc(s_out, 16)
            sp.wait_ge(s_out, 16 * KT)

        @block.scalar
        def _(act):
            w.split_hi(act, 0, 0)

            def pair(i):
                for b in range(2):
                    if b == 0:
                        w.split_hi(act, 1, i)
                    elif not (isinstance(i, int) and i == pairs - 1):
                        w.split_hi(act, 0, i + 1)
                    act.wait_ge(w.multiplied[b], i + 1)
                    wait(act, s_tr[b], i)
                    for h in range(2):
                        last = nc.scalar.activation(gelu[b][:, h * HALF:h * HALF + HALF], z[b][h][:, :],
                                                    ACT.Gelu_apprx_tanh)
                    last.then_inc(s_gelu[b], 1)
            repeat(act, pairs, pair)
            act.wait_ge(s_mv, 1)
            act.wait_ge(s_eps, 1)
            nc.scalar.activation(sd[:, :], mv[:, :, 1:2].rearrange("p m a -> p (m a)"), ACT.Sqrt,
                                 bias=eps[:, :]).then_inc(s_sd, 1)
            act.wait_ge(s_shift, 1)
            for m in range(KT):
                nc.scalar.activation(v[:, m, :], v[:, m, :], ACT.Identity, bias=shift[:, m:m + 1],
                                     scale=rstd[:, m:m + 1]).then_inc(s_vhat, 1)

        @block.tensor
        def _(pe):
            def transpose(b, n):
                pe.wait_ge(s_gelu[b], n + 1)
                wait(pe, s_copied[1 - b], n + b)
                for m in range(KT):
                    last = nc.tensor.transpose(tr[m // 4][:, (m % 4) * P:(m % 4 + 1) * P],
                                               gelu[b][:, m * P:m * P + P], ident)
                last.then_inc(s_tr[b], 1)

            def pair(i):
                for b in range(2):
                    pe.wait_ge(w.lo_done[b], i + 1)
                    wait(pe, s_gelu[b], i)
                    for h in range(2):
                        last = w.products(z[b][h][:, :], b, hi, lo, slice(h * HALF, h * HALF + HALF))
                    last.then_inc(w.multiplied[b], 1)
                    if b == 1:
                        transpose(0, i)
                    elif not (isinstance(i, int) and i == 0):
                        transpose(1, i - 1)
            repeat(pe, pairs, pair)
            transpose(1, pairs - 1)

        @block.vector
        def _(dve):
            chain = Chain(dve, s_c)
            nc.vector.memset(eps[:, :], EPS).then_inc(s_eps, 1)
            w.split_lo(dve, 0, 0)

            def pair(i):
                for b in range(2):
                    if b == 0:
                        w.split_lo(dve, 1, i)
                    elif not (isinstance(i, int) and i == pairs - 1):
                        w.split_lo(dve, 0, i + 1)
                    dve.wait_ge(s_tr[b], i + 1)
                    for h in range(2):
                        last = nc.vector.tensor_copy(v[:, 4 * h:4 * h + 4, bass.ds((2 * i + b) * P, P)],
                                                     tr[h][:, :].rearrange("p (m d) -> p m d", d=P))
                    last.then_inc(s_copied[b], 1)
            repeat(dve, pairs, pair)
            dve.wait_ge(s_copied[1], pairs)
            for m in range(KT):
                for c in range(4):
                    last = nc.vector.bn_stats(stats[:, 4 * m + c, :], v[:, m, c * HALF:c * HALF + HALF])
            chain.link(last)
            for m in range(KT):
                last = nc.vector.bn_aggr(mv[:, m, :], stats[:, 4 * m:4 * m + 4, :])
            last.then_inc(s_mv, 1)
            dve.wait_ge(s_sd, 1)
            chain.link(nc.vector.reciprocal(rstd[:, :], sd[:, :]))
            nc.vector.scalar_tensor_tensor(shift[:, :], mv[:, :, 0:1].rearrange("p m a -> p (m a)"), -1.0,
                                           rstd[:, :], ALU.mult, ALU.mult).then_inc(s_shift, 1)


def gmlp_gate(nc, hi, lo, w_ug, vhat, ws_t, b_s, ln_g, ln_b, yo):
    halves = 2
    heads = A_HEADS // halves
    down = KT // 2
    pairs = heads + down
    with Stage(nc, "ag") as st:
        w = Weights(st, w_ug)
        y_hi = st.sb("y_hi", [P, heads, T], F32R)
        y_lo = st.sb("y_lo", [P, heads, T], F32R)
        v_raw = st.sb("v_raw", [P, T])
        v = st.sb("v", [P, T])
        gain = st.sb("gain", [P, P])
        bias = st.sb("bias", [P, P])
        ws = st.sb("ws", [P, P])
        bs = st.sb("bs", [P, P])
        th = st.sb("th", [P, T])
        gu = st.sb("gu", [P, T])
        s = st.sb("s", [P, T])
        z = [[st.ps(f"z{b}{h}", [P, HALF]) for h in range(2)] for b in range(2)]
        sg = [st.ps(f"sg{h}", [P, HALF]) for h in range(2)]
        s_vin, s_pin, s_v, s_gu, s_th, s_a, s_s, s_sg, s_y, s_yhi, s_ylo, s_c, s_cv = (
            st.sem(n) for n in ("vin", "pin", "v_s", "gu_s", "th_s", "a_s", "s_s", "sg_s", "y_s", "yhi_s", "ylo_s", "chain", "chain_v"))
        s_down = st.sems("down", 2)
        block = st.block()
        view = lambda t: t[:, :].rearrange("p (m d) -> p m d", d=P)
        each = lambda t: t[:, :].rearrange("p (a d) -> p a d", a=1).broadcast_to([P, KT, P])
        row = lambda a, j: bass.AP(a.tensor, j * P, [[0, P], [1, P]])

        @block.sync
        def _(sp):
            for hf in range(halves):
                def head(i):
                    j = hf * heads + i
                    n = hf * pairs + i
                    for b in range(2):
                        w.load(sp, b, n, (2 * pairs) * hf + 2 * i + b)
                    wait(sp, s_v, j)
                    sp.dma_start(v_raw[:, :], vhat[bass.ds(j, 1), :, :, :].rearrange("a q m d -> q (a m d)")).then_inc(s_vin, 16)
                    sp.dma_start(gain[:, :], row(ln_g, j)).then_inc(s_vin, 16)
                    sp.dma_start(bias[:, :], row(ln_b, j)).then_inc(s_vin, 16)
                    wait(sp, s_y, j)
                    sp.dma_start(ws[:, :], ws_t[bass.ds(j, 1), :, :].rearrange("a q p -> q (a p)")).then_inc(s_pin, 16)
                    sp.dma_start(bs[:, :], row(b_s, j)).then_inc(s_pin, 16)
                repeat(sp, heads, head)

                def out(i):
                    for b in range(2):
                        w.load(sp, b, hf * pairs + heads + i, (2 * pairs) * hf + 2 * heads + 2 * i + b)
                repeat(sp, down, out)

        @block.scalar
        def _(act):
            w.split_hi(act, 0, 0)
            for hf in range(halves):
                def head(i):
                    j, n = hf * heads + i, hf * pairs + i
                    w.split_hi(act, 1, n)
                    act.wait_ge(w.multiplied[0], n + 1)
                    wait(act, s_y, j)
                    for h in range(2):
                        last = nc.scalar.activation(gu[:, h * HALF:h * HALF + HALF], z[0][h][:, :], ACT.Gelu_apprx_tanh)
                    last.then_inc(s_gu, 1)
                    w.split_hi(act, 0, n + 1)
                    act.wait_ge(w.multiplied[1], n + 1)
                    for h in range(2):
                        last = nc.scalar.activation(th[:, h * HALF:h * HALF + HALF], z[1][h][:, :], ACT.Tanh, scale=0.5)
                    last.then_inc(s_th, 1)
                    act.wait_ge(s_y, j + 1)
                    nc.scalar.activation(y_hi[:, bass.ds(i, 1), :].rearrange("p a t -> p (a t)"), th[:, :], ACT.Copy).then_inc(s_yhi, 1)
                repeat(act, heads, head)

                def out(i):
                    n = hf * pairs + heads + i
                    w.split_hi(act, 1, n)
                    if not (hf == halves - 1 and isinstance(i, int) and i == down - 1):
                        w.split_hi(act, 0, n + 1)
                repeat(act, down, out)

        @block.tensor
        def _(pe):
            for hf in range(halves):
                def head(i):
                    j, n = hf * heads + i, hf * pairs + i
                    for b in range(2):
                        pe.wait_ge(w.lo_done[b], n + 1)
                        wait(pe, (s_gu, s_a)[b], j)
                        wait(pe, s_down[b], hf * down)
                        for h in range(2):
                            last = w.products(z[b][h][:, :], b, hi, lo, slice(h * HALF, h * HALF + HALF))
                        last.then_inc(w.multiplied[b], 1)
                        if b == 0:
                            pe.wait_ge(s_v, j + 1)
                            pe.wait_ge(s_pin, 32 * j + 32)
                            wait(pe, s_s, j)
                            for m in range(KT):
                                last = nc.tensor.matmul(sg[m // 4][:, (m % 4) * P:(m % 4 + 1) * P],
                                                        v[:, m * P:m * P + P], ws[:, :], start=True, stop=True)
                            last.then_inc(s_sg, 1)
                repeat(pe, heads, head)

                def out(i):
                    n = hf * pairs + heads + i
                    for b in range(2):
                        pe.wait_ge(w.lo_done[b], n + 1)
                        pe.wait_ge((s_gu, s_a)[b], (hf + 1) * heads)
                        wait(pe, s_down[b], hf * down + i)
                        pe.wait_ge(s_ylo, (hf + 1) * heads)
                        for h in range(2):
                            last = w.products(z[b][h][:, :], b, y_hi, y_lo, slice(h * HALF, h * HALF + HALF))
                        last.then_inc(w.multiplied[b], 1)
                repeat(pe, down, out)

        @block.vector
        def _(dve):
            c1 = Chain(dve, s_c)
            w.split_lo(dve, 0, 0)
            for hf in range(halves):
                def head(i):
                    j, n = hf * heads + i, hf * pairs + i
                    w.split_lo(dve, 1, n)
                    dve.wait_ge(s_vin, 48 * j + 48)
                    wait(dve, s_sg, j)
                    c1.start(j, 2)
                    c1.link(nc.vector.tensor_tensor(view(v), view(v_raw), each(gain), ALU.mult))
                    nc.vector.tensor_tensor(view(v), view(v), each(bias), ALU.add).then_inc(s_v, 1)
                    w.split_lo(dve, 0, n + 1)
                    dve.wait_ge(s_th, j + 1)
                    for h in range(2):
                        last = nc.vector.scalar_tensor_tensor(th[:, h * HALF:h * HALF + HALF], th[:, h * HALF:h * HALF + HALF],
                                                              1.0, z[1][h][:, :], ALU.add, ALU.mult)
                    last.then_inc(s_a, 1)
                    dve.wait_ge(s_sg, j + 1)
                    dve.wait_ge(s_pin, 32 * j + 32)
                    for h in range(2):
                        last = nc.vector.tensor_tensor(
                            s[:, h * HALF:h * HALF + HALF].rearrange("p (m d) -> p m d", d=P),
                            sg[h][:, :].rearrange("p (m d) -> p m d", d=P),
                            bs[:, :].rearrange("p (a d) -> p a d", a=1).broadcast_to([P, 4, P]), ALU.add)
                    last.then_inc(s_s, 1)
                    dve.wait_ge(s_gu, j + 1)
                    dve.wait_ge(s_a, j + 1)
                    c1.link(nc.vector.scalar_tensor_tensor(th[:, :], th[:, :], 0.5, gu[:, :], ALU.mult, ALU.mult))
                    dve.wait_ge(s_s, j + 1)
                    nc.vector.tensor_tensor(th[:, :], th[:, :], s[:, :], ALU.mult).then_inc(s_y, 1)
                    dve.wait_ge(s_yhi, j + 1)
                    nc.vector.tensor_tensor(y_lo[:, bass.ds(i, 1), :].rearrange("p a t -> p (a t)"), th[:, :],
                                            y_hi[:, bass.ds(i, 1), :].rearrange("p a t -> p (a t)").bitcast(F32),
                                            ALU.subtract).then_inc(s_ylo, 1)
                repeat(dve, heads, head)

                def out(i):
                    n = hf * pairs + heads + i
                    for b in range(2):
                        if b == 0:
                            w.split_lo(dve, 1, n)
                        elif not (hf == halves - 1 and isinstance(i, int) and i == down - 1):
                            w.split_lo(dve, 0, n + 1)
                        dve.wait_ge(w.multiplied[b], n + 1)
                        for h in range(2):
                            dst = yo[:, bass.ds(2 * i + b, 1), h * HALF:h * HALF + HALF].rearrange("p a t -> p (a t)")
                            if hf == 0:
                                last = nc.vector.tensor_copy(dst, z[b][h][:, :])
                            else:
                                last = nc.vector.tensor_tensor(dst, dst, z[b][h][:, :], ALU.add)
                        last.then_inc(s_down[b], 1)
                repeat(dve, down, out)


GROUPS = ((1, 1024), (4, 256), (16, 64))
WINDOW = 64
B_HEADS = 16
B_PAIRS = B_HEADS // 2
VEC = 384
FAR = 1e30
REL_BUCKETS = 32


def bias_vectors(nc, rel_bias, onehot, far, vecs, tiles):
    with Stage(nc, "bv") as st:
        table = st.sb("table", [REL_BUCKETS, 3 * B_HEADS])
        hot = st.sb("hot", [REL_BUCKETS, 3 * VEC])
        out_of = st.sb("out_of", [B_HEADS, 3 * VEC])
        v = st.sb("v", [B_HEADS, 3 * VEC])
        ps = [st.ps(f"ps{g}", [B_HEADS, VEC]) for g in range(3)]
        s_in, s_mm, s_v, s_out = (st.sem(n) for n in ("in", "mm", "v_s", "out"))
        block = st.block()

        @block.sync
        def _(sp):
            sp.dma_start(table[:, :], rel_bias).then_inc(s_in, 16)
            sp.dma_start(hot[:, :], onehot).then_inc(s_in, 16)
            sp.dma_start(out_of[:, :], far).then_inc(s_in, 16)
            sp.wait_ge(s_v, 3)
            for g in range(3):
                sp.dma_start(vecs[g * B_HEADS:(g + 1) * B_HEADS, :], v[:, g * VEC:(g + 1) * VEC]).then_inc(s_out, 16)
            sp.wait_ge(s_out, 48)
            for g in range(3):
                for h in range(0, B_HEADS, 4):
                    sp.dma_start(tiles[g * B_HEADS + h:g * B_HEADS + h + 4, :, :],
                                 bass.AP(vecs.tensor, (g * B_HEADS + h) * VEC + P - 1, [[VEC, 4], [-1, P], [1, 2 * P]])).then_inc(s_out, 16)
            sp.wait_ge(s_out, 48 + 16 * 12)

        @block.tensor
        def _(pe):
            pe.wait_ge(s_in, 48)
            for g in range(3):
                nc.tensor.matmul(ps[g][:, :], table[:, g * B_HEADS:(g + 1) * B_HEADS], hot[:, g * VEC:(g + 1) * VEC],
                                 start=True, stop=True).then_inc(s_mm, 1)

        @block.vector
        def _(dve):
            dve.wait_ge(s_in, 48)
            for g in range(3):
                dve.wait_ge(s_mm, g + 1)
                c = slice(g * VEC, (g + 1) * VEC)
                nc.vector.scalar_tensor_tensor(v[:, c], ps[g][:, :], -1.0, out_of[:, c], ALU.mult, ALU.add).then_inc(s_v, 1)


def dilated_attention(nc, hi, lo, w_qkv, bias_dram, o_dram, lse_dram, ident):
    turns = 3 * B_PAIRS
    tiles = T // P
    SUB = 12
    with Stage(nc, "da") as st:
        w = Weights(st, w_qkv, buffers=3)
        q_new = st.sb("q_new", [P, T])
        k_new = st.sb("k_new", [P, T])
        v_new = st.sb("v_new", [P, T + 2 * WINDOW])
        q = st.sb("q", [P, T])
        k = st.sb("k", [P, T + 2 * WINDOW])
        v = st.sb("v", [P, tiles + 1, P])
        nvar = (3, 2, 1)
        width = (256, 256, 128)
        bias = [[[st.sb(f"bias{g}{h}{x}", [P, width[g]]) for x in range(nvar[g])] for h in range(2)] for g in range(3)]
        logit = [st.sb(f"logit{b}", [P, 2, 256]) for b in range(2)]
        p = [st.sb(f"p{b}", [P, 2, 256]) for b in range(2)]
        pt = [st.sb(f"pt{b}", [P, 512]) for b in range(2)]
        o = st.sb("o", [P, tiles, P])
        rden = [st.sb(f"rden{b}", [P, 2]) for b in range(2)]
        nmax = st.sb("nmax", [P, 3, tiles, B_HEADS])
        pad = st.sb("pad", [P, 1])
        pair_max = st.sb("pair_max", [P, tiles, 2])
        den = st.sb("den", [P, 3, tiles, B_HEADS])
        z = [st.ps(f"z{h}", [P, HALF]) for h in range(2)]
        qk = [st.ps(f"qk{b}", [P, HALF]) for b in range(2)]
        tr = [st.ps(f"tr{b}", [P, HALF]) for b in range(2)]
        pv = [st.ps(f"pv{b}", [P, HALF]) for b in range(2)]
        s_piece, s_new = st.sems("piece", 2), st.sem("new")
        (s_qs, s_vt, s_vts, s_qk, s_max, s_exp, s_t, s_pt, s_pv, s_rden, s_o, s_keep, s_bias, s_odma, s_zero, s_l, s_ldma) = (
            st.sem(x) for x in ("qs", "vt", "vts", "qk_s", "max", "exp", "t", "pt_s", "pv_s", "rden_s", "o_s", "keep", "bias_s", "odma", "zero", "l", "ldma"))
        block = st.block()

        def n_bias(g):
            return 2 * (2 if g == 2 else nvar[g])

        def streams(t2, g):
            d, L = GROUPS[g]
            return t2.rearrange("p (r l) -> p l r", r=d, l=L)

        def schedule(eng, turn):
            turn(0, 0, 0, None, None)
            for g in range(3):
                base = g * B_PAIRS
                if g:
                    turn(base, g, 0, g - 1, B_PAIRS - 1)
                else:
                    turn(1, 0, 1, 0, 0)
                with eng.Fori(1 if g else 2, B_PAIRS - 1) as hp:
                    turn(base + hp, g, hp, g, hp - 1)
                turn(base + B_PAIRS - 1, g, B_PAIRS - 1, g, B_PAIRS - 2)
            turn(turns, None, None, 2, B_PAIRS - 1)

        @block.sync
        def _(sp):
            def load_next(n):
                for b in range(3):
                    w.load(sp, b, n, 3 * n + b)
            sp.wait_ge(s_zero, 1)
            load_next(0)

            def turn(n, g, hp, ag, ahp):
                if ag is None:
                    load_next(1)
                else:
                    a = n - 1
                    wait(sp, s_max, tiles * a)
                    for h in range(2):
                        head = ag * B_HEADS + 2 * ahp + h
                        for x in range(nvar[ag]):
                            tile = bias[ag][h][x]
                            if ag < 2:
                                c0 = WINDOW if x == 0 else 0
                                c1 = 192 if x == 1 else 256
                                sp.dma_start(tile[:, c0:c1], bias_dram[bass.ds(head, 1), :, c0:c1].rearrange("a i j -> i (a j)")).then_inc(s_bias, 16)
                            else:
                                for u in range(2):
                                    sp.dma_start(tile[64 * u:64 * u + 64, 64 * u:64 * u + 64],
                                                 bias_dram[bass.ds(head, 1), 0:64, 64:128].rearrange("a i j -> i (a j)")).then_inc(s_bias, 16)
                    if not (isinstance(n, int) and n >= turns - 1):
                        load_next(n + 1)
                    sp.wait_ge(s_o, tiles * n)
                    d, L = GROUPS[ag]
                    cols = ahp * P + ag * T * D
                    if ag == 0:
                        for u in range(2):
                            sp.dma_start(bass.AP(o_dram.tensor, cols + u * 4 * P * D, [[D, P], [P * D, 4], [1, P]]),
                                         o[:, 4 * u:4 * u + 4, :]).then_inc(s_odma, 16)
                    elif ag == 1:
                        for u in range(2):
                            sp.dma_start(bass.AP(o_dram.tensor, cols + u * P * d * D, [[d * D, P], [D, 4], [1, P]]),
                                         o[:, u::2, :]).then_inc(s_odma, 16)
                    else:
                        for u in range(2):
                            sp.dma_start(bass.AP(o_dram.tensor, cols + u * D, [[d * D, 64], [2 * D, tiles], [1, P]]),
                                         o[64 * u:64 * u + 64, :, :]).then_inc(s_odma, 16)
            schedule(sp, turn)
            sp.wait_ge(s_odma, 32 * turns)
            sp.wait_ge(s_l, 1)
            for g, (d, L) in enumerate(GROUPS):
                for m in range(tiles):
                    base = g * T * B_HEADS
                    if g < 2:
                        start = (m // (L // P)) + (m % (L // P)) * P * d
                        sp.dma_start(bass.AP(lse_dram.tensor, base + start * B_HEADS, [[d * B_HEADS, P], [1, B_HEADS]]),
                                     den[:, g, m, :]).then_inc(s_ldma, 16)
                    else:
                        for u in range(2):
                            sp.dma_start(bass.AP(lse_dram.tensor, base + (2 * m + u) * B_HEADS, [[d * B_HEADS, 64], [1, B_HEADS]]),
                                         den[64 * u:64 * u + 64, g, m, :]).then_inc(s_ldma, 16)
            sp.wait_ge(s_ldma, 16 * (2 * tiles + 2 * tiles))

        def bias_count(ag, ahp):
            return 16 * (sum(n_bias(g) * B_PAIRS for g in range(ag)) + n_bias(ag) * (ahp + 1))

        @block.scalar
        def _(act):
            w.split_hi(act, 0, 0)

            def turn(n, g, hp, ag, ahp):
                a = n - 1
                for s in range(SUB):
                    u, h = s // 4, (s // 2) % 2
                    if g is not None and s % 4 == 0:
                        if u < 2:
                            w.split_hi(act, u + 1, n, free=(s_piece[1], 3 * n + u - 1))
                        elif not (isinstance(n, int) and n == turns - 1):
                            w.split_hi(act, 0, n + 1, free=(s_piece[1], 3 * n + 1))
                    if g is not None and s % 2 == 1:
                        act.wait_ge(s_piece[h], 3 * n + u + 1)
                        cut = GROUPS[g][0]
                        l0, l1 = h * HALF // cut, (h + 1) * HALF // cut
                        src = z[h][:, :].rearrange("p (l r) -> p l r", r=cut)
                        if u == 0:
                            wait(act, s_qs, n)
                            nc.scalar.activation(streams(q_new[:, :], g)[:, l0:l1, :], src, ACT.Copy, scale=-0.125).then_inc(s_new, 1)
                        elif u == 1:
                            nc.scalar.activation(streams(k_new[:, :], g)[:, l0:l1, :], src, ACT.Copy).then_inc(s_new, 1)
                        else:
                            wait(act, s_vt, n)
                            act.wait_ge(s_zero, 1)
                            nc.scalar.activation(streams(v_new[:, WINDOW:WINDOW + T], g)[:, l0:l1, :], src, ACT.Copy).then_inc(s_new, 1)
                    if ag is not None and 3 <= s < 3 + tiles:
                        t = s - 3
                        c = tiles * a + t
                        act.wait_ge(s_t, c + 1)
                        wait(act, s_pv, c - 1)
                        wd = 4 * P if ag < 2 else 2 * P
                        nc.scalar.activation(pt[t % 2][:, 0:wd], tr[t % 2][:, 0:wd], ACT.Copy).then_inc(s_pt, 1)
                    if ag is not None and 1 <= s < 1 + tiles:
                        t = s - 1
                        c = tiles * a + t
                        act.wait_ge(s_max, c + 1)
                        wait(act, s_t, c - 1)
                        wd = width[ag]
                        for hh in range(2):
                            last = nc.scalar.activation(p[t % 2][:, hh, 0:wd], logit[t % 2][:, hh, 0:wd], ACT.Exp, scale=-1.0,
                                                        bias=pair_max[:, t, hh:hh + 1],
                                                        accum_out=den[:, ag, t, bass.ds(2 * ahp + hh, 1)])
                        last.then_inc(s_exp, 1)
            schedule(act, turn)
            act.wait_ge(s_o, tiles * turns)
            act.wait_ge(s_exp, tiles * turns)
            nc.scalar.activation(den[:, :, :, :], den[:, :, :, :], ACT.Ln).then_inc(s_exp, 1)

        @block.tensor
        def _(pe):
            def turn(n, g, hp, ag, ahp):
                a = n - 1
                for s in range(SUB):
                    u, h, half = s // 4, (s // 2) % 2, s % 2
                    if g is not None:
                        if s % 4 == 0:
                            pe.wait_ge(w.lo_done[u], n + 1)
                        if half == 0:
                            wait(pe, s_new, 6 * n + 2 * u - 1 + h)
                        cols = slice(h * HALF, h * HALF + HALF)
                        for kk in range(4 * half, 4 * half + 4):
                            ws = slice(kk * P, kk * P + P)
                            for m, (wp, ap) in enumerate(((w.hi, hi), (w.lo, hi), (w.hi, lo))):
                                last = nc.tensor.matmul(z[h][:, :], wp[u][:, ws], ap[:, kk, cols],
                                                        start=(kk == 0 and m == 0), stop=(kk == KT - 1 and m == 2))
                        if half == 1:
                            last.then_inc(s_piece[h], 1)
                    if ag is None:
                        continue
                    wd = width[ag]
                    if s == 0:
                        pe.wait_ge(s_new, 6 * n)
                        wait(pe, s_pt, tiles * a)
                        wait(pe, s_o, tiles * a)
                        off, cnt = (0, tiles + 1) if ag < 2 else (WINDOW, tiles)
                        for m in range(cnt):
                            dst = (tr[0], tr[1], pv[0])[m // 4]
                            c0 = (m % 4) * P
                            last = nc.tensor.transpose(dst[:, c0:c0 + P], v_new[:, off + m * P:off + m * P + P], ident)
                        last.then_inc(s_vt, 1)
                    if 1 <= s < 1 + tiles:
                        t = s - 1
                        c = tiles * a + t
                        if t == 0:
                            pe.wait_ge(s_qs, n)
                        wait(pe, s_max, c)
                        k0 = t * P + (WINDOW if ag == 2 else 0)
                        for hh in range(2):
                            hs = slice(64 * hh, 64 * hh + 64)
                            last = nc.tensor.matmul(qk[hh][:, 0:wd], q[hs, t * P:t * P + P],
                                                    k[hs, k0:k0 + wd], start=True, stop=True)
                        last.then_inc(s_qk, 1)
                    if 3 <= s < 3 + tiles:
                        t = s - 3
                        c = tiles * a + t
                        pe.wait_ge(s_exp, c + 1)
                        pe.wait_ge(s_vts, n)
                        wait(pe, s_pt, c - 1)
                        for hh in range(2):
                            for x in range(wd // P):
                                i = hh * (wd // P) + x
                                last = nc.tensor.transpose(tr[t % 2][:, i * P:i * P + P], p[t % 2][:, hh, x * P:x * P + P], ident)
                        last.then_inc(s_t, 1)
                    if 4 <= s < 4 + tiles:
                        t = s - 4
                        c = tiles * a + t
                        pe.wait_ge(s_pt, c + 1)
                        pe.wait_ge(s_vts, n)
                        wait(pe, s_o, c - 1)
                        for hh in range(2):
                            for x in range(wd // P):
                                i = hh * (wd // P) + x
                                last = nc.tensor.matmul(pv[t % 2][:, 64 * hh:64 * hh + 64],
                                                        pt[t % 2][:, i * P:i * P + P], v[:, t + x, 64 * hh:64 * hh + 64],
                                                        start=(x == 0), stop=(x == wd // P - 1))
                        last.then_inc(s_pv, 1)
            schedule(pe, turn)

        @block.vector
        def _(dve):
            for g in range(3):
                for h in range(2):
                    for tile in bias[g][h]:
                        nc.vector.memset(tile[:, :], FAR)
            for t2 in (k, v_new):
                nc.vector.memset(t2[:, 0:WINDOW], 0.0)
                last = nc.vector.memset(t2[:, WINDOW + T:], 0.0)
            last.then_inc(s_zero, 1)
            w.split_lo(dve, 0, 0)

            def turn(n, g, hp, ag, ahp):
                a = n - 1
                for s in range(SUB):
                    u = s // 4
                    if g is not None and s % 4 == 0:
                        if u < 2:
                            w.split_lo(dve, u + 1, n)
                        elif not (isinstance(n, int) and n == turns - 1):
                            w.split_lo(dve, 0, n + 1)
                    if ag is None:
                        continue
                    wd = width[ag]
                    if s == 0:
                        dve.wait_ge(s_vt, n)
                        wait(dve, s_pv, tiles * a)
                        nc.vector.tensor_copy(v[:, 0:4, :], tr[0][:, :].rearrange("p (m c) -> p m c", c=P))
                        last = nc.vector.tensor_copy(v[:, 4:8, :], tr[1][:, :].rearrange("p (m c) -> p m c", c=P))
                        if ag < 2:
                            last = nc.vector.tensor_copy(v[:, 8, :], pv[0][:, 0:P])
                        last.then_inc(s_vts, 1)
                    if 1 <= s < 1 + tiles:
                        t = s - 1
                        c = tiles * a + t
                        if t == 0:
                            dve.wait_ge(s_bias, bias_count(ag, ahp))
                        dve.wait_ge(s_qk, c + 1)
                        wait(dve, s_exp, c - 1)
                        nc.vector.memset(pad[:, :], 0.0)
                        L = GROUPS[ag][1]
                        x = 0 if ag == 2 or t % (L // P) == 0 else 1 if (t + 1) % (L // P) == 0 else 2
                        for hh in range(2):
                            last = nc.vector.tensor_tensor_reduce(
                                out=logit[t % 2][:, hh, 0:wd], in0=qk[hh][:, 0:wd], in1=bias[ag][hh][x][:, :],
                                scale=1.0, scalar=3e38, op0=ALU.add, op1=ALU.min,
                                accum_out=pair_max[:, t, hh:hh + 1])
                        last.then_inc(s_max, 1)
                    if 4 <= s < 4 + tiles:
                        t = s - 4
                        c = tiles * a + t
                        dve.wait_ge(s_exp, c + 1)
                        wait(dve, s_o, c - 1)
                        nc.vector.reciprocal(rden[t % 2][:, :], den[:, ag, t, bass.ds(2 * ahp, 2)]).then_inc(s_rden, 1)
                        dve.wait_ge(s_rden, c + 1)
                        dve.wait_ge(s_pv, c + 1)
                        if t == 0:
                            wait(dve, s_odma, 32 * a)
                        nc.vector.tensor_tensor(o[:, t, :].rearrange("p (h c) -> p h c", h=2),
                                                pv[t % 2][:, 0:P].rearrange("p (h c) -> p h c", h=2),
                                                rden[t % 2][:, :].rearrange("p (h a) -> p h a", a=1).broadcast_to([P, 2, 64]),
                                                ALU.mult).then_inc(s_o, 1)
                if ag is not None:
                    dve.wait_ge(s_max, tiles * n)
                    nc.vector.tensor_copy(nmax[:, ag, :, bass.ds(2 * ahp, 2)], pair_max[:, :, :]).then_inc(s_keep, 1)
                if g is not None:
                    dve.wait_ge(s_new, 6 * n + 4)
                    wait(dve, s_qk, tiles * n)
                    nc.vector.tensor_copy(q[:, :], q_new[:, :])
                    nc.vector.tensor_copy(k[:, WINDOW:WINDOW + T], k_new[:, :]).then_inc(s_qs, 1)
            schedule(dve, turn)
            dve.wait_ge(s_exp, tiles * turns + 1)
            dve.wait_ge(s_keep, turns)
            nc.vector.tensor_tensor(den[:, :, :, :], den[:, :, :, :], nmax[:, :, :, :], ALU.subtract).then_inc(s_l, 1)


def attention_output(nc, hi, lo, w_stream, o_dram, lse_dram, ident, yo):
    pairs = KT // 2
    tiles = T // P
    NG = len(GROUPS)
    with Stage(nc, "bo") as st:
        w = Weights(st, w_stream)
        gate = st.sb("gate", [P, KT, T])
        comb = yo
        o = st.sb("o", [P, NG, D])
        th = st.sb("th", [P, T])
        y = [st.sb(f"y{b}", [P, KT // 2, P]) for b in range(2)]
        lse = st.sb("lse", [P, tiles, NG, B_HEADS])
        top = st.sb("top", [P, tiles, B_HEADS])
        total = st.sb("total", [P, tiles, B_HEADS])
        z = [[st.ps(f"z{b}{h}", [P, HALF]) for h in range(2)] for b in range(2)]
        tr = [st.ps(f"tr{h}", [P, HALF]) for h in range(2)]
        s_th, s_gate, s_lse, s_sub, s_e, s_wt, s_o, s_c, s_comb, s_tr, s_y, s_hi, s_lo = (
            st.sem(x) for x in ("th_s", "gate_s", "lse_s", "sub", "e", "wt", "o_s", "chain", "comb_s", "tr_s", "y_s", "hi_s", "lo_s"))
        s_down = st.sems("down", 2)
        block = st.block()
        g1 = lambda t3: t3.rearrange("p (m a) h -> p m a h", a=1).broadcast_to([P, tiles, NG, B_HEADS])

        @block.sync
        def _(sp):
            for g in range(NG):
                sp.dma_start(lse[:, :, g, :], lse_dram[g].rearrange("(m p) h -> p m h", p=P)).then_inc(s_lse, 16)

            def units(i):
                for b in range(2):
                    w.load(sp, b, i, 2 * i + b)
                for b in range(2):
                    m = 2 * i + b
                    wait(sp, s_comb, m)
                    for g in range(NG):
                        sp.dma_start(o[:, g, :], o_dram[g, bass.ds(m * P, P), :]).then_inc(s_o, 16)
            repeat(sp, pairs, units)

            def out(i):
                for b in range(2):
                    w.load(sp, b, pairs + i, 2 * pairs + 2 * i + b)
            repeat(sp, pairs, out)

        @block.scalar
        def _(act):
            w.split_hi(act, 0, 0)
            act.wait_ge(s_sub, 1)
            nc.scalar.activation(lse[:, :, :, :], lse[:, :, :, :], ACT.Exp).then_inc(s_e, 1)

            def units(i):
                for b in range(2):
                    w.split_hi(act, 1 - b, i + b)
                    act.wait_ge(w.multiplied[b], i + 1)
                    wait(act, s_gate, 2 * i + b)
                    for h in range(2):
                        last = nc.scalar.activation(th[:, h * HALF:h * HALF + HALF], z[b][h][:, :], ACT.Tanh, scale=0.5)
                    last.then_inc(s_th, 1)
            repeat(act, pairs, units)
            for m in range(tiles):
                for c in range(2):
                    n = 2 * m + c
                    act.wait_ge(s_y, n + 1)
                    nc.scalar.activation(hi[:, 4 * c:4 * c + 4, m * P:m * P + P], y[c][:, :, :], ACT.Copy).then_inc(s_hi, 1)

            def out(i):
                for b in range(2):
                    if b == 0 or not (isinstance(i, int) and i == pairs - 1):
                        w.split_hi(act, 1 - b, pairs + i + b)
            repeat(act, pairs, out)

        @block.tensor
        def _(pe):
            def units(i):
                for b in range(2):
                    pe.wait_ge(w.lo_done[b], i + 1)
                    wait(pe, s_gate, 2 * i + b - 1)
                    for h in range(2):
                        last = w.products(z[b][h][:, :], b, hi, lo, slice(h * HALF, h * HALF + HALF))
                    last.then_inc(w.multiplied[b], 1)
            repeat(pe, pairs, units)
            for m in range(tiles):
                pe.wait_ge(s_comb, m + 1)
                for c in range(2):
                    n = 2 * m + c
                    wait(pe, s_y, n - 1)
                    for k in range(4):
                        last = nc.tensor.transpose(tr[c][:, k * P:k * P + P], comb[:, m, (4 * c + k) * P:(4 * c + k + 1) * P], ident)
                    last.then_inc(s_tr, 1)
            pe.wait_ge(s_lo, 2 * tiles)

            def out(i):
                for b in range(2):
                    pe.wait_ge(w.lo_done[b], pairs + i + 1)
                    wait(pe, s_down[b], i)
                    for h in range(2):
                        last = w.products(z[b][h][:, :], b, hi, lo, slice(h * HALF, h * HALF + HALF))
                    last.then_inc(w.multiplied[b], 1)
            repeat(pe, pairs, out)

        @block.vector
        def _(dve):
            c1 = Chain(dve, s_c)
            w.split_lo(dve, 0, 0)
            dve.wait_ge(s_lse, 16 * NG)
            c1.link(nc.vector.tensor_tensor(top[:, :, :], lse[:, :, 0, :], lse[:, :, 1, :], ALU.max))
            c1.link(nc.vector.tensor_tensor(top[:, :, :], top[:, :, :], lse[:, :, 2, :], ALU.max))
            for g in range(NG):
                last = nc.vector.tensor_tensor(lse[:, :, g, :], lse[:, :, g, :], top[:, :, :], ALU.subtract)
            last.then_inc(s_sub, 1)
            dve.wait_ge(s_e, 1)
            c1.link(nc.vector.tensor_tensor(total[:, :, :], lse[:, :, 0, :], lse[:, :, 1, :], ALU.add))
            c1.link(nc.vector.tensor_tensor(total[:, :, :], total[:, :, :], lse[:, :, 2, :], ALU.add))
            c1.link(nc.vector.reciprocal(total[:, :, :], total[:, :, :]))
            for g in range(NG):
                last = nc.vector.tensor_tensor(lse[:, :, g, :], lse[:, :, g, :], total[:, :, :], ALU.mult)
            c1.link(last)
            first = c1.n

            def units(i):
                c1.base, c1.n = first + 6 * i, 0
                for b in range(2):
                    m = 2 * i + b
                    w.split_lo(dve, 1 - b, i + b)
                    dve.wait_ge(s_o, 16 * NG * (m + 1))
                    for g in range(NG):
                        v3 = o[:, g, :].rearrange("p (h c) -> p h c", h=B_HEADS)
                        wt = lse[:, bass.ds(m, 1), g, :].rearrange("p a h -> p h a").broadcast_to([P, B_HEADS, 64])
                        last = nc.vector.tensor_tensor(v3, v3, wt, ALU.mult)
                    c1.link(last)
                    c1.link(nc.vector.tensor_tensor(o[:, 0, :], o[:, 0, :], o[:, 1, :], ALU.add))
                    nc.vector.tensor_tensor(comb[:, bass.ds(m, 1), :].rearrange("p a c -> p (a c)"), o[:, 0, :], o[:, 2, :],
                                            ALU.add).then_inc(s_comb, 1)
                    dve.wait_ge(s_th, m + 1)
                    c1.link(nc.vector.tensor_scalar(th[:, :], th[:, :], 0.5, 0.5, ALU.mult, ALU.add))
                    for h in range(2):
                        hs = slice(h * HALF, h * HALF + HALF)
                        last = nc.vector.tensor_tensor(gate[:, bass.ds(m, 1), hs].rearrange("p a t -> p (a t)"), th[:, hs],
                                                       z[b][h][:, :], ALU.mult)
                    last.then_inc(s_gate, 1)
                assert c1.n == 6
            repeat(dve, pairs, units)
            dve.wait_ge(s_gate, 2 * pairs)
            dve.wait_ge(w.multiplied[0], pairs)
            dve.wait_ge(w.multiplied[1], pairs)
            for m in range(tiles):
                for c in range(2):
                    n = 2 * m + c
                    dve.wait_ge(s_tr, n + 1)
                    wait(dve, s_lo, n - 1)
                    wait(dve, s_hi, n - 1)
                    tr3 = tr[c][:, :].rearrange("p (k t) -> p k t", t=P)
                    nc.vector.tensor_tensor(y[c][:, :, :], tr3, gate[:, 4 * c:4 * c + 4, m * P:m * P + P], ALU.mult).then_inc(s_y, 1)
                    dve.wait_ge(s_hi, n + 1)
                    nc.vector.tensor_tensor(lo[:, 4 * c:4 * c + 4, m * P:m * P + P], y[c][:, :, :],
                                            hi[:, 4 * c:4 * c + 4, m * P:m * P + P].bitcast(F32), ALU.subtract).then_inc(s_lo, 1)

            def out(i):
                for b in range(2):
                    if b == 0 or not (isinstance(i, int) and i == pairs - 1):
                        w.split_lo(dve, 1 - b, pairs + i + b)
                    dve.wait_ge(w.multiplied[b], pairs + i + 1)
                    for h in range(2):
                        last = nc.vector.tensor_copy(yo[:, bass.ds(2 * i + b, 1), h * HALF:h * HALF + HALF].rearrange("p a t -> p (a t)"),
                                                     z[b][h][:, :])
                    last.then_inc(s_down[b], 1)
            repeat(dve, pairs, out)


L2 = T + P
PIECE = L2 // 3


U_Z, U_HQ, U_HG, U_SQ, U_SK, U_SV, U_X, U_DT, U_HF, U_HI = 0, 4, 6, 8, 10, 12, 14, 22, 23, 25
N_SILU, N_UNITS = 8, 27


def second_projection(nc, hi, lo, w_in, proj):
    turns = N_UNITS // 3
    with Stage(nc, "ci") as st:
        w = Weights(st, w_in, buffers=3)
        out = [st.sb(f"out{b}", [P, L2]) for b in range(3)]
        th = [st.sb(f"th{j}", [P, PIECE]) for j in range(3)]
        z = [st.ps(f"z{j}", [P, HALF]) for j in range(3)]
        s_piece, s_th, s_out, s_left, s_c = st.sems("piece", 3), st.sems("th_s", 3), st.sems("out_s", 3), st.sems("left", 3), st.sem("chain")
        block = st.block()

        def schedule(eng, turn):
            full = N_SILU // 3
            turn(0, 3)
            for i in range(1, full):
                turn(i, 3)
            turn(full, N_SILU % 3)
            with eng.Fori(full + 1, turns - 1) as i:
                turn(i, 0)
            turn(turns - 1, 0)

        @block.sync
        def _(sp):
            def turn(i):
                for b in range(3):
                    w.load(sp, b, i, 3 * i + b)
            repeat(sp, turns, turn)

        @block.scalar
        def _(act):
            w.split_hi(act, 0, 0)

            def turn(i, silus):
                for b in range(3):
                    if b < 2:
                        w.split_hi(act, b + 1, i, free=(s_piece[2], 3 * i + b - 1))
                    elif not (isinstance(i, int) and i == turns - 1):
                        w.split_hi(act, 0, i + 1, free=(s_piece[2], 3 * i + 1))
                    wait(act, s_left[b], 16 * i)
                    for j in range(3):
                        act.wait_ge(s_piece[j], 3 * i + b + 1)
                        if b < silus:
                            wait(act, s_out[j], 3 * i + b)
                            nc.scalar.activation(th[j][:, :], z[j][:, 0:PIECE], ACT.Tanh, scale=0.5).then_inc(s_th[j], 1)
                        else:
                            nc.scalar.activation(out[b][:, j * PIECE:(j + 1) * PIECE], z[j][:, 0:PIECE], ACT.Copy).then_inc(s_out[j], 1)
                    for j in range(3):
                        act.wait_ge(s_out[j], 3 * i + b + 1)
                    act.dma_start(proj[bass.ds(3 * i + b, 1), :, :].rearrange("a p t -> p (a t)"), out[b][:, :]).then_inc(s_left[b], 16)
            schedule(act, turn)
            for b in range(3):
                act.wait_ge(s_left[b], 16 * turns)

        @block.tensor
        def _(pe):
            def turn(i):
                for b in range(3):
                    pe.wait_ge(w.lo_done[b], i + 1)
                    for j in range(3):
                        wait(pe, s_out[j], 3 * i + b)
                        last = w.products(z[j][:, 0:PIECE], b, hi, lo, slice(j * PIECE, (j + 1) * PIECE))
                        last.then_inc(s_piece[j], 1)
            repeat(pe, turns, turn)

        @block.vector
        def _(dve):
            chain = Chain(dve, s_c)
            w.split_lo(dve, 0, 0)

            def turn(i, silus):
                for b in range(3):
                    if b < 2:
                        w.split_lo(dve, b + 1, i)
                    elif not (isinstance(i, int) and i == turns - 1):
                        w.split_lo(dve, 0, i + 1)
                    if b < silus:
                        wait(dve, s_left[b], 16 * i)
                        for j in range(3):
                            dve.wait_ge(s_th[j], 3 * i + b + 1)
                            chain.link(nc.vector.tensor_scalar(th[j][:, :], th[j][:, :], 0.5, 0.5, ALU.mult, ALU.add))
                            nc.vector.tensor_tensor(out[b][:, j * PIECE:(j + 1) * PIECE], th[j][:, :], z[j][:, 0:PIECE],
                                                    ALU.mult).then_inc(s_out[j], 1)
            schedule(dve, turn)


SB_HEADS, HD = 4, 64
EXP_LN = "natural_log_exp_and_others"


def stick_breaking(nc, proj, q_gain, k_gain, out_gain, cst, o_cat):
    steps = []
    for qb in range(2):
        t0 = 1 + 4 * qb
        for kt in range(t0 + 3, -1, -1):
            first = max(kt, t0)
            steps.append((qb, kt, (first - 1) * P, (t0 + 4 - first) * P, kt >= t0))
    NS = len(steps)
    tri, strict, neg, blocks, row, rowneg, ones, ident = (cst[x] for x in ("suffix", "before", "not_before", "block64", "row_ok", "row_neg", "ones", "ident"))
    with Stage(nc, "sb") as st:
        raw = st.sb("raw", [P, L2])
        vraw = st.sb("vraw", [HD, L2])
        sq = st.sb("sq", [P, L2])
        ms = st.sb("ms", [P, L2])
        nrm = st.sb("nrm", [P, L2])
        q = st.sb("q", [HD, T])
        k = st.sb("k", [HD, L2])
        v_new = st.sb("v_new", [P, 9 * HD])
        v = st.sb("v", [P, 9 * HD])
        gain = st.sb("gain", [P, 1])
        eps4 = st.sb("eps4", [P, 1])
        og = st.sb("og", [P, SB_HEADS * HD])
        a = [st.sb(f"a{b}", [P, HALF]) for b in range(2)]
        zs = [st.sb(f"zs{b}", [P, HALF]) for b in range(2)]
        l = [st.sb(f"l{b}", [P, HALF]) for b in range(2)]
        sp_ = [st.sb(f"sp{b}", [P, HALF]) for b in range(2)]
        acc = st.sb("acc", [P, HALF])
        lw = [st.sb(f"lw{b}", [P, HALF]) for b in range(2)]
        wt = [st.sb(f"wt{b}", [P, HALF]) for b in range(2)]
        o = [st.sb(f"o{b}", [P, 4, HD]) for b in range(2)]
        osq = st.sb("osq", [P, 4, HD])
        oss = st.sb("oss", [P, 4])
        oln = st.sb("oln", [P, 4])
        orr = st.sb("orr", [P, 4])
        zb = [st.ps(f"z{b}", [P, HALF]) for b in range(2)]
        sb_ = [st.ps(f"sum{b}", [P, HALF]) for b in range(2)]
        ob = [st.ps(f"ob{b}", [P, HALF]) for b in range(2)]
        pb = [st.ps(f"pb{b}", [P, HALF]) for b in range(2)]
        (s_par, s_gain, s_raw, s_sq, s_blk, s_ms, s_rt, s_nrm, s_vt, s_vnew, s_cur, s_vcur, s_z, s_a, s_e, s_l, s_sp, s_sum, s_lw, s_acc, s_w,
         s_pv, s_oc, s_oss, s_oln, s_orr, s_of, s_odma, s_c, s_cp, s_zs) = (
            st.sem(x) for x in ("par", "gain_s", "raw_s", "sq_s", "blk", "ms_s", "rt", "nrm_s", "vt", "vnew", "cur", "vcur", "z_s", "a_s", "e_s", "l_s",
                                "sp_s", "sum_s", "lw_s", "acc_s", "w_s", "pv", "oc", "oss_s", "oln_s", "orr_s", "of", "odma", "chain", "chain_prep", "zs_s"))
        block = st.block()

        def schedule(eng, turn):
            turn(0)
            turn(1)
            with eng.Fori(2, SB_HEADS) as i:
                turn(i)
            turn(SB_HEADS)

        prep_of = lambda n: not (isinstance(n, int) and n == SB_HEADS)
        main_of = lambda n: not (isinstance(n, int) and n == 0)
        flat = proj.rearrange("u f t -> (u f) t")

        @block.sync
        def _(sp):
            sp.dma_start(gain[0:HD, :], q_gain).then_inc(s_par, 16)
            sp.dma_start(gain[HD:P, :], k_gain).then_inc(s_par, 16)
            sp.dma_start(og[:, :], bass.AP(out_gain.tensor, 0, [[0, P], [1, SB_HEADS * HD]])).then_inc(s_par, 16)

            def turn(n):
                if prep_of(n):
                    wait(sp, s_nrm, n)
                    sp.dma_start(raw[0:HD, :], flat[bass.ds(U_SQ * P + n * HD, HD), :]).then_inc(s_raw, 16)
                    sp.dma_start(raw[HD:P, :], flat[bass.ds(U_SK * P + n * HD, HD), :]).then_inc(s_raw, 16)
                    wait(sp, s_vt, n)
                    sp.dma_start(vraw[:, :], flat[bass.ds(U_SV * P + n * HD, HD), :]).then_inc(s_raw, 16)
                if main_of(n):
                    for qb in range(2):
                        sp.wait_ge(s_of, 2 * (n - 1) + qb + 1)
                        for x in range(4):
                            sp.dma_start(o_cat[(4 * qb + x) * P:(4 * qb + x + 1) * P, bass.ds((n - 1) * HD, HD)], o[qb][:, x, :]).then_inc(s_odma, 16)
                if prep_of(n):
                    sp.wait_ge(s_nrm, n + 1)
                    sp.dma_start(q[:, :], nrm[0:HD, P:L2]).then_inc(s_cur, 16)
                    sp.dma_start(k[:, :], nrm[HD:P, :]).then_inc(s_cur, 16)
            schedule(sp, turn)
            sp.wait_ge(s_odma, 16 * 8 * SB_HEADS)

        @block.scalar
        def _(act):
            act.wait_ge(s_par, 49)
            nc.scalar.preload_act_table_set(EXP_LN)

            def turn(n):
                for s in range(NS + 3):
                    if prep_of(n):
                        if s == 1:
                            act.wait_ge(s_raw, 48 * n + 48)
                            wait(act, s_blk, 3 * n)
                            nc.scalar.activation(sq[:, :], raw[:, :], ACT.Square).then_inc(s_sq, 1)
                        if s == 6:
                            act.wait_ge(s_ms, 3 * n + 3)
                            nc.scalar.activation(ms[:, :], ms[:, :], ACT.Sqrt).then_inc(s_rt, 1)
                            nc.scalar.preload_act_table_set(EXP_LN)
                    if not main_of(n):
                        continue
                    c = NS * (n - 1) + s
                    if s < NS:
                        qb, kt, q0, N, diag = steps[s]
                        act.wait_ge(s_z, c + 1)
                        nc.scalar.activation(a[s % 2][:, 0:N], zb[s % 2][:, 0:N], ACT.Abs).then_inc(s_a, 1)
                        act.wait_ge(s_a, c + 1)
                        nc.scalar.activation(a[s % 2][:, 0:N], a[s % 2][:, 0:N], ACT.Exp, scale=-1.0).then_inc(s_e, 1)
                        act.wait_ge(s_e, c + 1)
                        wait(act, s_sp, c - 1)
                        nc.scalar.activation(l[s % 2][:, 0:N], a[s % 2][:, 0:N], ACT.Ln, bias=1.0).then_inc(s_l, 1)
                    if 1 <= s <= NS:
                        qb, kt, q0, N, diag = steps[s - 1]
                        b = (s - 1) % 2
                        act.wait_ge(s_lw, c)
                        wait(act, s_pv, c - 2)
                        nc.scalar.activation(wt[b][:, 0:N], lw[b][:, 0:N], ACT.Exp, bias=rowneg if kt == 0 else 0.0).then_inc(s_w, 1)
                    if s - 3 in (4, NS - 1):
                        qb = int(s - 3 != 4)
                        m = 2 * (n - 1) + qb
                        act.wait_ge(s_oss, m + 1)
                        nc.scalar.activation(oln[:, :], oss[:, :], ACT.Ln, scale=1.0 / HD, bias=eps4[:, :]).then_inc(s_oln, 1)
                        act.wait_ge(s_oln, m + 1)
                        nc.scalar.activation(orr[:, :], oln[:, :], ACT.Exp, scale=-0.5).then_inc(s_orr, 1)
            schedule(act, turn)

        @block.tensor
        def _(pe):
            def z_of(n, s):
                qb, kt, q0, N, diag = steps[s]
                c = NS * (n - 1) + s
                if s == 0:
                    pe.wait_ge(s_cur, 32 * n)
                wait(pe, s_zs, c - 1)
                nc.tensor.matmul(zb[s % 2][:, 0:N], k[:, kt * P:kt * P + P], q[:, q0:q0 + N], start=True, stop=True).then_inc(s_z, 1)

            def turn(n):
                if main_of(n):
                    z_of(n, 0)
                for s in range(NS + 1):
                    if prep_of(n):
                        if s == 2:
                            pe.wait_ge(s_sq, n + 1)
                            wait(pe, s_vnew, n)
                            for j in range(2):
                                nc.tensor.matmul(pb[j][:, 0:PIECE], blocks, sq[:, j * PIECE:(j + 1) * PIECE], start=True, stop=True).then_inc(s_blk, 1)
                        if s == 4:
                            pe.wait_ge(s_ms, 3 * n + 1)
                            nc.tensor.matmul(pb[0][:, 0:PIECE], blocks, sq[:, 2 * PIECE:3 * PIECE], start=True, stop=True).then_inc(s_blk, 1)
                        if s == 8:
                            pe.wait_ge(s_raw, 48 * n + 48)
                            pe.wait_ge(s_ms, 3 * n + 3)
                            for m in range(9):
                                last = nc.tensor.matmul(pb[m // 8][:, (m % 8) * HD:(m % 8 + 1) * HD], vraw[:, m * P:m * P + P], ident[0:HD, 0:HD],
                                                        start=True, stop=True)
                            last.then_inc(s_vt, 1)
                    if not main_of(n):
                        continue
                    c = NS * (n - 1) + s
                    if s + 1 < NS:
                        z_of(n, s + 1)
                    if s < NS:
                        qb, kt, q0, N, diag = steps[s]
                        old = P if diag else 0
                        pe.wait_ge(s_sp, c + 1)
                        wait(pe, s_acc, c)
                        wait(pe, s_lw, c - 1)
                        more = N > old
                        if old:
                            last = nc.tensor.matmul(sb_[s % 2][:, 0:old], tri, sp_[s % 2][:, 0:old], start=True, stop=True)
                        if more:
                            nc.tensor.matmul(sb_[s % 2][:, old:N], tri, sp_[s % 2][:, old:N], start=True, stop=False)
                            last = nc.tensor.matmul(sb_[s % 2][:, old:N], ones, acc[:, HALF - N + old:HALF], start=False, stop=True)
                        last.then_inc(s_sum, 1)
                    if s >= 1:
                        qb, kt, q0, N, diag = steps[s - 1]
                        if s == 1:
                            pe.wait_ge(s_vcur, n)
                        pe.wait_ge(s_w, c)
                        first = kt == 4 + 4 * qb
                        if first:
                            wait(pe, s_oc, 2 * (n - 1) + qb - 1)
                        for x in range(N // P):
                            y0 = 4 - N // P + x
                            last = nc.tensor.matmul(ob[qb][:, y0 * HD:y0 * HD + HD], wt[(s - 1) % 2][:, x * P:x * P + P],
                                                    v[:, kt * HD:kt * HD + HD], start=first, stop=kt == 0, skip_group_check=True)
                        last.then_inc(s_pv, 1)
            schedule(pe, turn)

        @block.vector
        def _(dve):
            nc.vector.memset(eps4[:, :], EPS)
            dve.wait_ge(s_par, 48)
            nc.vector.tensor_scalar(gain[0:HD, :], gain[0:HD, :], HD ** -0.5, None, ALU.mult).then_inc(s_par, 1)
            dve.wait_ge(s_par, 49)
            prep_chain, chain = Chain(dve, s_cp), Chain(dve, s_c)
            ends = {4: 0, NS - 1: 1}

            def turn(n):
                if prep_of(n):
                    prep_chain.start(n, 1)
                if main_of(n):
                    chain.start(n - 1, 22)
                for s in range(NS + 3):
                    if prep_of(n):
                        if s in (3, 5):
                            for j in ((0, 1) if s == 3 else (2,)):
                                dve.wait_ge(s_blk, 3 * n + j + 1)
                                nc.vector.tensor_scalar(ms[:, j * PIECE:(j + 1) * PIECE], pb[j % 2][:, 0:PIECE], 1.0 / HD, EPS,
                                                        ALU.mult, ALU.add).then_inc(s_ms, 1)
                        if s == 7:
                            dve.wait_ge(s_rt, n + 1)
                            prep_chain.link(nc.vector.reciprocal(sq[:, :], ms[:, :]))
                            wait(dve, s_cur, 32 * n)
                            nc.vector.scalar_tensor_tensor(nrm[:, :], raw[:, :], gain[:, 0:1], sq[:, :], ALU.mult, ALU.mult).then_inc(s_nrm, 1)
                        if s == 9:
                            dve.wait_ge(s_vt, n + 1)
                            nc.vector.tensor_copy(v_new[:, 0:8 * HD], pb[0][:, 0:8 * HD])
                            nc.vector.tensor_copy(v_new[:, 8 * HD:9 * HD], pb[1][:, 0:HD]).then_inc(s_vnew, 1)
                    if not main_of(n):
                        continue
                    c = NS * (n - 1) + s
                    if s < NS:
                        qb, kt, q0, N, diag = steps[s]
                        dve.wait_ge(s_z, c + 1)
                        dve.wait_ge(s_a, c + 1)
                        nc.vector.tensor_copy(zs[s % 2][:, 0:N], zb[s % 2][:, 0:N]).then_inc(s_zs, 1)
                    if 1 <= s <= NS:
                        qb, kt, q0, N, diag = steps[s - 1]
                        b = (s - 1) % 2
                        dve.wait_ge(s_sum, c)
                        wait(dve, s_w, c - 2)
                        last = nc.vector.tensor_tensor(lw[b][:, 0:N], zs[b][:, 0:N], sb_[b][:, 0:N], ALU.subtract)
                        if diag:
                            chain.link(last)
                            last = nc.vector.tensor_tensor(lw[b][:, 0:P], lw[b][:, 0:P], neg, ALU.add)
                        last.then_inc(s_lw, 1)
                        new = P if diag else 0
                        c0 = HALF - N
                        dve.wait_ge(s_sp, c)
                        wait(dve, s_acc, c - 1)
                        if new:
                            last = nc.vector.tensor_copy(acc[:, c0:c0 + new], sp_[b][:, 0:new])
                        if N > new:
                            last = nc.vector.tensor_tensor(acc[:, c0 + new:HALF], acc[:, c0 + new:HALF], sp_[b][:, new:N], ALU.add)
                        last.then_inc(s_acc, 1)
                    if s < NS:
                        qb, kt, q0, N, diag = steps[s]
                        b = s % 2
                        dve.wait_ge(s_l, c + 1)
                        wait(dve, s_sum, c - 1)
                        dve.wait_ge(s_zs, c + 1)
                        last = nc.vector.scalar_tensor_tensor(sp_[b][:, 0:N], zs[b][:, 0:N], 0.0, l[b][:, 0:N], ALU.max, ALU.add)
                        if diag:
                            chain.link(last)
                            last = nc.vector.tensor_tensor(sp_[b][:, 0:P], sp_[b][:, 0:P], strict, ALU.mult)
                        if kt == 0:
                            chain.link(last)
                            last = nc.vector.tensor_scalar(sp_[b][:, 0:N], sp_[b][:, 0:N], row, None, ALU.mult)
                        last.then_inc(s_sp, 1)
                    if s - 3 in ends:
                        qb = ends[s - 3]
                        m = 2 * (n - 1) + qb
                        dve.wait_ge(s_pv, NS * (n - 1) + s - 2)
                        wait(dve, s_odma, 64 * (m - 1))
                        nc.vector.tensor_copy(o[qb][:, :, :], ob[qb][:, 0:4 * HD].rearrange("p (x c) -> p x c", x=4)).then_inc(s_oc, 1)
                        dve.wait_ge(s_oc, m + 1)
                        chain.link(nc.vector.tensor_tensor(osq[:, :, :], o[qb][:, :, :], o[qb][:, :, :], ALU.mult))
                        nc.vector.tensor_reduce(oss[:, :], osq[:, :, :], AX.X, ALU.add).then_inc(s_oss, 1)
                        dve.wait_ge(s_orr, m + 1)
                        chain.link(nc.vector.tensor_tensor(o[qb][:, :, :], o[qb][:, :, :],
                                                           orr[:, :].rearrange("p (x a) -> p x a", a=1).broadcast_to([P, 4, HD]), ALU.mult))
                        nc.vector.tensor_tensor(o[qb][:, :, :], o[qb][:, :, :],
                                                og[:, bass.ds((n - 1) * HD, HD)].rearrange("p (a c) -> p a c", a=1).broadcast_to([P, 4, HD]),
                                                ALU.mult).then_inc(s_of, 1)
                if prep_of(n):
                    dve.wait_ge(s_vnew, n + 1)
                    wait(dve, s_pv, NS * n)
                    nc.vector.tensor_copy(v[:, :], v_new[:, :]).then_inc(s_vcur, 1)
            schedule(dve, turn)


SSD_HEADS, GH = 8, 4
NCH = L2 // P
TAPS = 4


def ssd_conv(nc, proj, conv_w, conv_b, conv):
    units = 8
    pairs = units // 2
    with Stage(nc, "cv") as st:
        x = [st.sb(f"x{b}", [P, TAPS - 1 + L2]) for b in range(2)]
        y = [st.sb(f"y{b}", [P, L2]) for b in range(2)]
        th = [st.sb(f"th{b}", [P, L2]) for b in range(2)]
        taps = st.sb("taps", [P, units, TAPS])
        bias = st.sb("bias", [P, units])
        s_par, s_half, s_c, s_zero = (st.sem(v) for v in ("par", "half", "chain", "zero"))
        s_in, s_y, s_th, s_done, s_out = (st.sems(v, 2) for v in ("in", "y_s", "th_s", "done", "out"))
        block = st.block()

        @block.sync
        def _(sp):
            sp.dma_start(taps[:, :, :], conv_w).then_inc(s_par, 16)
            sp.dma_start(bias[:, :], conv_b).then_inc(s_par, 16)
            sp.wait_ge(s_zero, 1)

            def pair(i):
                for b in range(2):
                    wait(sp, s_done[b], i)
                    sp.dma_start(x[b][:, TAPS - 1:], proj[bass.ds(U_X + 2 * i + b, 1), :, :].rearrange("a p t -> p (a t)")).then_inc(s_in[b], 16)
            repeat(sp, pairs, pair)

        @block.scalar
        def _(act):
            def pair(i):
                for b in range(2):
                    act.wait_ge(s_y[b], i + 1)
                    wait(act, s_done[b], i)
                    nc.scalar.activation(th[b][:, :], y[b][:, :], ACT.Tanh).then_inc(s_th[b], 1)
                for b in range(2):
                    act.wait_ge(s_done[b], i + 1)
                    act.dma_start(conv[bass.ds(2 * i + b, 1), :, :].rearrange("a p t -> p (a t)"), y[b][:, :]).then_inc(s_out[b], 16)
            repeat(act, pairs, pair)
            for b in range(2):
                act.wait_ge(s_out[b], 16 * pairs)

        @block.vector
        def _(dve):
            chain = Chain(dve, s_c)
            for b in range(2):
                last = nc.vector.memset(x[b][:, 0:TAPS - 1], 0.0)
            last.then_inc(s_zero, 1)
            dve.wait_ge(s_zero, 1)
            dve.wait_ge(s_par, 32)
            nc.vector.tensor_scalar(taps[:, :, :], taps[:, :, :], 0.5, None, ALU.mult).then_inc(s_half, 1)
            nc.vector.tensor_scalar(bias[:, :], bias[:, :], 0.5, None, ALU.mult).then_inc(s_half, 1)
            dve.wait_ge(s_half, 2)

            def pair(i):
                chain.start(i, 8)
                for b in range(2):
                    unit = 2 * i + b
                    tap = lambda j: taps[:, bass.ds(unit, 1), j:j + 1].rearrange("p a b -> p (a b)")
                    dve.wait_ge(s_in[b], 16 * i + 16)
                    wait(dve, s_out[b], 16 * i)
                    chain.link(nc.vector.tensor_scalar(y[b][:, :], x[b][:, 0:L2], tap(0), bias[:, bass.ds(unit, 1)], ALU.mult, ALU.add))
                    for j in range(1, TAPS):
                        last = nc.vector.scalar_tensor_tensor(y[b][:, :], x[b][:, j:j + L2], tap(j), y[b][:, :], ALU.mult, ALU.add)
                        if j < TAPS - 1:
                            chain.link(last)
                    last.then_inc(s_y[b], 1)
                for b in range(2):
                    dve.wait_ge(s_th[b], i + 1)
                    chain.link(nc.vector.tensor_scalar(th[b][:, :], th[b][:, :], 1.0, None, ALU.add))
                    nc.vector.tensor_tensor(y[b][:, :], th[b][:, :], y[b][:, :], ALU.mult).then_inc(s_done[b], 1)
            repeat(dve, pairs, pair)


def ssd(nc, proj, conv, dt_bias, a_log, d_skip, gain, cst, o_cat):
    G = 2
    W = GH * HD
    with Stage(nc, "sd") as st:
        dtf = st.sb("dtf", [SSD_HEADS, L2])
        tmp = st.sb("tmp", [SSD_HEADS, L2])
        af = st.sb("af", [SSD_HEADS, L2])
        par = st.sb("par", [SSD_HEADS, 4])
        dt = st.sb("dt", [P, NCH, SSD_HEADS])
        a = st.sb("a", [P, NCH, SSD_HEADS])
        cum = st.sb("cum", [P, NCH, SSD_HEADS])
        ecum = st.sb("ecum", [P, NCH, SSD_HEADS])
        wend = st.sb("wend", [P, NCH, SSD_HEADS])
        elast = st.sb("elast", [P, NCH, SSD_HEADS])
        dsk = st.sb("dsk", [P, SSD_HEADS])
        gn = st.sb("gn", [P, G * W])
        xbc = st.sb("xbc", [P, 8, P])
        zf = st.sb("zf", [P, 4, P])
        x = st.sb("x", [P, SSD_HEADS, HD])
        xdt = st.sb("xdt", [P, SSD_HEADS, HD])
        xw = st.sb("xw", [P, SSD_HEADS, HD])
        ab = st.sb("ab", [P, SSD_HEADS, P])
        bt = st.sb("bt", [P, G, P])
        cbm = st.sb("cbm", [P, G, P])
        seg = [st.sb(f"seg{g}", [P, GH, P]) for g in range(G)]
        state = st.sb("state", [P, G, W])
        y = st.sb("y", [P, SSD_HEADS, HD])
        yd = st.sb("yd", [P, SSD_HEADS, HD])
        ysq = st.sb("ysq", [P, G, W])
        ss = st.sb("ss", [P, G])
        rms = st.sb("rms", [P, G])
        eps = st.sb("eps", [P, 1])
        pX = st.ps("pX", [P, HALF])
        pB = st.ps("pB", [P, HALF])
        pA = [st.ps(f"pA{g}", [P, HALF]) for g in range(G)]
        pD = st.ps("pD", [P, HALF])
        pO = st.ps("pO", [P, HALF])
        pS = st.ps("pS", [P, HALF])
        ident, upto, ones = cst["ident"], cst["upto"], cst["ones"]
        (s_in, s_par, s_v, s_e, s_c, s_tr, s_dt, s_cum, s_xbc, s_zf) = (
            st.sem(v) for v in ("in", "par_s", "v", "e", "chain", "tr", "dt_s", "cum_s", "xbc_s", "zf_s"))
        (s_xt, s_bt, s_cb, s_ab, s_zt, s_x, s_btc, s_cbm, s_seg, s_es, s_m, s_yd, s_yo, s_st, s_state, s_y, s_z, s_ss, s_rms, s_out,
         s_left, s_xw, s_yr, s_abc) = (
            st.sem(v) for v in ("xt", "bt_s", "cb", "ab", "zt", "x_s", "btc", "cbm_s", "seg_s", "es", "m", "yd_s", "yo", "st_s", "state_s", "y_s",
                                "z_s", "ss_s", "rms_s", "out", "left", "xw_s", "yr", "abc"))
        block = st.block()
        bc = lambda t2, n: t2.rearrange("p (h a) -> p h a", a=1).broadcast_to([P, t2.shape[1], n])
        row = lambda t, c: t[:, bass.ds(c, 1), :].rearrange("p a h -> p (a h)")

        @block.sync
        def _(sp):
            sp.dma_start(dtf[:, :], proj[U_DT, 0:SSD_HEADS, :]).then_inc(s_in, 16)
            sp.dma_start(par[:, 0:1], dt_bias).then_inc(s_in, 16)
            sp.dma_start(par[:, 1:2], a_log).then_inc(s_in, 16)
            sp.dma_start(dsk[:, :], bass.AP(d_skip.tensor, 0, [[0, P], [1, SSD_HEADS]])).then_inc(s_par, 16)
            sp.dma_start(gn[:, :], bass.AP(gain.tensor, 0, [[0, P], [1, G * W]])).then_inc(s_par, 16)

            def chunk(c):
                wait(sp, s_m, G * c)
                wait(sp, s_yo, c)
                sp.dma_start(xbc[:, :, :], conv[:, :, bass.ds(c * P, P)].rearrange("u p t -> p u t")).then_inc(s_xbc, 16)
                wait(sp, s_zt, c)
                sp.dma_start(zf[:, :, :], proj[U_Z:U_Z + 4, :, bass.ds(c * P, P)].rearrange("u p t -> p u t")).then_inc(s_zf, 16)
                if not (isinstance(c, int) and c == 0):
                    sp.wait_ge(s_out, c + 1)
                    sp.dma_start(o_cat[bass.ds((c - 1) * P, P), W:3 * W], y[:, :, :].rearrange("p h d -> p (h d)")).then_inc(s_left, 16)
            repeat(sp, NCH, chunk)
            sp.wait_ge(s_left, 16 * (NCH - 1))

        @block.scalar
        def _(act):
            act.wait_ge(s_in, 48)
            nc.scalar.preload_act_table_set(EXP_LN)
            nc.scalar.activation(par[:, 2:3], par[:, 1:2], ACT.Exp).then_inc(s_e, 1)
            act.wait_ge(s_v, 1)
            nc.scalar.activation(tmp[:, :], tmp[:, :], ACT.Exp, scale=-1.0).then_inc(s_e, 1)
            act.wait_ge(s_e, 2)
            nc.scalar.activation(tmp[:, :], tmp[:, :], ACT.Ln, bias=1.0).then_inc(s_e, 1)
            act.wait_ge(s_cum, 1)
            nc.scalar.activation(ecum[:, :, :], cum[:, :, :], ACT.Exp).then_inc(s_e, 1)
            nc.scalar.activation(wend[:, :, :], wend[:, :, :], ACT.Exp).then_inc(s_e, 1)
            nc.scalar.activation(elast[:, :, :], elast[:, :, :], ACT.Exp).then_inc(s_e, 1)

            def chunk(c):
                for g in range(G):
                    act.wait_ge(s_seg, G * c + g + 1)
                    nc.scalar.activation(seg[g][:, :, :], seg[g][:, :, :], ACT.Exp).then_inc(s_es, 1)
                act.wait_ge(s_ss, c + 1)
                nc.scalar.activation(rms[:, :], ss[:, :], ACT.Sqrt, scale=1.0 / W, bias=eps[:, :]).then_inc(s_rms, 1)
            repeat(act, NCH, chunk)

        @block.tensor
        def _(pe):
            for n, src in enumerate((dtf, af)):
                pe.wait_ge(s_v, 2 + n)
                for c in range(NCH):
                    last = nc.tensor.transpose(pA[n][:, c * SSD_HEADS:(c + 1) * SSD_HEADS], src[:, c * P:c * P + P], ident[0:SSD_HEADS, 0:SSD_HEADS])
                last.then_inc(s_tr, 1)
            pe.wait_ge(s_dt, 1)
            flat = a[:, :, :].rearrange("p c h -> p (c h)")
            nc.tensor.matmul(pD[:, 0:NCH * SSD_HEADS], upto, flat, start=True, stop=True)
            nc.tensor.matmul(pO[:, 0:NCH * SSD_HEADS], ones, flat, start=True, stop=True).then_inc(s_tr, 1)

            def chunk(c):
                pe.wait_ge(s_xbc, 16 * c + 16)
                wait(pe, s_z, c)
                for u in range(4):
                    last = nc.tensor.transpose(pX[:, u * P:u * P + P], xbc[:, u, :], ident)
                last.then_inc(s_xt, 1)
                wait(pe, s_cbm, G * c)
                for g in range(G):
                    last = nc.tensor.transpose(pB[:, g * P:g * P + P], xbc[:, 4 + g, :], ident)
                for g in range(G):
                    last = nc.tensor.matmul(pB[:, (2 + g) * P:(3 + g) * P], xbc[:, 4 + g, :], xbc[:, 6 + g, :], start=True, stop=True)
                last.then_inc(s_cb, 1)
                pe.wait_ge(s_abc, c + 1)
                for g in range(G):
                    wait(pe, s_seg, G * c - 1 + g)
                    for h in range(GH):
                        last = nc.tensor.matmul(pA[g][:, h * P:h * P + P], ab[:, g * GH + h, :], upto, start=True, stop=True)
                    last.then_inc(s_ab, 1)
                pe.wait_ge(s_x, c + 1)
                pe.wait_ge(s_zf, 16 * c + 16)
                for u in range(4):
                    last = nc.tensor.transpose(pX[:, u * P:u * P + P], zf[:, u, :], ident)
                last.then_inc(s_zt, 1)
                wait(pe, s_y, c)
                for g in range(G):
                    pe.wait_ge(s_m, G * c + g + 1)
                    for h in range(GH):
                        last = nc.tensor.matmul(pD[:, g * W + h * HD:g * W + (h + 1) * HD], seg[g][:, h, :], xdt[:, g * GH + h, :], start=True, stop=True)
                last.then_inc(s_yd, 1)
                pe.wait_ge(s_state, c + 1)
                for g in range(G):
                    last = nc.tensor.matmul(pO[:, g * W:(g + 1) * W], xbc[:, 6 + g, :], state[:, g, :], start=True, stop=True)
                last.then_inc(s_yo, 1)
                pe.wait_ge(s_xw, c + 1)
                pe.wait_ge(s_btc, c + 1)
                for g in range(G):
                    last = nc.tensor.matmul(pS[:, g * W:(g + 1) * W], bt[:, g, :], xw[:, g * GH:(g + 1) * GH, :], start=True, stop=True)
                last.then_inc(s_st, 1)
            repeat(pe, NCH, chunk)

        @block.vector
        def _(dve):
            chain = Chain(dve, s_c)
            pre = Chain(dve, s_yr)
            nc.vector.memset(eps[:, :], EPS)
            nc.vector.memset(state[:, :, :], 0.0).then_inc(s_state, 1)
            dve.wait_ge(s_in, 48)
            pre.link(nc.vector.tensor_scalar(dtf[:, :], dtf[:, :], par[:, 0:1], None, ALU.add))
            nc.vector.scalar_tensor_tensor(tmp[:, :], dtf[:, :], -1.0, dtf[:, :], ALU.mult, ALU.max).then_inc(s_v, 1)
            dve.wait_ge(s_e, 3)
            pre.link(nc.vector.scalar_tensor_tensor(dtf[:, :], dtf[:, :], 0.0, tmp[:, :], ALU.max, ALU.add))
            nc.vector.memset(dtf[:, 0:P - 16], 0.0).then_inc(s_v, 1)
            dve.wait_ge(s_v, 2)
            nc.vector.tensor_scalar(af[:, :], dtf[:, :], par[:, 2:3], -1.0, ALU.mult, ALU.mult).then_inc(s_v, 1)
            dve.wait_ge(s_tr, 2)
            nc.vector.tensor_copy(dt[:, :, :], pA[0][:, 0:NCH * SSD_HEADS].rearrange("p (c h) -> p c h", c=NCH))
            nc.vector.tensor_copy(a[:, :, :], pA[1][:, 0:NCH * SSD_HEADS].rearrange("p (c h) -> p c h", c=NCH)).then_inc(s_dt, 1)
            dve.wait_ge(s_tr, 3)
            pre.link(nc.vector.tensor_copy(cum[:, :, :], pD[:, 0:NCH * SSD_HEADS].rearrange("p (c h) -> p c h", c=NCH)))
            pre.link(nc.vector.tensor_copy(elast[:, :, :], pO[:, 0:NCH * SSD_HEADS].rearrange("p (c h) -> p c h", c=NCH)))
            nc.vector.tensor_tensor(wend[:, :, :], elast[:, :, :], cum[:, :, :], ALU.subtract).then_inc(s_cum, 1)
            dve.wait_ge(s_e, 6)
            dve.wait_ge(s_par, 32)

            def chunk(c):
                chain.start(c, 9)
                wait(dve, s_ab, G * c)
                nc.vector.tensor_copy(ab[:, :, :], bc(row(a, c), P)).then_inc(s_abc, 1)
                dve.wait_ge(s_xt, c + 1)
                wait(dve, s_st, c)
                wait(dve, s_yd, c)
                nc.vector.tensor_copy(x[:, :, :], pX[:, :].rearrange("p (h d) -> p h d", h=SSD_HEADS)).then_inc(s_x, 1)
                dve.wait_ge(s_x, c + 1)
                chain.link(nc.vector.tensor_tensor(xdt[:, :, :], x[:, :, :], bc(row(dt, c), HD), ALU.mult))
                nc.vector.tensor_tensor(xw[:, :, :], xdt[:, :, :], bc(row(wend, c), HD), ALU.mult).then_inc(s_xw, 1)
                dve.wait_ge(s_cb, c + 1)
                nc.vector.tensor_copy(bt[:, :, :], pB[:, 0:G * P].rearrange("p (g n) -> p g n", g=G)).then_inc(s_btc, 1)
                for g in range(G):
                    nc.vector.tensor_tensor(cbm[:, g, :], pB[:, (2 + g) * P:(3 + g) * P], upto, ALU.mult).then_inc(s_cbm, 1)
                for g in range(G):
                    dve.wait_ge(s_ab, G * c + g + 1)
                    chain.link(nc.vector.tensor_tensor(seg[g][:, :, :], pA[g][:, :].rearrange("p (h t) -> p h t", h=GH),
                                                       bc(row(cum, c)[:, g * GH:(g + 1) * GH], P), ALU.subtract))
                    nc.vector.tensor_scalar(seg[g][:, :, :], seg[g][:, :, :], 0.0, None, ALU.min).then_inc(s_seg, 1)
                for g in range(G):
                    dve.wait_ge(s_es, G * c + g + 1)
                    dve.wait_ge(s_cbm, G * c + g + 1)
                    nc.vector.tensor_tensor(seg[g][:, :, :], seg[g][:, :, :],
                                            cbm[:, g:g + 1, :].broadcast_to([P, GH, P]), ALU.mult).then_inc(s_m, 1)
                dve.wait_ge(s_yo, c + 1)
                dve.wait_ge(s_yd, c + 1)
                wait(dve, s_left, 16 * (c - 1))
                nc.vector.tensor_tensor(yd[:, :, :], x[:, :, :], bc(dsk[:, :], HD), ALU.mult)
                chain.link(nc.vector.tensor_tensor(y[:, :, :], pO[:, :].rearrange("p (h d) -> p h d", h=SSD_HEADS), bc(row(ecum, c), HD), ALU.mult))
                nc.vector.tensor_tensor(y[:, :, :], y[:, :, :], pD[:, :].rearrange("p (h d) -> p h d", h=SSD_HEADS), ALU.add).then_inc(s_y, 1)
                dve.wait_ge(s_y, c + 1)
                chain.link(nc.vector.tensor_tensor(y[:, :, :], y[:, :, :], yd[:, :, :], ALU.add))
                dve.wait_ge(s_st, c + 1)
                st3 = state[:, :, :].rearrange("p g (h d) -> p (g h) d", d=HD)
                chain.link(nc.vector.tensor_tensor(st3, st3, bc(row(elast, c), HD), ALU.mult))
                nc.vector.tensor_tensor(state[:, :, :], state[:, :, :], pS[:, :].rearrange("p (g w) -> p g w", g=G), ALU.add).then_inc(s_state, 1)
                dve.wait_ge(s_zt, c + 1)
                nc.vector.tensor_tensor(y[:, :, :], y[:, :, :], pX[:, :].rearrange("p (h d) -> p h d", h=SSD_HEADS), ALU.mult).then_inc(s_z, 1)
                dve.wait_ge(s_z, c + 1)
                y3 = y[:, :, :].rearrange("p (g h) d -> p g (h d)", g=G)
                chain.link(nc.vector.tensor_tensor(ysq[:, :, :], y3, y3, ALU.mult))
                nc.vector.tensor_reduce(ss[:, :], ysq[:, :, :], AX.X, ALU.add).then_inc(s_ss, 1)
                dve.wait_ge(s_rms, c + 1)
                chain.link(nc.vector.reciprocal(rms[:, :], rms[:, :]))
                chain.link(nc.vector.tensor_tensor(y3, y3, bc(rms[:, :], W), ALU.mult))
                nc.vector.tensor_tensor(y3, y3, gn[:, :].rearrange("p (g w) -> p g w", g=G), ALU.mult).then_inc(s_out, 1)
            repeat(dve, NCH, chunk)


LEVELS = 7
LN_TINY = float(np.log(1e-30))


def gated_recurrence(nc, proj, gain, cst, o_cat):
    NL = LEVELS + 1
    with Stage(nc, "hg") as st:
        raw = st.sb("raw", [P, 8, P])
        mag = st.sb("mag", [P, 2, P])
        soft = st.sb("soft", [P, 2, P])
        logf = st.sb("logf", [P, 2, P])
        key = st.sb("key", [P, 2, P])
        cum = st.sb("cum", [P, 2, P])
        ecum = st.sb("ecum", [P, 2, P])
        kend = st.sb("kend", [P, 2, P])
        qe = st.sb("qe", [P, 2, P])
        dist = st.sb("dist", [P, LEVELS, 2, P])
        dq = st.sb("dq", [P, LEVELS, 2, P])
        dk = st.sb("dk", [P, LEVELS, 2, P])
        tm = st.sb("tm", [P, 4, P])
        masked = [st.sb(f"masked{h}", [P, NL, P]) for h in range(2)]
        state = st.sb("state", [P, 2, P])
        add = st.sb("add", [P, 2, P])
        o = st.sb("o", [P, 4, HD])
        osq = st.sb("osq", [P, 4, HD])
        ss = st.sb("ss", [P, 4])
        ln = st.sb("ln", [P, 4])
        rr = st.sb("rr", [P, 4])
        gn = st.sb("gn", [P, 4 * HD])
        eps = st.sb("eps", [P, 1])
        one = st.sb("one", [P, P])
        sc = [st.ps(f"sc{h}", [P, NL * P]) for h in range(2)]
        pT = st.ps("pT", [P, HALF])
        pG = st.ps("pG", [P, HALF])
        pO = st.ps("pO", [P, HALF])
        pS = st.ps("pS", [P, HALF])
        ident, levels, block64 = cst["ident"], cst["levels"], cst["block64"]
        (s_raw, s_par, s_mag, s_em, s_soft, s_logf, s_lk, s_key, s_cum, s_ecum, s_end, s_kend, s_qe, s_dist, s_ed, s_dq, s_dk, s_tr, s_tm,
         s_sc, s_masked, s_op, s_sp, s_state, s_o, s_ss, s_ln, s_rr, s_gt, s_out, s_left, s_c, s_one, s_kz, s_o2, s_lz) = (
            st.sem(v) for v in ("raw_s", "par", "mag_s", "em", "soft_s", "logf_s", "lk", "key_s", "cum_s", "ecum_s", "end", "kend_s", "qe_s",
                                "dist_s", "ed", "dq_s", "dk_s", "tr", "tm_s", "sc_s", "masked_s", "op", "sp", "state_s", "o_s", "ss_s", "ln_s",
                                "rr_s", "gt", "out", "left", "chain", "one_s", "kz", "o2", "lz"))
        block = st.block()

        @block.sync
        def _(sp):
            sp.dma_start(gn[:, :], bass.AP(gain.tensor, 0, [[0, P], [1, 4 * HD]])).then_inc(s_par, 16)

            def chunk(c):
                wait(sp, s_sc, 2 * c)
                wait(sp, s_gt, c)
                wait(sp, s_kend, c)
                wait(sp, s_dq, c)
                cols = bass.ds(c * P, P)
                sp.dma_start(raw[:, 0:4, :], proj[U_HQ:U_HQ + 4, :, cols].rearrange("u p t -> p u t")).then_inc(s_raw, 16)
                sp.dma_start(raw[:, 4:8, :], proj[U_HF:U_HF + 4, :, cols].rearrange("u p t -> p u t")).then_inc(s_raw, 16)
                if not (isinstance(c, int) and c == 0):
                    sp.wait_ge(s_out, c + 1)
                    sp.dma_start(o_cat[bass.ds((c - 1) * P, P), 3 * 4 * HD:], o[:, :, :].rearrange("p h d -> p (h d)")).then_inc(s_left, 16)
            repeat(sp, NCH, chunk)
            sp.wait_ge(s_left, 16 * (NCH - 1))

        @block.scalar
        def _(act):
            nc.scalar.preload_act_table_set(EXP_LN)
            act.wait_ge(s_one, 1)

            def chunk(c):
                act.wait_ge(s_raw, 32 * c + 32)
                wait(act, s_lk, c)
                nc.scalar.activation(mag[:, :, :], raw[:, 4:6, :], ACT.Abs).then_inc(s_mag, 1)
                act.wait_ge(s_mag, c + 1)
                nc.scalar.activation(mag[:, :, :], mag[:, :, :], ACT.Exp, scale=-1.0).then_inc(s_em, 1)
                act.wait_ge(s_em, c + 1)
                nc.scalar.activation(soft[:, :, :], mag[:, :, :], ACT.Ln, bias=1.0).then_inc(s_soft, 1)
                act.wait_ge(s_lk, c + 1)
                nc.scalar.activation(key[:, :, :], key[:, :, :], ACT.Exp, scale=-1.0).then_inc(s_key, 1)
                act.wait_ge(s_cum, c + 1)
                wait(act, s_state, c)
                nc.scalar.activation(ecum[:, :, :], cum[:, :, :], ACT.Exp).then_inc(s_ecum, 1)
                wait(act, s_tr, c)
                for hp in range(2):
                    last = nc.scalar.activation(kend[:, hp, :], cum[:, hp, :], ACT.Exp, scale=-1.0, bias=cum[:, hp, P - 1:P])
                last.then_inc(s_end, 1)
                act.wait_ge(s_dist, c + 1)
                nc.scalar.activation(dist[:, :, :, :], dist[:, :, :, :], ACT.Exp).then_inc(s_ed, 1)
                act.wait_ge(s_tr, c + 1)
                nc.scalar.activation(tm[:, :, :], pT[:, :].rearrange("p (u t) -> p u t", u=4), ACT.Copy).then_inc(s_tm, 1)
                act.wait_ge(s_ss, c + 1)
                nc.scalar.activation(ln[:, :], ss[:, :], ACT.Ln, scale=1.0 / HD, bias=eps[:, :]).then_inc(s_ln, 1)
                act.wait_ge(s_ln, c + 1)
                nc.scalar.activation(rr[:, :], ln[:, :], ACT.Exp, scale=-0.5).then_inc(s_rr, 1)
            repeat(act, NCH, chunk)

        @block.gpsimd
        def _(pool):
            def chunk(c):
                pool.wait_ge(s_ed, c + 1)
                pool.wait_ge(s_key, c + 1)
                if isinstance(c, int) and c == 0:
                    pool.wait_ge(s_kz, 1)
                wait(pool, s_sc, 2 * c)
                nc.gpsimd.tensor_tensor(dk[:, :, :, :].rearrange("p l h t -> p l (h t)"), dist[:, :, :, :].rearrange("p l h t -> p l (h t)"),
                                        key[:, :, :].rearrange("p (a h) t -> p a (h t)", a=1).broadcast_to([P, LEVELS, 2 * P]),
                                        ALU.mult).then_inc(s_dk, 1)
            repeat(pool, NCH, chunk)

        @block.tensor
        def _(pe):
            def chunk(c):
                pe.wait_ge(s_kend, c + 1)
                wait(pe, s_tm, c)
                for u in range(2):
                    nc.tensor.transpose(pT[:, u * P:u * P + P], kend[:, u, :], ident)
                for u in range(2):
                    last = nc.tensor.transpose(pT[:, (2 + u) * P:(3 + u) * P], raw[:, 6 + u, :], ident)
                last.then_inc(s_tr, 1)
                wait(pe, s_out, c)
                for u in range(2):
                    last = nc.tensor.transpose(pG[:, u * P:u * P + P], raw[:, 2 + u, :], ident)
                last.then_inc(s_gt, 1)
                pe.wait_ge(s_dq, c + 1)
                pe.wait_ge(s_dk, c + 1)
                pe.wait_ge(s_qe, c + 1)
                for hp in range(2):
                    wait(pe, s_masked, 4 * c + 2 * hp)
                    for l in range(NL):
                        for h in range(2):
                            hs = slice(64 * h, 64 * h + 64)
                            k_l = dk[hs, l, hp, :] if l < LEVELS else key[hs, hp, :]
                            q_l = dq[hs, l, hp, :] if l < LEVELS else raw[hs, hp, :]
                            last = nc.tensor.matmul(sc[h][:, l * P:l * P + P], k_l, q_l, start=True, stop=True)
                    last.then_inc(s_sc, 1)
                    if hp == 0:
                        wait(pe, s_o, c)
                        pe.wait_ge(s_tm, c + 1)
                    pe.wait_ge(s_state, c + 1)
                    nc.tensor.matmul(pO[:, hp * P:hp * P + P], qe[:, hp, :], state[:, hp, :], start=True, stop=False, skip_group_check=True)
                    for h in range(2):
                        pe.wait_ge(s_masked, 4 * c + 2 * hp + h + 1)
                        for l in range(NL):
                            last = nc.tensor.matmul(pO[:, hp * P + h * HD:hp * P + (h + 1) * HD], masked[h][:, l, :],
                                                    tm[:, 2 + hp, h * HD:(h + 1) * HD], start=False, stop=l == NL - 1, skip_group_check=True)
                    last.then_inc(s_op, 1)
                wait(pe, s_state, c + 1)
                for hp in range(2):
                    last = nc.tensor.matmul(pS[:, hp * P:hp * P + P], tm[:, hp, :], tm[:, 2 + hp, :], start=True, stop=True)
                last.then_inc(s_sp, 1)
            repeat(pe, NCH, chunk)

        @block.vector
        def _(dve):
            chain = Chain(dve, s_c)
            nc.vector.memset(eps[:, :], EPS)
            nc.vector.memset(state[:, :, :], 0.0).then_inc(s_state, 1)
            nc.vector.memset(one[:, :], 1.0).then_inc(s_one, 1)
            dve.wait_ge(s_one, 1)
            dve.wait_ge(s_par, 16)

            def chunk(c):
                first = isinstance(c, int) and c == 0
                chain.start(c, 4)
                dve.wait_ge(s_soft, c + 1)
                wait(dve, s_dk, c)
                wait(dve, s_sc, 2 * c)
                nc.vector.scalar_tensor_tensor(key[:, :, :], raw[:, 4:6, :], 0.0, soft[:, :, :], ALU.max, ALU.add).then_inc(s_lk, 1)
                chain.link(nc.vector.scalar_tensor_tensor(logf[:, :, :], raw[:, 4:6, :], 0.0, soft[:, :, :], ALU.min, ALU.subtract))
                chain.link(nc.vector.tensor_scalar(logf[:, :, :], logf[:, :, :], LN_TINY, None, ALU.max))
                if first:
                    nc.vector.memset(logf[:, :, 0:P - 16], 0.0).then_inc(s_lz, 1)
                    dve.wait_ge(s_lz, 1)
                for hp in range(2):
                    last = nc.vector.tensor_tensor_scan(cum[:, hp, :], one[:, :], logf[:, hp, :], 0.0, ALU.mult, ALU.add)
                last.then_inc(s_cum, 1)
                dve.wait_ge(s_cum, c + 1)
                flat = cum[:, :, :].rearrange("p h t -> p (h t)")
                for l in range(LEVELS):
                    B = 2 << l
                    half = B // 2
                    src = flat.rearrange("p (n b) -> p n b", b=B)
                    dst = dist[:, l, :, :].rearrange("p h t -> p (h t)").rearrange("p (n b) -> p n b", b=B)
                    ref = src[:, :, half - 1:half].broadcast_to([P, 2 * P // B, half])
                    nc.vector.tensor_tensor(dst[:, :, 0:half], ref, src[:, :, 0:half], ALU.subtract)
                    last = nc.vector.tensor_tensor(dst[:, :, half:B], src[:, :, half:B], ref, ALU.subtract)
                last.then_inc(s_dist, 1)
                dve.wait_ge(s_key, c + 1)
                if first:
                    nc.vector.memset(key[:, :, 0:P - 16], 0.0).then_inc(s_kz, 1)
                    dve.wait_ge(s_kz, 1)
                dve.wait_ge(s_end, c + 1)
                nc.vector.tensor_tensor(kend[:, :, :], kend[:, :, :], key[:, :, :], ALU.mult).then_inc(s_kend, 1)
                wait(dve, s_op, 2 * c)
                nc.vector.tensor_tensor(qe[:, :, :], ecum[:, :, :], raw[:, 0:2, :], ALU.mult).then_inc(s_qe, 1)
                dve.wait_ge(s_ed, c + 1)
                nc.vector.tensor_tensor(dq[:, :, :, :].rearrange("p l h t -> p l (h t)"), dist[:, :, :, :].rearrange("p l h t -> p l (h t)"),
                                        raw[:, 0:2, :].rearrange("p (a h) t -> p a (h t)", a=1).broadcast_to([P, LEVELS, 2 * P]),
                                        ALU.mult).then_inc(s_dq, 1)
                for hp in range(2):
                    dve.wait_ge(s_sc, 2 * c + hp + 1)
                    wait(dve, s_op, 2 * c + hp)
                    for h in range(2):
                        nc.vector.tensor_tensor(masked[h][:, :, :], sc[h][:, :].rearrange("p (l t) -> p l t", l=NL),
                                                levels.rearrange("p (l t) -> p l t", l=NL), ALU.mult).then_inc(s_masked, 1)
                dve.wait_ge(s_sp, c + 1)
                dve.wait_ge(s_op, 2 * c + 2)
                chain.link(nc.vector.tensor_tensor(add[:, :, :], pS[:, 0:2 * P].rearrange("p (h t) -> p h t", h=2),
                                                   block64.rearrange("p (a t) -> p a t", a=1).broadcast_to([P, 2, P]), ALU.mult))
                for hp in range(2):
                    last = nc.vector.scalar_tensor_tensor(state[:, hp, :], state[:, hp, :], ecum[:, hp, P - 1:P], add[:, hp, :], ALU.mult, ALU.add)
                last.then_inc(s_state, 1)
                wait(dve, s_left, 16 * (c - 1))
                nc.vector.tensor_copy(o[:, :, :], pO[:, 0:2 * P].rearrange("p (h d) -> p h d", d=HD)).then_inc(s_o, 1)
                dve.wait_ge(s_o, c + 1)
                chain.link(nc.vector.tensor_tensor(osq[:, :, :], o[:, :, :], o[:, :, :], ALU.mult))
                nc.vector.tensor_reduce(ss[:, :], osq[:, :, :], AX.X, ALU.add).then_inc(s_ss, 1)
                dve.wait_ge(s_rr, c + 1)
                nc.vector.tensor_tensor(o[:, :, :], o[:, :, :], rr[:, :].rearrange("p (h a) -> p h a", a=1).broadcast_to([P, 4, HD]), ALU.mult).then_inc(s_o2, 1)
                dve.wait_ge(s_o2, 2 * c + 1)
                nc.vector.tensor_tensor(o[:, :, :], o[:, :, :], gn[:, :].rearrange("p (h d) -> p h d", d=HD), ALU.mult).then_inc(s_o2, 1)
                dve.wait_ge(s_o2, 2 * c + 2)
                dve.wait_ge(s_gt, c + 1)
                nc.vector.tensor_tensor(o[:, :, :], o[:, :, :], pG[:, 0:2 * P].rearrange("p (h d) -> p h d", d=HD), ALU.mult).then_inc(s_out, 1)
            repeat(dve, NCH, chunk)


def mixers_output(nc, hi, lo, w_out, o_cat, ident, x):
    tiles = T // P
    pairs = KT // 2
    with Stage(nc, "mo") as st:
        w = Weights(st, w_out)
        o = [st.sb(f"o{b}", [P, D]) for b in range(2)]
        f = [st.sb(f"f{b}", [P, HALF]) for b in range(2)]
        z = [[st.ps(f"z{b}{h}", [P, HALF]) for h in range(2)] for b in range(2)]
        tr = [st.ps(f"tr{h}", [P, HALF]) for h in range(2)]
        s_o, s_added = st.sems("o_s", 2), st.sems("added", 2)
        s_tr, s_f, s_hi, s_lo = (st.sem(v) for v in ("tr_s", "f_s", "hi_s", "lo_s"))
        block = st.block()

        @block.sync
        def _(sp):
            for b in range(2):
                w.load(sp, b, 0, b)
            for m in range(tiles):
                wait(sp, s_tr, 2 * (m - 1))
                sp.dma_start(o[m % 2][:, :], o_cat[m * P:(m + 1) * P, :]).then_inc(s_o[m % 2], 16)

            def out(i):
                for b in range(2):
                    w.load(sp, b, i, 2 * i + b)
            with sp.Fori(1, pairs) as i:
                out(i)

        @block.scalar
        def _(act):
            w.split_hi(act, 0, 0)
            w.split_hi(act, 1, 0)
            for n in range(2 * tiles):
                m, c = n // 2, n % 2
                act.wait_ge(s_tr, n + 1)
                wait(act, s_lo, n - 1)
                nc.scalar.activation(f[c][:, :], tr[c][:, :], ACT.Copy).then_inc(s_f, 1)
                act.wait_ge(s_f, n + 1)
                nc.scalar.activation(hi[:, 4 * c:4 * c + 4, m * P:m * P + P], f[c][:, :].rearrange("p (k t) -> p k t", k=4), ACT.Copy).then_inc(s_hi, 1)
            with act.Fori(1, pairs) as i:
                for b in range(2):
                    w.split_hi(act, b, i)

        @block.tensor
        def _(pe):
            for n in range(2 * tiles):
                m, c = n // 2, n % 2
                pe.wait_ge(s_o[m % 2], 16 * (m // 2) + 16)
                wait(pe, s_f, n - 1)
                for k in range(4):
                    last = nc.tensor.transpose(tr[c][:, k * P:k * P + P], o[m % 2][:, (4 * c + k) * P:(4 * c + k + 1) * P], ident)
                last.then_inc(s_tr, 1)
            pe.wait_ge(s_lo, 2 * tiles)

            def out(i):
                for b in range(2):
                    pe.wait_ge(w.lo_done[b], i + 1)
                    wait(pe, s_added[b], i)
                    for h in range(2):
                        last = w.products(z[b][h][:, :], b, hi, lo, slice(h * HALF, h * HALF + HALF))
                    last.then_inc(w.multiplied[b], 1)
            repeat(pe, pairs, out)

        @block.vector
        def _(dve):
            w.split_lo(dve, 0, 0)
            w.split_lo(dve, 1, 0)
            for n in range(2 * tiles):
                m, c = n // 2, n % 2
                dve.wait_ge(s_hi, n + 1)
                at = (slice(None), slice(4 * c, 4 * c + 4), slice(m * P, m * P + P))
                nc.vector.tensor_tensor(lo[at], f[c][:, :].rearrange("p (k t) -> p k t", k=4), hi[at].bitcast(F32), ALU.subtract).then_inc(s_lo, 1)

            def out(i):
                for b in range(2):
                    dve.wait_ge(w.multiplied[b], i + 1)
                    for h in range(2):
                        dst = x[:, bass.ds(2 * i + b, 1), h * HALF:h * HALF + HALF].rearrange("p a t -> p (a t)")
                        last = nc.vector.tensor_tensor(dst, dst, z[b][h][:, :], ALU.add)
                    last.then_inc(s_added[b], 1)
                    if not (isinstance(i, int) and i == pairs - 1):
                        w.split_lo(dve, b, i + 1)
            repeat(dve, pairs, out)


def mlp(nc, hi, lo, w_mlp, x):
    quarters, pairs = 4, KT // 2
    with Stage(nc, "mlp") as st:
        w = Weights(st, w_mlp)
        h_hi = st.sb("h_hi", [P, KT, T], F32R)
        h_lo = st.sb("h_lo", [P, KT, T], F32R)
        r = [st.sb(f"r{b}", [P, T]) for b in range(2)]
        y = [st.sb(f"y{b}", [P, T]) for b in range(2)]
        z = [[st.ps(f"z{b}{h}", [P, HALF]) for h in range(2)] for b in range(2)]
        s_r, s_y, s_hi, s_lo, s_added = (st.sems(v, 2) for v in ("r_s", "y_s", "hi_s", "lo_s", "added"))
        block = st.block()
        total = 2 * quarters * pairs
        done = lambda i, qr, part: qr * 2 * pairs + part * pairs + i

        def schedule(eng, up, down):
            for qr in range(quarters):
                repeat(eng, pairs, lambda i: up(qr, i))
                repeat(eng, pairs, lambda i: down(qr, i))

        @block.sync
        def _(sp):
            def up(qr, i):
                for b in range(2):
                    w.load(sp, b, done(i, qr, 0), 2 * done(i, qr, 0) + b)

            def down(qr, i):
                for b in range(2):
                    w.load(sp, b, done(i, qr, 1), 2 * done(i, qr, 1) + b)
            schedule(sp, up, down)

        @block.scalar
        def _(act):
            w.split_hi(act, 0, 0)

            def ahead(n, b):
                if b == 0 or not (isinstance(n, int) and n == total - 1):
                    w.split_hi(act, 1 - b, n + b)

            def up(qr, i):
                n, j = done(i, qr, 0), qr * pairs + i
                for b in range(2):
                    ahead(n, b)
                    act.wait_ge(w.multiplied[b], n + 1)
                    wait(act, s_y[b], j)
                    for h in range(2):
                        hs = slice(h * HALF, h * HALF + HALF)
                        last = nc.scalar.activation(r[b][:, hs], z[b][h][:, :], ACT.Relu)
                    last.then_inc(s_r[b], 1)
                    act.wait_ge(s_y[b], j + 1)
                    nc.scalar.activation(h_hi[:, bass.ds(2 * i + b, 1), :].rearrange("p a t -> p (a t)"), y[b][:, :], ACT.Copy).then_inc(s_hi[b], 1)

            def down(qr, i):
                for b in range(2):
                    ahead(done(i, qr, 1), b)
            schedule(act, up, down)

        @block.tensor
        def _(pe):
            def unit(n, b, a_hi, a_lo):
                pe.wait_ge(w.lo_done[b], n + 1)
                for h in range(2):
                    last = w.products(z[b][h][:, :], b, a_hi, a_lo, slice(h * HALF, h * HALF + HALF))
                last.then_inc(w.multiplied[b], 1)

            def up(qr, i):
                for b in range(2):
                    wait(pe, s_y[b], qr * pairs + i)
                    wait(pe, s_added[b], qr * pairs)
                    unit(done(i, qr, 0), b, hi, lo)

            def down(qr, i):
                for b in range(2):
                    for c in range(2):
                        pe.wait_ge(s_lo[c], (qr + 1) * pairs)
                    wait(pe, s_added[b], qr * pairs + i)
                    unit(done(i, qr, 1), b, h_hi, h_lo)
            schedule(pe, up, down)

        @block.vector
        def _(dve):
            w.split_lo(dve, 0, 0)

            def ahead(n, b):
                if b == 0 or not (isinstance(n, int) and n == total - 1):
                    w.split_lo(dve, 1 - b, n + b)

            def up(qr, i):
                n, j = done(i, qr, 0), qr * pairs + i
                for b in range(2):
                    ahead(n, b)
                    dve.wait_ge(s_r[b], j + 1)
                    wait(dve, s_hi[b], j)
                    for h in range(2):
                        hs = slice(h * HALF, h * HALF + HALF)
                        last = nc.vector.tensor_tensor(y[b][:, hs], r[b][:, hs], z[b][h][:, :], ALU.mult)
                    last.then_inc(s_y[b], 1)
                    dve.wait_ge(s_hi[b], j + 1)
                    at = h_hi[:, bass.ds(2 * i + b, 1), :].rearrange("p a t -> p (a t)").bitcast(F32)
                    nc.vector.tensor_tensor(h_lo[:, bass.ds(2 * i + b, 1), :].rearrange("p a t -> p (a t)"), y[b][:, :], at,
                                            ALU.subtract).then_inc(s_lo[b], 1)

            def down(qr, i):
                n = done(i, qr, 1)
                for b in range(2):
                    ahead(n, b)
                    dve.wait_ge(w.multiplied[b], n + 1)
                    for h in range(2):
                        dst = x[:, bass.ds(2 * i + b, 1), h * HALF:h * HALF + HALF].rearrange("p a t -> p (a t)")
                        last = nc.vector.tensor_tensor(dst, dst, z[b][h][:, :], ALU.add)
                    last.then_inc(s_added[b], 1)
            schedule(dve, up, down)


def move(nc, name, pairs):
    with Stage(nc, name) as st:
        s = st.sem("moved")
        block = st.block()

        @block.sync
        def _(sp):
            for to, frm in pairs:
                sp.dma_start(to, frm).then_inc(s, 16)
            sp.wait_ge(s, 16 * len(pairs))


def constants():
    i, j = np.arange(P)[:, None], np.arange(P)[None, :]
    meta = P - 16
    parts = {
        "ident": i == j,
        "ones": (i >= 0) & (j >= 0),
        "suffix": i >= j,
        "before": i < j,
        "not_before": np.where(i < j, 0, -1e30),
        "block64": i // 64 == j // 64,
        "upto": i <= j,
        "row_ok": i >= meta,
        "row_neg": np.where(i >= meta, 0, -1e30),
        "levels": np.concatenate([(i // B == j // B) & (i % B < B // 2) & (j % B >= B // 2)
                                  for B in (2 << l for l in range(LEVELS))] + [i == j], 1),
    }
    where, at = {}, 0
    for name, m in parts.items():
        where[name] = (at, m.shape[1])
        at += m.shape[1]
    return np.concatenate([m.astype(np.float32) for m in parts.values()], 1), where


def bucket_tables():
    hot = np.zeros((REL_BUCKETS, len(GROUPS) * VEC), np.float32)
    far = np.full((B_HEADS, len(GROUPS) * VEC), FAR, np.float32)
    half, exact = REL_BUCKETS // 2, 8
    for g, (d, _) in enumerate(GROUPS):
        for e in range(VEC):
            rel = e - 191
            if abs(rel) > WINDOW:
                continue
            n = abs(rel * d)
            large = exact + int(np.float32(np.log(np.float32(max(n, 1)) / np.float32(exact))) / np.float32(np.log(1024 / exact)) * np.float32(half - exact))
            hot[(half if rel > 0 else 0) + (n if n < exact else min(large, half - 1)), g * VEC + e] = 1.0
            far[:, g * VEC + e] = 0.0
    return hot, far


def build(nc, a, out):
    vhat = nc.dram_tensor("vhat", [A_HEADS, P, KT, P], F32).ap()
    vecs = nc.dram_tensor("vecs", [len(GROUPS) * B_HEADS, VEC], F32).ap()
    tiles = nc.dram_tensor("bias_tiles", [len(GROUPS) * B_HEADS, P, 2 * P], F32).ap()
    o_dram = nc.dram_tensor("o_groups", [len(GROUPS), T, D], F32).ap()
    lse_dram = nc.dram_tensor("lse_groups", [len(GROUPS), T, B_HEADS], F32).ap()
    proj = nc.dram_tensor("proj", [N_UNITS, P, L2], F32).ap()
    conv = nc.dram_tensor("conv", [8, P, L2], F32).ap()
    o_cat = nc.dram_tensor("o_cat", [T, D], F32).ap()
    x_dram = nc.dram_tensor("x_kept", [2, P, KT, T], F32).ap()
    where = constants()[1]
    late = where["suffix"][0]
    total = sum(n for _, n in where.values())
    with Stage(nc, "all") as top:
        ident = top.sb("ident", [P, P])[:, :]
        ones = top.sb("ones", [P, P])[:, :]
        with Stage(nc, "ab") as ab:
            hi = ab.sb("hi", [P, KT, T], F32R)
            lo = ab.sb("lo", [P, KT, T], F32R)
            with Stage(nc, "x0") as st:
                x = st.sb("x", [P, KT, T])
                move(nc, "load0", [(x[:, :, :], a["x"]), (ident, a["cst"][:, 0:P]), (ones, a["cst"][:, P:2 * P])])
                norm_stage(nc, "n0", x, a["pre0"], ones, hi, lo, T)
            gmlp_values(nc, hi, lo, a["w_v"], vhat, ident)
            with Stage(nc, "r0") as st:
                yo = st.sb("yo", [P, KT, T])
                gmlp_gate(nc, hi, lo, a["w_ug"], vhat, a["ws_t"], a["b_s"], a["ln_g"], a["ln_b"], yo)
                x = st.sb("x", [P, KT, T])
                move(nc, "load1", [(x[:, :, :], a["x"])])
                norm_stage(nc, "n1", x, a["pre1"], ones, hi, lo, T, post=yo, post_gain=a["post0"])
                move(nc, "keep1", [(x_dram[0], x[:, :, :])])
            bias_vectors(nc, a["rel_bias"], a["hot"], a["far"], vecs, tiles)
            dilated_attention(nc, hi, lo, a["w_qkv"], tiles, o_dram, lse_dram, ident)
            with Stage(nc, "r1") as st:
                yo = st.sb("yo", [P, KT, T])
                attention_output(nc, hi, lo, a["w_bo"], o_dram, lse_dram, ident, yo)
                x = st.sb("x", [P, KT, T])
                move(nc, "load3", [(x[:, :, :], x_dram[0])])
                norm_stage(nc, "n2", x, None, ones, None, None, T, post=yo, post_gain=a["post1"])
                move(nc, "keep2", [(x_dram[1], x[:, :, :])])
        x = top.sb("x", [P, KT, T])
        with Stage(nc, "three") as st:
            hi = st.sb("hi", [P, KT, L2], F32R)
            lo = st.sb("lo", [P, KT, L2], F32R)
            with Stage(nc, "lead") as ld:
                lead = ld.sb("lead", [P, KT, P])
                move(nc, "load2", [(x[:, :, :], x_dram[1]), (lead[:, :, :], a["lead"])])
                norm_stage(nc, "n3", lead, a["pre2"], ones, hi, lo, P)
            norm_stage(nc, "n5", x, a["pre2"], ones, hi, lo, T, col0=P)
            second_projection(nc, hi, lo, a["w_in2"], proj)
        with Stage(nc, "mixers") as st:
            c = st.sb("cst", [P, total - late])
            cst = {name: c[:, at - late:at - late + n] for name, (at, n) in where.items() if at >= late}
            cst.update(ident=ident, ones=ones)
            move(nc, "load4", [(c[:, :], a["cst"][:, late:total])])
            stick_breaking(nc, proj, a["q_gain"], a["k_gain"], a["sb_gain"], cst, o_cat)
            ssd_conv(nc, proj, a["conv_w"], a["conv_b"], conv)
            ssd(nc, proj, conv, a["dt_bias"], a["a_log"], a["d_skip"], a["ssd_gain"], cst, o_cat)
            gated_recurrence(nc, proj, a["hg_gain"], cst, o_cat)
        hi = top.sb("hi", [P, KT, T], F32R)
        lo = top.sb("lo", [P, KT, T], F32R)
        mixers_output(nc, hi, lo, a["w_out2"], o_cat, ident, x)
        norm_stage(nc, "n4", x, a["pre3"], ones, hi, lo, T)
        mlp(nc, hi, lo, a["w_mlp"], x)
        move(nc, "store", [(out, x[:, :, :])])


def units(w):
    k, n = w.shape
    return w.reshape(k // P, P, n // P, P).transpose(2, 1, 0, 3).reshape(n // P, P, (k // P) * P)


def by_feature(x):
    return x.T.reshape(-1, P, x.shape[0]).transpose(1, 0, 2)


def vector(g):
    return g.reshape(-1, P).T


def layout(v):
    aw, bw, w2 = v["a_w_in"][0], v["b_w_in"][0], v["w_in_2"][0]
    u, g = units(aw[:, :2 * D]), units(aw[:, 4 * D:])
    ug = []
    for hf in range(2):
        for j in range(A_HEADS // 2):
            ug += [u[hf * 8 + j:hf * 8 + j + 1], g[hf * 8 + j:hf * 8 + j + 1]]
        ug.append(units(v["a_w_out"][0][hf * D:(hf + 1) * D]))
    qkv = []
    for gi in range(len(GROUPS)):
        three = [units(bw[:, (3 * gi + j) * D:(3 * gi + j + 1) * D]) for j in range(3)]
        for hp in range(B_PAIRS):
            qkv += [t[hp:hp + 1] for t in three]
    cut = np.cumsum([256, 256, 256, 512, 512, 256, 256, 8, 256, 256, 256])
    q, k, vv, z, xs, bm, cm, dt, hq, hf_, hi_, hg = np.split(w2, cut, axis=1)
    dt = np.concatenate([dt, np.zeros((D, P - 8), np.float32)], 1)
    in2 = units(np.concatenate([z, hq, hg, q, k, vv, xs, bm, cm, dt, hf_, hi_], 1))
    up = units(v["w_up_2"][0])
    mlp_w = []
    for qr in range(4):
        mlp_w += [up[8 * qr:8 * qr + 8], units(v["w_down_2"][0][qr * D:(qr + 1) * D])]
    lead = np.concatenate([np.zeros((P - 16, D), np.float32), v["meta_tokens_2"]], 0)
    hot, far = bucket_tables()
    return {
        "x": by_feature(v["x"][0]), "cst": constants()[0], "hot": hot, "far": far, "lead": by_feature(lead),
        "pre0": vector(v["norm_pre"][0]), "pre1": vector(v["norm_pre"][1]),
        "post0": vector(v["norm_post"][0]), "post1": vector(v["norm_post"][1]),
        "pre2": vector(v["norm_mix_w_2"][0]), "pre3": vector(v["norm_mlp_w_2"][0]),
        "w_v": units(aw[:, 2 * D:4 * D]), "w_ug": np.concatenate(ug), "ws_t": v["a_w_s"][0].transpose(0, 2, 1),
        "b_s": v["a_b_s"][0], "ln_g": v["a_vnorm_g"][0], "ln_b": v["a_vnorm_b"][0],
        "rel_bias": v["rel_bias"], "w_qkv": np.concatenate(qkv),
        "w_bo": np.concatenate([units(bw[:, 9 * D:]), units(v["b_w_out"][0])]),
        "w_in2": in2, "q_gain": v["sb_q_norm_2"].T, "k_gain": v["sb_k_norm_2"].T, "sb_gain": v["sb_out_norm_2"][0],
        "conv_w": v["ssd_conv_w_2"][0].reshape(TAPS, 8, P).transpose(2, 1, 0), "conv_b": vector(v["ssd_conv_b_2"][0]),
        "dt_bias": v["ssd_dt_bias_2"].T, "a_log": v["ssd_A_log_2"].T, "d_skip": v["ssd_D_2"][0],
        "ssd_gain": v["ssd_norm_w_2"][0], "hg_gain": v["hg_out_norm_2"][0],
        "w_out2": units(v["w_out_2"][0]), "w_mlp": np.concatenate(mlp_w),
    }


def kernel(**inputs):
    import numpy as _np
    import concourse.bacc as _bacc
    from concourse.bass_utils import run_bass_kernel_spmd as _run

    nc = _bacc.Bacc("TRN2", target_bir_lowering=False, num_devices=1)
    arrays, aps = {}, {}
    for name, a in layout({n: _np.asarray(v) for n, v in inputs.items()}).items():
        arrays[f"in_{name}"] = _np.ascontiguousarray(a)
        aps[name] = nc.dram_tensor(f"in_{name}", a.shape, F32, kind="ExternalInput").ap()
    out = nc.dram_tensor("out", [P, KT, T], F32, kind="ExternalOutput").ap()
    build(nc, aps, out)
    r = _run(nc, [arrays], core_ids=[0])
    y = r.results[0]["out"]
    return _np.ascontiguousarray(y.transpose(1, 0, 2).reshape(D, T).T).reshape(1, T, D)
```

```python
from contextlib import ExitStack

import numpy as np
import concourse.bass as bass
import concourse.mybir as mybir

F32 = mybir.dt.float32
F32R = mybir.dt.float32r
ACT = mybir.ActivationFunctionType
ALU = mybir.AluOpType
AX = mybir.AxisListType

P = 128
T = 1024
D = 1024
KT = D // P
EPS = 1e-6
HALF = 512


class Stage:

    def __init__(self, nc, name):
        self.nc, self.name, self.stack, self.used = nc, name, ExitStack(), []

    def __enter__(self):
        self.stack.__enter__()
        return self

    def __exit__(self, *a):
        self.stack.__exit__(*a)
        if self.used and a[0] is None:
            self.nc.clear_and_free_semaphores(self.used)
            self.nc.all_engine_barrier()

    def sb(self, name, shape, dt=F32):
        return self.stack.enter_context(self.nc.sbuf_tensor(f"{self.name}_{name}", shape, dt))

    def ps(self, name, shape):
        return self.stack.enter_context(self.nc.psum_tensor(f"{self.name}_{name}", shape, F32))

    def sem(self, name):
        self.used.append(self.nc.alloc_semaphore(f"{self.name}_{name}"))
        return self.used[-1]

    def sems(self, name, n):
        return [self.sem(f"{name}{i}") for i in range(n)]

    def block(self):
        return self.stack.enter_context(self.nc.Block())


def wait(eng, sem, value):
    if isinstance(value, int) and value <= 0:
        return
    eng.wait_ge(sem, value)


def repeat(eng, n, body):
    body(0)
    if n > 2:
        with eng.Fori(1, n - 1) as i:
            body(i)
    if n > 1:
        body(n - 1)


class Chain:

    def __init__(self, eng, sem):
        self.eng, self.sem, self.base, self.n = eng, sem, 0, 0

    def start(self, i, per):
        if self.n:
            assert self.per == self.n, (self.sem, self.per, self.n)
        self.base, self.n, self.per = i * per, 0, per

    def link(self, ins):
        ins.then_inc(self.sem, 1)
        self.n += 1
        self.eng.wait_ge(self.sem, self.base + self.n)


class Weights:

    def __init__(self, st, dram, buffers=2, ahead=False):
        self.nc, self.dram, self.nb, self.ahead = st.nc, dram, buffers, ahead
        self.raw = [st.sb(f"w_raw{b}", [P, KT * P]) for b in range(buffers)]
        self.hi = [st.sb(f"w_hi{b}", [P, KT * P], F32R) for b in range(buffers)]
        self.lo = [st.sb(f"w_lo{b}", [P, KT * P], F32R) for b in range(buffers)]
        self.loaded = st.sems("w_loaded", buffers)
        self.hi_done = st.sems("w_hi_done", buffers)
        self.lo_done = st.sems("w_lo_done", buffers)
        self.multiplied = st.sems("w_multiplied", buffers)

    def first_loads(self, sp):
        for b in range(self.nb):
            sp.dma_start(self.raw[b][:, :], self.dram[b]).then_inc(self.loaded[b], 16)

    def first_hi(self, act):
        act.wait_ge(self.loaded[0], 16)
        self.nc.scalar.activation(self.hi[0][:, :], self.raw[0][:, :], ACT.Copy).then_inc(self.hi_done[0], 1)

    def first_lo(self, dve):
        dve.wait_ge(self.hi_done[0], 1)
        self.nc.vector.tensor_tensor(self.lo[0][:, :], self.raw[0][:, :], self.hi[0][:, :].bitcast(F32),
                                     ALU.subtract).then_inc(self.lo_done[0], 1)

    def load(self, sp, b, n, unit):
        if self.ahead and isinstance(n, int) and n == 0:
            return
        wait(sp, self.lo_done[b], n)
        sp.dma_start(self.raw[b][:, :], self.dram[bass.ds(unit, 1), :, :].rearrange("a p n -> p (a n)")
                     ).then_inc(self.loaded[b], 16)

    def split_hi(self, act, b, n, free=None):
        if self.ahead and isinstance(n, int) and n == 0 and b == 0:
            return
        act.wait_ge(self.loaded[b], 16 * n + 16)
        wait(act, *(free or (self.multiplied[b], n)))
        self.nc.scalar.activation(self.hi[b][:, :], self.raw[b][:, :], ACT.Copy).then_inc(self.hi_done[b], 1)

    def split_lo(self, dve, b, n):
        if self.ahead and isinstance(n, int) and n == 0 and b == 0:
            return
        dve.wait_ge(self.hi_done[b], n + 1)
        self.nc.vector.tensor_tensor(self.lo[b][:, :], self.raw[b][:, :], self.hi[b][:, :].bitcast(F32),
                                     ALU.subtract).then_inc(self.lo_done[b], 1)

    def products(self, out, b, act_hi, act_lo, cols):
        for k in range(KT):
            w = slice(k * P, k * P + P)
            for m, (wp, ap) in enumerate(((self.hi, act_hi), (self.lo, act_hi), (self.hi, act_lo))):
                last = self.nc.tensor.matmul(out, wp[b][:, w], ap[:, k, cols],
                                             start=(k == 0 and m == 0), stop=(k == KT - 1 and m == 2))
        return last


def norm_stage(nc, name, x, gain, ones, hi, lo, tokens, post=None, post_gain=None, col0=0, w=None, x_from=None,
               x_to=None, copies=()):
    chunks = [(c, min(c + HALF, tokens)) for c in range(0, tokens, HALF)]
    jobs = ([("post", post, post_gain)] if post is not None else []) + [("pre", x, gain)]
    if hi is None:
        jobs = jobs[:1]
    with Stage(nc, name) as st:
        sq = [st.sb(f"sq{b}", [P, tokens]) for b in range(2)]
        acc = st.sb("acc", [P, tokens])
        rms = st.sb("rms", [P, tokens])
        inv = st.sb("inv", [P, tokens])
        h = [st.sb(f"h{b}", [P, tokens]) for b in range(2)]
        eps = st.sb("eps", [P, 1])
        gains = [st.sb(f"gain{j}", [P, KT]) for j in range(len(jobs))]
        total = [st.ps(f"total{c}", [P, HALF]) for c in range(len(chunks))]
        s_gain, s_eps, s_sq, s_acc, s_tot, s_rms, s_inv = (st.sem(n) for n in ("gain_s", "eps_s", "sq_s", "acc_s", "tot_s", "rms_s", "inv_s"))
        s_h, s_hi, s_lo, s_x, s_c, s_xin, s_moved, s_lo_odd = (st.sem(n) for n in ("h_s", "hi_s", "lo_s", "x_s", "chain", "x_in", "moved", "lo_odd"))
        block = st.block()

        @block.sync
        def _(sp):
            for j, (_, _, g) in enumerate(jobs):
                sp.dma_start(gains[j][:, :], g).then_inc(s_gain, 16)
            if x_from is not None:
                sp.dma_start(x[:, :, :], x_from).then_inc(s_xin, 16)
            if w:
                w.first_loads(sp)
            for to, frm in copies:
                sp.dma_start(to, frm).then_inc(s_moved, 16)
            if x_to is not None:
                sp.wait_ge(s_x, KT)
                sp.dma_start(x_to, x[:, :, :]).then_inc(s_moved, 16)
            wait(sp, s_moved, 16 * (len(copies) + (x_to is not None)))

        @block.scalar
        def _(act):
            act.wait_ge(s_eps, 1)
            for j, (kind, src, _) in enumerate(jobs):
                if j:
                    act.wait_ge(s_x, KT)
                for k in range(KT):
                    n = j * KT + k
                    wait(act, s_acc, n - 1)
                    nc.scalar.activation(sq[k % 2][:, :], src[:, k, 0:tokens], ACT.Square).then_inc(s_sq, 1)
                if w and j == len(jobs) - 1:
                    w.first_hi(act)
                act.wait_ge(s_tot, j + 1)
                for c, (a, b) in enumerate(chunks):
                    nc.scalar.activation(rms[:, a:b], total[c][:, 0:b - a], ACT.Sqrt, bias=eps[:, :],
                                         scale=1.0 / D).then_inc(s_rms, 1)
                if kind == "pre":
                    for k in range(KT):
                        act.wait_ge(s_h, k + 1)
                        nc.scalar.activation(hi[:, k, col0:col0 + tokens], h[k % 2][:, :], ACT.Copy).then_inc(s_hi, 1)

        @block.tensor
        def _(pe):
            for j in range(len(jobs)):
                pe.wait_ge(s_acc, (j + 1) * KT)
                for c, (a, b) in enumerate(chunks):
                    last = nc.tensor.matmul(total[c][:, 0:b - a], ones, acc[:, a:b], start=True, stop=True)
                last.then_inc(s_tot, 1)

        @block.vector
        def _(dve):
            chain = Chain(dve, s_c)
            nc.vector.memset(eps[:, :], EPS).then_inc(s_eps, 1)
            dve.wait_ge(s_gain, 16 * len(jobs))
            for j, (kind, src, _) in enumerate(jobs):
                for k in range(KT):
                    dve.wait_ge(s_sq, j * KT + k + 1)
                    if k == 0:
                        wait(dve, s_tot, j)
                        nc.vector.tensor_copy(acc[:, :], sq[0][:, :]).then_inc(s_acc, 1)
                    else:
                        dve.wait_ge(s_acc, j * KT + k)
                        nc.vector.tensor_tensor(acc[:, :], acc[:, :], sq[k % 2][:, :], ALU.add).then_inc(s_acc, 1)
                if w and j == len(jobs) - 1:
                    w.first_lo(dve)
                dve.wait_ge(s_rms, (j + 1) * len(chunks))
                chain.link(nc.vector.reciprocal(inv[:, :], rms[:, :]))
                for k in range(KT):
                    if kind == "post":
                        if x_from is not None and k == 0:
                            dve.wait_ge(s_xin, 16)
                        chain.link(nc.vector.scalar_tensor_tensor(h[k % 2][:, :], src[:, k, 0:tokens], gains[j][:, k:k + 1],
                                                                  inv[:, :], ALU.mult, ALU.mult))
                        nc.vector.tensor_tensor(x[:, k, 0:tokens], x[:, k, 0:tokens], h[k % 2][:, :], ALU.add).then_inc(s_x, 1)
                    else:
                        wait(dve, s_hi, k - 1)
                        wait(dve, (s_lo, s_lo_odd)[k % 2], k // 2)
                        if post is not None and k == 0:
                            dve.wait_ge(s_x, KT)
                        nc.vector.scalar_tensor_tensor(h[k % 2][:, :], src[:, k, 0:tokens], gains[j][:, k:k + 1],
                                                       inv[:, :], ALU.mult, ALU.mult).then_inc(s_h, 1)
                        if k % 2 == 1:
                            dve.wait_ge(s_hi, k)
                            nc.vector.tensor_tensor(lo[:, k - 1, col0:col0 + tokens], h[0][:, :],
                                                    hi[:, k - 1, col0:col0 + tokens].bitcast(F32), ALU.subtract).then_inc(s_lo, 1)

        @block.gpsimd
        def _(pool):
            if hi is None:
                return
            for k in range(1, KT, 2):
                pool.wait_ge(s_hi, k + 1)
                nc.gpsimd.tensor_tensor(lo[:, k, col0:col0 + tokens], h[1][:, :],
                                        hi[:, k, col0:col0 + tokens].bitcast(F32), ALU.subtract).then_inc(s_lo_odd, 1)


A_HEADS = 16


def gmlp_values(nc, hi, lo, w, vhat, ident):
    units = A_HEADS
    pairs = units // 2
    with Stage(nc, "av") as st:
        gelu = [st.sb(f"gelu{b}", [P, T]) for b in range(2)]
        v = st.sb("v", [P, KT, units * P])
        stats = st.sb("stats", [P, KT * 4, 6])
        mv = st.sb("mv", [P, KT, 2])
        sd = st.sb("sd", [P, KT])
        rstd = st.sb("rstd", [P, KT])
        shift = st.sb("shift", [P, KT])
        eps = st.sb("eps", [P, 1])
        z = [[st.ps(f"z{b}{h}", [P, HALF]) for h in range(2)] for b in range(2)]
        tr = [st.ps(f"tr{h}", [P, HALF]) for h in range(2)]
        s_gelu, s_tr = st.sems("gelu_s", 2), st.sems("tr_s", 2)
        s_copied = st.sems("copied", 2)
        s_eps, s_mv, s_sd, s_shift, s_vhat, s_out, s_c = (st.sem(n) for n in ("eps_s", "mv_s", "sd_s", "shift_s", "vhat_s", "out_s", "chain"))
        block = st.block()

        @block.sync
        def _(sp):
            def load_pair(i):
                for b in range(2):
                    w.load(sp, b, i, 2 * i + b)
            repeat(sp, pairs, load_pair)
            for m in range(KT):
                sp.wait_ge(s_vhat, m + 1)
                sp.dma_start(vhat[:, :, m, :].rearrange("j q d -> q j d"),
                             v[:, m, :].rearrange("p (j d) -> p j d", d=P)).then_inc(s_out, 16)
            sp.wait_ge(s_out, 16 * KT)

        @block.scalar
        def _(act):
            w.split_hi(act, 0, 0)

            def pair(i):
                for b in range(2):
                    if b == 0:
                        w.split_hi(act, 1, i)
                    elif not (isinstance(i, int) and i == pairs - 1):
                        w.split_hi(act, 0, i + 1)
                    act.wait_ge(w.multiplied[b], i + 1)
                    wait(act, s_tr[b], i)
                    for h in range(2):
                        last = nc.scalar.activation(gelu[b][:, h * HALF:h * HALF + HALF], z[b][h][:, :],
                                                    ACT.Gelu_apprx_tanh)
                    last.then_inc(s_gelu[b], 1)
            repeat(act, pairs, pair)
            act.wait_ge(s_mv, 1)
            act.wait_ge(s_eps, 1)
            nc.scalar.activation(sd[:, :], mv[:, :, 1:2].rearrange("p m a -> p (m a)"), ACT.Sqrt,
                                 bias=eps[:, :]).then_inc(s_sd, 1)
            act.wait_ge(s_shift, 1)
            for m in range(KT):
                nc.scalar.activation(v[:, m, :], v[:, m, :], ACT.Identity, bias=shift[:, m:m + 1],
                                     scale=rstd[:, m:m + 1]).then_inc(s_vhat, 1)

        @block.tensor
        def _(pe):
            def transpose(b, n):
                pe.wait_ge(s_gelu[b], n + 1)
                wait(pe, s_copied[1 - b], n + b)
                for m in range(KT):
                    last = nc.tensor.transpose(tr[m // 4][:, (m % 4) * P:(m % 4 + 1) * P],
                                               gelu[b][:, m * P:m * P + P], ident)
                last.then_inc(s_tr[b], 1)

            def pair(i):
                for b in range(2):
                    pe.wait_ge(w.lo_done[b], i + 1)
                    wait(pe, s_gelu[b], i)
                    for h in range(2):
                        last = w.products(z[b][h][:, :], b, hi, lo, slice(h * HALF, h * HALF + HALF))
                    last.then_inc(w.multiplied[b], 1)
                    if b == 1:
                        transpose(0, i)
                    elif not (isinstance(i, int) and i == 0):
                        transpose(1, i - 1)
            repeat(pe, pairs, pair)
            transpose(1, pairs - 1)

        @block.vector
        def _(dve):
            chain = Chain(dve, s_c)
            nc.vector.memset(eps[:, :], EPS).then_inc(s_eps, 1)
            w.split_lo(dve, 0, 0)

            def pair(i):
                for b in range(2):
                    if b == 0:
                        w.split_lo(dve, 1, i)
                    elif not (isinstance(i, int) and i == pairs - 1):
                        w.split_lo(dve, 0, i + 1)
                    dve.wait_ge(s_tr[b], i + 1)
                    for h in range(2):
                        last = nc.vector.tensor_copy(v[:, 4 * h:4 * h + 4, bass.ds((2 * i + b) * P, P)],
                                                     tr[h][:, :].rearrange("p (m d) -> p m d", d=P))
                    last.then_inc(s_copied[b], 1)
            repeat(dve, pairs, pair)
            dve.wait_ge(s_copied[1], pairs)
            for m in range(KT):
                for c in range(4):
                    last = nc.vector.bn_stats(stats[:, 4 * m + c, :], v[:, m, c * HALF:c * HALF + HALF])
            chain.link(last)
            for m in range(KT):
                last = nc.vector.bn_aggr(mv[:, m, :], stats[:, 4 * m:4 * m + 4, :])
            last.then_inc(s_mv, 1)
            dve.wait_ge(s_sd, 1)
            chain.link(nc.vector.reciprocal(rstd[:, :], sd[:, :]))
            nc.vector.scalar_tensor_tensor(shift[:, :], mv[:, :, 0:1].rearrange("p m a -> p (m a)"), -1.0,
                                           rstd[:, :], ALU.mult, ALU.mult).then_inc(s_shift, 1)


def gmlp_gate(nc, hi, lo, w_ug, vhat, ws_t, b_s, ln_g, ln_b, yo):
    halves = 2
    heads = A_HEADS // halves
    down = KT // 2
    pairs = heads + down
    with Stage(nc, "ag") as st:
        w = Weights(st, w_ug)
        y_hi = st.sb("y_hi", [P, heads, T], F32R)
        y_lo = st.sb("y_lo", [P, heads, T], F32R)
        v_raw = st.sb("v_raw", [P, T])
        v = st.sb("v", [P, T])
        gain = st.sb("gain", [P, P])
        bias = st.sb("bias", [P, P])
        ws = st.sb("ws", [P, P])
        bs = st.sb("bs", [P, P])
        th = st.sb("th", [P, T])
        gu = st.sb("gu", [P, T])
        s = st.sb("s", [P, T])
        z = [[st.ps(f"z{b}{h}", [P, HALF]) for h in range(2)] for b in range(2)]
        sg = [st.ps(f"sg{h}", [P, HALF]) for h in range(2)]
        s_vin, s_pin, s_v, s_gu, s_th, s_a, s_s, s_sg, s_y, s_yhi, s_ylo, s_c, s_cv = (
            st.sem(n) for n in ("vin", "pin", "v_s", "gu_s", "th_s", "a_s", "s_s", "sg_s", "y_s", "yhi_s", "ylo_s", "chain", "chain_v"))
        s_down = st.sems("down", 2)
        block = st.block()
        view = lambda t: t[:, :].rearrange("p (m d) -> p m d", d=P)
        each = lambda t: t[:, :].rearrange("p (a d) -> p a d", a=1).broadcast_to([P, KT, P])
        row = lambda a, j: bass.AP(a.tensor, j * P, [[0, P], [1, P]])

        @block.sync
        def _(sp):
            for hf in range(halves):
                def head(i):
                    j = hf * heads + i
                    n = hf * pairs + i
                    for b in range(2):
                        w.load(sp, b, n, (2 * pairs) * hf + 2 * i + b)
                    wait(sp, s_v, j)
                    sp.dma_start(v_raw[:, :], vhat[bass.ds(j, 1), :, :, :].rearrange("a q m d -> q (a m d)")).then_inc(s_vin, 16)
                    sp.dma_start(gain[:, :], row(ln_g, j)).then_inc(s_vin, 16)
                    sp.dma_start(bias[:, :], row(ln_b, j)).then_inc(s_vin, 16)
                    wait(sp, s_y, j)
                    sp.dma_start(ws[:, :], ws_t[bass.ds(j, 1), :, :].rearrange("a q p -> q (a p)")).then_inc(s_pin, 16)
                    sp.dma_start(bs[:, :], row(b_s, j)).then_inc(s_pin, 16)
                repeat(sp, heads, head)

                def out(i):
                    for b in range(2):
                        w.load(sp, b, hf * pairs + heads + i, (2 * pairs) * hf + 2 * heads + 2 * i + b)
                repeat(sp, down, out)

        @block.scalar
        def _(act):
            w.split_hi(act, 0, 0)
            for hf in range(halves):
                def head(i):
                    j, n = hf * heads + i, hf * pairs + i
                    w.split_hi(act, 1, n)
                    act.wait_ge(w.multiplied[0], n + 1)
                    wait(act, s_y, j)
                    for h in range(2):
                        last = nc.scalar.activation(gu[:, h * HALF:h * HALF + HALF], z[0][h][:, :], ACT.Gelu_apprx_tanh)
                    last.then_inc(s_gu, 1)
                    w.split_hi(act, 0, n + 1)
                    act.wait_ge(w.multiplied[1], n + 1)
                    for h in range(2):
                        last = nc.scalar.activation(th[:, h * HALF:h * HALF + HALF], z[1][h][:, :], ACT.Tanh, scale=0.5)
                    last.then_inc(s_th, 1)
                    act.wait_ge(s_y, j + 1)
                    nc.scalar.activation(y_hi[:, bass.ds(i, 1), :].rearrange("p a t -> p (a t)"), th[:, :], ACT.Copy).then_inc(s_yhi, 1)
                repeat(act, heads, head)

                def out(i):
                    n = hf * pairs + heads + i
                    w.split_hi(act, 1, n)
                    if not (hf == halves - 1 and isinstance(i, int) and i == down - 1):
                        w.split_hi(act, 0, n + 1)
                repeat(act, down, out)

        @block.tensor
        def _(pe):
            for hf in range(halves):
                def head(i):
                    j, n = hf * heads + i, hf * pairs + i
                    for b in range(2):
                        pe.wait_ge(w.lo_done[b], n + 1)
                        wait(pe, (s_gu, s_a)[b], j)
                        wait(pe, s_down[b], hf * down)
                        for h in range(2):
                            last = w.products(z[b][h][:, :], b, hi, lo, slice(h * HALF, h * HALF + HALF))
                        last.then_inc(w.multiplied[b], 1)
                        if b == 0:
                            pe.wait_ge(s_v, j + 1)
                            pe.wait_ge(s_pin, 32 * j + 32)
                            wait(pe, s_s, j)
                            for m in range(KT):
                                last = nc.tensor.matmul(sg[m // 4][:, (m % 4) * P:(m % 4 + 1) * P],
                                                        v[:, m * P:m * P + P], ws[:, :], start=True, stop=True)
                            last.then_inc(s_sg, 1)
                repeat(pe, heads, head)

                def out(i):
                    n = hf * pairs + heads + i
                    for b in range(2):
                        pe.wait_ge(w.lo_done[b], n + 1)
                        pe.wait_ge((s_gu, s_a)[b], (hf + 1) * heads)
                        wait(pe, s_down[b], hf * down + i)
                        pe.wait_ge(s_ylo, (hf + 1) * heads)
                        for h in range(2):
                            last = w.products(z[b][h][:, :], b, y_hi, y_lo, slice(h * HALF, h * HALF + HALF))
                        last.then_inc(w.multiplied[b], 1)
                repeat(pe, down, out)

        @block.vector
        def _(dve):
            c1 = Chain(dve, s_c)
            w.split_lo(dve, 0, 0)
            for hf in range(halves):
                def head(i):
                    j, n = hf * heads + i, hf * pairs + i
                    w.split_lo(dve, 1, n)
                    dve.wait_ge(s_vin, 48 * j + 48)
                    wait(dve, s_sg, j)
                    c1.start(j, 2)
                    c1.link(nc.vector.tensor_tensor(view(v), view(v_raw), each(gain), ALU.mult))
                    nc.vector.tensor_tensor(view(v), view(v), each(bias), ALU.add).then_inc(s_v, 1)
                    w.split_lo(dve, 0, n + 1)
                    dve.wait_ge(s_th, j + 1)
                    for h in range(2):
                        last = nc.vector.scalar_tensor_tensor(th[:, h * HALF:h * HALF + HALF], th[:, h * HALF:h * HALF + HALF],
                                                              1.0, z[1][h][:, :], ALU.add, ALU.mult)
                    last.then_inc(s_a, 1)
                    dve.wait_ge(s_sg, j + 1)
                    dve.wait_ge(s_pin, 32 * j + 32)
                    for h in range(2):
                        last = nc.vector.tensor_tensor(
                            s[:, h * HALF:h * HALF + HALF].rearrange("p (m d) -> p m d", d=P),
                            sg[h][:, :].rearrange("p (m d) -> p m d", d=P),
                            bs[:, :].rearrange("p (a d) -> p a d", a=1).broadcast_to([P, 4, P]), ALU.add)
                    last.then_inc(s_s, 1)
                    dve.wait_ge(s_gu, j + 1)
                    dve.wait_ge(s_a, j + 1)
                    c1.link(nc.vector.scalar_tensor_tensor(th[:, :], th[:, :], 0.5, gu[:, :], ALU.mult, ALU.mult))
                    dve.wait_ge(s_s, j + 1)
                    nc.vector.tensor_tensor(th[:, :], th[:, :], s[:, :], ALU.mult).then_inc(s_y, 1)
                    dve.wait_ge(s_yhi, j + 1)
                    nc.vector.tensor_tensor(y_lo[:, bass.ds(i, 1), :].rearrange("p a t -> p (a t)"), th[:, :],
                                            y_hi[:, bass.ds(i, 1), :].rearrange("p a t -> p (a t)").bitcast(F32),
                                            ALU.subtract).then_inc(s_ylo, 1)
                repeat(dve, heads, head)

                def out(i):
                    n = hf * pairs + heads + i
                    for b in range(2):
                        if b == 0:
                            w.split_lo(dve, 1, n)
                        elif not (hf == halves - 1 and isinstance(i, int) and i == down - 1):
                            w.split_lo(dve, 0, n + 1)
                        dve.wait_ge(w.multiplied[b], n + 1)
                        for h in range(2):
                            dst = yo[:, bass.ds(2 * i + b, 1), h * HALF:h * HALF + HALF].rearrange("p a t -> p (a t)")
                            if hf == 0:
                                last = nc.vector.tensor_copy(dst, z[b][h][:, :])
                            else:
                                last = nc.vector.tensor_tensor(dst, dst, z[b][h][:, :], ALU.add)
                        last.then_inc(s_down[b], 1)
                repeat(dve, down, out)


GROUPS = ((1, 1024), (4, 256), (16, 64))
WINDOW = 64
B_HEADS = 16
B_PAIRS = B_HEADS // 2
VEC = 384
FAR = 1e30
REL_BUCKETS = 32


def bias_vectors(nc, rel_bias, onehot, far, vecs, tiles):
    with Stage(nc, "bv") as st:
        table = st.sb("table", [REL_BUCKETS, 3 * B_HEADS])
        hot = st.sb("hot", [REL_BUCKETS, 3 * VEC])
        out_of = st.sb("out_of", [B_HEADS, 3 * VEC])
        v = st.sb("v", [B_HEADS, 3 * VEC])
        ps = [st.ps(f"ps{g}", [B_HEADS, VEC]) for g in range(3)]
        s_in, s_mm, s_v, s_out = (st.sem(n) for n in ("in", "mm", "v_s", "out"))
        block = st.block()

        @block.sync
        def _(sp):
            sp.dma_start(table[:, :], rel_bias).then_inc(s_in, 16)
            sp.dma_start(hot[:, :], onehot).then_inc(s_in, 16)
            sp.dma_start(out_of[:, :], far).then_inc(s_in, 16)
            sp.wait_ge(s_v, 3)
            for g in range(3):
                sp.dma_start(vecs[g * B_HEADS:(g + 1) * B_HEADS, :], v[:, g * VEC:(g + 1) * VEC]).then_inc(s_out, 16)
            sp.wait_ge(s_out, 48)
            for g in range(3):
                for h in range(0, B_HEADS, 4):
                    sp.dma_start(tiles[g * B_HEADS + h:g * B_HEADS + h + 4, :, :],
                                 bass.AP(vecs.tensor, (g * B_HEADS + h) * VEC + P - 1, [[VEC, 4], [-1, P], [1, 2 * P]])).then_inc(s_out, 16)
            sp.wait_ge(s_out, 48 + 16 * 12)

        @block.tensor
        def _(pe):
            pe.wait_ge(s_in, 48)
            for g in range(3):
                nc.tensor.matmul(ps[g][:, :], table[:, g * B_HEADS:(g + 1) * B_HEADS], hot[:, g * VEC:(g + 1) * VEC],
                                 start=True, stop=True).then_inc(s_mm, 1)

        @block.vector
        def _(dve):
            dve.wait_ge(s_in, 48)
            for g in range(3):
                dve.wait_ge(s_mm, g + 1)
                c = slice(g * VEC, (g + 1) * VEC)
                nc.vector.scalar_tensor_tensor(v[:, c], ps[g][:, :], -1.0, out_of[:, c], ALU.mult, ALU.add).then_inc(s_v, 1)


def dilated_attention(nc, hi, lo, w_qkv, bias_dram, o_dram, lse_dram, ident):
    turns = 3 * B_PAIRS
    tiles = T // P
    SUB = 12
    with Stage(nc, "da") as st:
        w = Weights(st, w_qkv, buffers=3)
        q_new = st.sb("q_new", [P, T])
        k_new = st.sb("k_new", [P, T])
        v_new = st.sb("v_new", [P, T + 2 * WINDOW])
        q = st.sb("q", [P, T])
        k = st.sb("k", [P, T + 2 * WINDOW])
        v = st.sb("v", [P, tiles + 1, P])
        nvar = (3, 2, 1)
        width = (256, 256, 128)
        bias = [[[st.sb(f"bias{g}{h}{x}", [P, width[g]]) for x in range(nvar[g])] for h in range(2)] for g in range(3)]
        logit = [st.sb(f"logit{b}", [P, 2, 256]) for b in range(2)]
        p = [st.sb(f"p{b}", [P, 2, 256]) for b in range(2)]
        pt = [st.sb(f"pt{b}", [P, 512]) for b in range(2)]
        o = st.sb("o", [P, tiles, P])
        rden = [st.sb(f"rden{b}", [P, 2]) for b in range(2)]
        nmax = st.sb("nmax", [P, 3, tiles, B_HEADS])
        pad = st.sb("pad", [P, 1])
        pair_max = st.sb("pair_max", [P, tiles, 2])
        den = st.sb("den", [P, 3, tiles, B_HEADS])
        z = [st.ps(f"z{h}", [P, HALF]) for h in range(2)]
        qk = [st.ps(f"qk{b}", [P, HALF]) for b in range(2)]
        tr = [st.ps(f"tr{b}", [P, HALF]) for b in range(2)]
        pv = [st.ps(f"pv{b}", [P, HALF]) for b in range(2)]
        s_piece, s_new = st.sems("piece", 2), st.sem("new")
        (s_qs, s_vt, s_vts, s_qk, s_max, s_exp, s_t, s_pt, s_pv, s_rden, s_o, s_keep, s_bias, s_odma, s_zero, s_l, s_ldma) = (
            st.sem(x) for x in ("qs", "vt", "vts", "qk_s", "max", "exp", "t", "pt_s", "pv_s", "rden_s", "o_s", "keep", "bias_s", "odma", "zero", "l", "ldma"))
        block = st.block()

        def n_bias(g):
            return 2 * (2 if g == 2 else nvar[g])

        def streams(t2, g):
            d, L = GROUPS[g]
            return t2.rearrange("p (r l) -> p l r", r=d, l=L)

        def schedule(eng, turn):
            turn(0, 0, 0, None, None)
            for g in range(3):
                base = g * B_PAIRS
                if g:
                    turn(base, g, 0, g - 1, B_PAIRS - 1)
                else:
                    turn(1, 0, 1, 0, 0)
                with eng.Fori(1 if g else 2, B_PAIRS - 1) as hp:
                    turn(base + hp, g, hp, g, hp - 1)
                turn(base + B_PAIRS - 1, g, B_PAIRS - 1, g, B_PAIRS - 2)
            turn(turns, None, None, 2, B_PAIRS - 1)

        @block.sync
        def _(sp):
            def load_next(n):
                for b in range(3):
                    w.load(sp, b, n, 3 * n + b)
            sp.wait_ge(s_zero, 1)
            load_next(0)

            def turn(n, g, hp, ag, ahp):
                if ag is None:
                    load_next(1)
                else:
                    a = n - 1
                    wait(sp, s_max, tiles * a)
                    for h in range(2):
                        head = ag * B_HEADS + 2 * ahp + h
                        for x in range(nvar[ag]):
                            tile = bias[ag][h][x]
                            if ag < 2:
                                c0 = WINDOW if x == 0 else 0
                                c1 = 192 if x == 1 else 256
                                sp.dma_start(tile[:, c0:c1], bias_dram[bass.ds(head, 1), :, c0:c1].rearrange("a i j -> i (a j)")).then_inc(s_bias, 16)
                            else:
                                for u in range(2):
                                    sp.dma_start(tile[64 * u:64 * u + 64, 64 * u:64 * u + 64],
                                                 bias_dram[bass.ds(head, 1), 0:64, 64:128].rearrange("a i j -> i (a j)")).then_inc(s_bias, 16)
                    if not (isinstance(n, int) and n >= turns - 1):
                        load_next(n + 1)
                    sp.wait_ge(s_o, tiles * n)
                    d, L = GROUPS[ag]
                    cols = ahp * P + ag * T * D
                    if ag == 0:
                        for u in range(2):
                            sp.dma_start(bass.AP(o_dram.tensor, cols + u * 4 * P * D, [[D, P], [P * D, 4], [1, P]]),
                                         o[:, 4 * u:4 * u + 4, :]).then_inc(s_odma, 16)
                    elif ag == 1:
                        for u in range(2):
                            sp.dma_start(bass.AP(o_dram.tensor, cols + u * P * d * D, [[d * D, P], [D, 4], [1, P]]),
                                         o[:, u::2, :]).then_inc(s_odma, 16)
                    else:
                        for u in range(2):
                            sp.dma_start(bass.AP(o_dram.tensor, cols + u * D, [[d * D, 64], [2 * D, tiles], [1, P]]),
                                         o[64 * u:64 * u + 64, :, :]).then_inc(s_odma, 16)
            schedule(sp, turn)
            sp.wait_ge(s_odma, 32 * turns)
            sp.wait_ge(s_l, 1)
            for g, (d, L) in enumerate(GROUPS):
                for m in range(tiles):
                    base = g * T * B_HEADS
                    if g < 2:
                        start = (m // (L // P)) + (m % (L // P)) * P * d
                        sp.dma_start(bass.AP(lse_dram.tensor, base + start * B_HEADS, [[d * B_HEADS, P], [1, B_HEADS]]),
                                     den[:, g, m, :]).then_inc(s_ldma, 16)
                    else:
                        for u in range(2):
                            sp.dma_start(bass.AP(lse_dram.tensor, base + (2 * m + u) * B_HEADS, [[d * B_HEADS, 64], [1, B_HEADS]]),
                                         den[64 * u:64 * u + 64, g, m, :]).then_inc(s_ldma, 16)
            sp.wait_ge(s_ldma, 16 * (2 * tiles + 2 * tiles))

        def bias_count(ag, ahp):
            return 16 * (sum(n_bias(g) * B_PAIRS for g in range(ag)) + n_bias(ag) * (ahp + 1))

        @block.scalar
        def _(act):
            w.split_hi(act, 0, 0)

            def turn(n, g, hp, ag, ahp):
                a = n - 1
                for s in range(SUB):
                    u, h = s // 4, (s // 2) % 2
                    if g is not None and s % 4 == 0:
                        if u < 2:
                            w.split_hi(act, u + 1, n, free=(s_piece[1], 3 * n + u - 1))
                        elif not (isinstance(n, int) and n == turns - 1):
                            w.split_hi(act, 0, n + 1, free=(s_piece[1], 3 * n + 1))
                    if g is not None and s % 2 == 1:
                        act.wait_ge(s_piece[h], 3 * n + u + 1)
                        cut = GROUPS[g][0]
                        l0, l1 = h * HALF // cut, (h + 1) * HALF // cut
                        src = z[h][:, :].rearrange("p (l r) -> p l r", r=cut)
                        if u == 0:
                            wait(act, s_qs, n)
                            nc.scalar.activation(streams(q_new[:, :], g)[:, l0:l1, :], src, ACT.Copy, scale=-0.125).then_inc(s_new, 1)
                        elif u == 1:
                            nc.scalar.activation(streams(k_new[:, :], g)[:, l0:l1, :], src, ACT.Copy).then_inc(s_new, 1)
                        else:
                            wait(act, s_vt, n)
                            act.wait_ge(s_zero, 1)
                            nc.scalar.activation(streams(v_new[:, WINDOW:WINDOW + T], g)[:, l0:l1, :], src, ACT.Copy).then_inc(s_new, 1)
                    if ag is not None and 3 <= s < 3 + tiles:
                        t = s - 3
                        c = tiles * a + t
                        act.wait_ge(s_t, c + 1)
                        wait(act, s_pv, c - 1)
                        wd = 4 * P if ag < 2 else 2 * P
                        nc.scalar.activation(pt[t % 2][:, 0:wd], tr[t % 2][:, 0:wd], ACT.Copy).then_inc(s_pt, 1)
                    if ag is not None and 1 <= s < 1 + tiles:
                        t = s - 1
                        c = tiles * a + t
                        act.wait_ge(s_max, c + 1)
                        wait(act, s_t, c - 1)
                        wd = width[ag]
                        for hh in range(2):
                            last = nc.scalar.activation(p[t % 2][:, hh, 0:wd], logit[t % 2][:, hh, 0:wd], ACT.Exp, scale=-1.0,
                                                        bias=pair_max[:, t, hh:hh + 1],
                                                        accum_out=den[:, ag, t, bass.ds(2 * ahp + hh, 1)])
                        last.then_inc(s_exp, 1)
            schedule(act, turn)
            act.wait_ge(s_o, tiles * turns)
            act.wait_ge(s_exp, tiles * turns)
            nc.scalar.activation(den[:, :, :, :], den[:, :, :, :], ACT.Ln).then_inc(s_exp, 1)

        @block.tensor
        def _(pe):
            def turn(n, g, hp, ag, ahp):
                a = n - 1
                for s in range(SUB):
                    u, h, half = s // 4, (s // 2) % 2, s % 2
                    if g is not None:
                        if s % 4 == 0:
                            pe.wait_ge(w.lo_done[u], n + 1)
                        if half == 0:
                            wait(pe, s_new, 6 * n + 2 * u - 1 + h)
                        cols = slice(h * HALF, h * HALF + HALF)
                        for kk in range(4 * half, 4 * half + 4):
                            ws = slice(kk * P, kk * P + P)
                            for m, (wp, ap) in enumerate(((w.hi, hi), (w.lo, hi), (w.hi, lo))):
                                last = nc.tensor.matmul(z[h][:, :], wp[u][:, ws], ap[:, kk, cols],
                                                        start=(kk == 0 and m == 0), stop=(kk == KT - 1 and m == 2))
                        if half == 1:
                            last.then_inc(s_piece[h], 1)
                    if ag is None:
                        continue
                    wd = width[ag]
                    if s == 0:
                        pe.wait_ge(s_new, 6 * n)
                        wait(pe, s_pt, tiles * a)
                        wait(pe, s_o, tiles * a)
                        off, cnt = (0, tiles + 1) if ag < 2 else (WINDOW, tiles)
                        for m in range(cnt):
                            dst = (tr[0], tr[1], pv[0])[m // 4]
                            c0 = (m % 4) * P
                            last = nc.tensor.transpose(dst[:, c0:c0 + P], v_new[:, off + m * P:off + m * P + P], ident)
                        last.then_inc(s_vt, 1)
                    if 1 <= s < 1 + tiles:
                        t = s - 1
                        c = tiles * a + t
                        if t == 0:
                            pe.wait_ge(s_qs, n)
                        wait(pe, s_max, c)
                        k0 = t * P + (WINDOW if ag == 2 else 0)
                        for hh in range(2):
                            hs = slice(64 * hh, 64 * hh + 64)
                            last = nc.tensor.matmul(qk[hh][:, 0:wd], q[hs, t * P:t * P + P],
                                                    k[hs, k0:k0 + wd], start=True, stop=True)
                        last.then_inc(s_qk, 1)
                    if 3 <= s < 3 + tiles:
                        t = s - 3
                        c = tiles * a + t
                        pe.wait_ge(s_exp, c + 1)
                        pe.wait_ge(s_vts, n)
                        wait(pe, s_pt, c - 1)
                        for hh in range(2):
                            for x in range(wd // P):
                                i = hh * (wd // P) + x
                                last = nc.tensor.transpose(tr[t % 2][:, i * P:i * P + P], p[t % 2][:, hh, x * P:x * P + P], ident)
                        last.then_inc(s_t, 1)
                    if 4 <= s < 4 + tiles:
                        t = s - 4
                        c = tiles * a + t
                        pe.wait_ge(s_pt, c + 1)
                        pe.wait_ge(s_vts, n)
                        wait(pe, s_o, c - 1)
                        for hh in range(2):
                            for x in range(wd // P):
                                i = hh * (wd // P) + x
                                last = nc.tensor.matmul(pv[t % 2][:, 64 * hh:64 * hh + 64],
                                                        pt[t % 2][:, i * P:i * P + P], v[:, t + x, 64 * hh:64 * hh + 64],
                                                        start=(x == 0), stop=(x == wd // P - 1))
                        last.then_inc(s_pv, 1)
            schedule(pe, turn)

        @block.vector
        def _(dve):
            for g in range(3):
                for h in range(2):
                    for tile in bias[g][h]:
                        nc.vector.memset(tile[:, :], FAR)
            for t2 in (k, v_new):
                nc.vector.memset(t2[:, 0:WINDOW], 0.0)
                last = nc.vector.memset(t2[:, WINDOW + T:], 0.0)
            last.then_inc(s_zero, 1)
            w.split_lo(dve, 0, 0)

            def turn(n, g, hp, ag, ahp):
                a = n - 1
                for s in range(SUB):
                    u = s // 4
                    if g is not None and s % 4 == 0:
                        if u < 2:
                            w.split_lo(dve, u + 1, n)
                        elif not (isinstance(n, int) and n == turns - 1):
                            w.split_lo(dve, 0, n + 1)
                    if ag is None:
                        continue
                    wd = width[ag]
                    if s == 0:
                        dve.wait_ge(s_vt, n)
                        wait(dve, s_pv, tiles * a)
                        nc.vector.tensor_copy(v[:, 0:4, :], tr[0][:, :].rearrange("p (m c) -> p m c", c=P))
                        last = nc.vector.tensor_copy(v[:, 4:8, :], tr[1][:, :].rearrange("p (m c) -> p m c", c=P))
                        if ag < 2:
                            last = nc.vector.tensor_copy(v[:, 8, :], pv[0][:, 0:P])
                        last.then_inc(s_vts, 1)
                    if 1 <= s < 1 + tiles:
                        t = s - 1
                        c = tiles * a + t
                        if t == 0:
                            dve.wait_ge(s_bias, bias_count(ag, ahp))
                        dve.wait_ge(s_qk, c + 1)
                        wait(dve, s_exp, c - 1)
                        nc.vector.memset(pad[:, :], 0.0)
                        L = GROUPS[ag][1]
                        x = 0 if ag == 2 or t % (L // P) == 0 else 1 if (t + 1) % (L // P) == 0 else 2
                        for hh in range(2):
                            last = nc.vector.tensor_tensor_reduce(
                                out=logit[t % 2][:, hh, 0:wd], in0=qk[hh][:, 0:wd], in1=bias[ag][hh][x][:, :],
                                scale=1.0, scalar=3e38, op0=ALU.add, op1=ALU.min,
                                accum_out=pair_max[:, t, hh:hh + 1])
                        last.then_inc(s_max, 1)
                    if 4 <= s < 4 + tiles:
                        t = s - 4
                        c = tiles * a + t
                        dve.wait_ge(s_exp, c + 1)
                        wait(dve, s_o, c - 1)
                        nc.vector.reciprocal(rden[t % 2][:, :], den[:, ag, t, bass.ds(2 * ahp, 2)]).then_inc(s_rden, 1)
                        dve.wait_ge(s_rden, c + 1)
                        dve.wait_ge(s_pv, c + 1)
                        if t == 0:
                            wait(dve, s_odma, 32 * a)
                        nc.vector.tensor_tensor(o[:, t, :].rearrange("p (h c) -> p h c", h=2),
                                                pv[t % 2][:, 0:P].rearrange("p (h c) -> p h c", h=2),
                                                rden[t % 2][:, :].rearrange("p (h a) -> p h a", a=1).broadcast_to([P, 2, 64]),
                                                ALU.mult).then_inc(s_o, 1)
                if ag is not None:
                    dve.wait_ge(s_max, tiles * n)
                    nc.vector.tensor_copy(nmax[:, ag, :, bass.ds(2 * ahp, 2)], pair_max[:, :, :]).then_inc(s_keep, 1)
                if g is not None:
                    dve.wait_ge(s_new, 6 * n + 4)
                    wait(dve, s_qk, tiles * n)
                    nc.vector.tensor_copy(q[:, :], q_new[:, :])
                    nc.vector.tensor_copy(k[:, WINDOW:WINDOW + T], k_new[:, :]).then_inc(s_qs, 1)
            schedule(dve, turn)
            dve.wait_ge(s_exp, tiles * turns + 1)
            dve.wait_ge(s_keep, turns)
            nc.vector.tensor_tensor(den[:, :, :, :], den[:, :, :, :], nmax[:, :, :, :], ALU.subtract).then_inc(s_l, 1)


def attention_output(nc, hi, lo, w_stream, o_dram, lse_dram, ident, yo):
    pairs = KT // 2
    tiles = T // P
    NG = len(GROUPS)
    with Stage(nc, "bo") as st:
        w = Weights(st, w_stream)
        gate = st.sb("gate", [P, KT, T])
        comb = yo
        o = st.sb("o", [P, NG, D])
        th = st.sb("th", [P, T])
        y = [st.sb(f"y{b}", [P, KT // 2, P]) for b in range(2)]
        lse = st.sb("lse", [P, tiles, NG, B_HEADS])
        top = st.sb("top", [P, tiles, B_HEADS])
        total = st.sb("total", [P, tiles, B_HEADS])
        z = [[st.ps(f"z{b}{h}", [P, HALF]) for h in range(2)] for b in range(2)]
        tr = [st.ps(f"tr{h}", [P, HALF]) for h in range(2)]
        s_th, s_gate, s_lse, s_sub, s_e, s_wt, s_o, s_c, s_comb, s_tr, s_y, s_hi, s_lo = (
            st.sem(x) for x in ("th_s", "gate_s", "lse_s", "sub", "e", "wt", "o_s", "chain", "comb_s", "tr_s", "y_s", "hi_s", "lo_s"))
        s_down = st.sems("down", 2)
        block = st.block()
        g1 = lambda t3: t3.rearrange("p (m a) h -> p m a h", a=1).broadcast_to([P, tiles, NG, B_HEADS])

        @block.sync
        def _(sp):
            for g in range(NG):
                sp.dma_start(lse[:, :, g, :], lse_dram[g].rearrange("(m p) h -> p m h", p=P)).then_inc(s_lse, 16)

            def units(i):
                for b in range(2):
                    w.load(sp, b, i, 2 * i + b)
                for b in range(2):
                    m = 2 * i + b
                    wait(sp, s_comb, m)
                    for g in range(NG):
                        sp.dma_start(o[:, g, :], o_dram[g, bass.ds(m * P, P), :]).then_inc(s_o, 16)
            repeat(sp, pairs, units)

            def out(i):
                for b in range(2):
                    w.load(sp, b, pairs + i, 2 * pairs + 2 * i + b)
            repeat(sp, pairs, out)

        @block.scalar
        def _(act):
            w.split_hi(act, 0, 0)
            act.wait_ge(s_sub, 1)
            nc.scalar.activation(lse[:, :, :, :], lse[:, :, :, :], ACT.Exp).then_inc(s_e, 1)

            def units(i):
                for b in range(2):
                    w.split_hi(act, 1 - b, i + b)
                    act.wait_ge(w.multiplied[b], i + 1)
                    wait(act, s_gate, 2 * i + b)
                    for h in range(2):
                        last = nc.scalar.activation(th[:, h * HALF:h * HALF + HALF], z[b][h][:, :], ACT.Tanh, scale=0.5)
                    last.then_inc(s_th, 1)
            repeat(act, pairs, units)
            for m in range(tiles):
                for c in range(2):
                    n = 2 * m + c
                    act.wait_ge(s_y, n + 1)
                    nc.scalar.activation(hi[:, 4 * c:4 * c + 4, m * P:m * P + P], y[c][:, :, :], ACT.Copy).then_inc(s_hi, 1)

            def out(i):
                for b in range(2):
                    if b == 0 or not (isinstance(i, int) and i == pairs - 1):
                        w.split_hi(act, 1 - b, pairs + i + b)
            repeat(act, pairs, out)

        @block.tensor
        def _(pe):
            def units(i):
                for b in range(2):
                    pe.wait_ge(w.lo_done[b], i + 1)
                    wait(pe, s_gate, 2 * i + b - 1)
                    for h in range(2):
                        last = w.products(z[b][h][:, :], b, hi, lo, slice(h * HALF, h * HALF + HALF))
                    last.then_inc(w.multiplied[b], 1)
            repeat(pe, pairs, units)
            for m in range(tiles):
                pe.wait_ge(s_comb, m + 1)
                for c in range(2):
                    n = 2 * m + c
                    wait(pe, s_y, n - 1)
                    for k in range(4):
                        last = nc.tensor.transpose(tr[c][:, k * P:k * P + P], comb[:, m, (4 * c + k) * P:(4 * c + k + 1) * P], ident)
                    last.then_inc(s_tr, 1)
            pe.wait_ge(s_lo, 2 * tiles)

            def out(i):
                for b in range(2):
                    pe.wait_ge(w.lo_done[b], pairs + i + 1)
                    wait(pe, s_down[b], i)
                    for h in range(2):
                        last = w.products(z[b][h][:, :], b, hi, lo, slice(h * HALF, h * HALF + HALF))
                    last.then_inc(w.multiplied[b], 1)
            repeat(pe, pairs, out)

        @block.vector
        def _(dve):
            c1 = Chain(dve, s_c)
            w.split_lo(dve, 0, 0)
            dve.wait_ge(s_lse, 16 * NG)
            c1.link(nc.vector.tensor_tensor(top[:, :, :], lse[:, :, 0, :], lse[:, :, 1, :], ALU.max))
            c1.link(nc.vector.tensor_tensor(top[:, :, :], top[:, :, :], lse[:, :, 2, :], ALU.max))
            for g in range(NG):
                last = nc.vector.tensor_tensor(lse[:, :, g, :], lse[:, :, g, :], top[:, :, :], ALU.subtract)
            last.then_inc(s_sub, 1)
            dve.wait_ge(s_e, 1)
            c1.link(nc.vector.tensor_tensor(total[:, :, :], lse[:, :, 0, :], lse[:, :, 1, :], ALU.add))
            c1.link(nc.vector.tensor_tensor(total[:, :, :], total[:, :, :], lse[:, :, 2, :], ALU.add))
            c1.link(nc.vector.reciprocal(total[:, :, :], total[:, :, :]))
            for g in range(NG):
                last = nc.vector.tensor_tensor(lse[:, :, g, :], lse[:, :, g, :], total[:, :, :], ALU.mult)
            c1.link(last)
            first = c1.n

            def units(i):
                c1.base, c1.n = first + 6 * i, 0
                for b in range(2):
                    m = 2 * i + b
                    w.split_lo(dve, 1 - b, i + b)
                    dve.wait_ge(s_o, 16 * NG * (m + 1))
                    for g in range(NG):
                        v3 = o[:, g, :].rearrange("p (h c) -> p h c", h=B_HEADS)
                        wt = lse[:, bass.ds(m, 1), g, :].rearrange("p a h -> p h a").broadcast_to([P, B_HEADS, 64])
                        last = nc.vector.tensor_tensor(v3, v3, wt, ALU.mult)
                    c1.link(last)
                    c1.link(nc.vector.tensor_tensor(o[:, 0, :], o[:, 0, :], o[:, 1, :], ALU.add))
                    nc.vector.tensor_tensor(comb[:, bass.ds(m, 1), :].rearrange("p a c -> p (a c)"), o[:, 0, :], o[:, 2, :],
                                            ALU.add).then_inc(s_comb, 1)
                    dve.wait_ge(s_th, m + 1)
                    c1.link(nc.vector.tensor_scalar(th[:, :], th[:, :], 0.5, 0.5, ALU.mult, ALU.add))
                    for h in range(2):
                        hs = slice(h * HALF, h * HALF + HALF)
                        last = nc.vector.tensor_tensor(gate[:, bass.ds(m, 1), hs].rearrange("p a t -> p (a t)"), th[:, hs],
                                                       z[b][h][:, :], ALU.mult)
                    last.then_inc(s_gate, 1)
                assert c1.n == 6
            repeat(dve, pairs, units)
            dve.wait_ge(s_gate, 2 * pairs)
            dve.wait_ge(w.multiplied[0], pairs)
            dve.wait_ge(w.multiplied[1], pairs)
            for m in range(tiles):
                for c in range(2):
                    n = 2 * m + c
                    dve.wait_ge(s_tr, n + 1)
                    wait(dve, s_lo, n - 1)
                    wait(dve, s_hi, n - 1)
                    tr3 = tr[c][:, :].rearrange("p (k t) -> p k t", t=P)
                    nc.vector.tensor_tensor(y[c][:, :, :], tr3, gate[:, 4 * c:4 * c + 4, m * P:m * P + P], ALU.mult).then_inc(s_y, 1)
                    dve.wait_ge(s_hi, n + 1)
                    nc.vector.tensor_tensor(lo[:, 4 * c:4 * c + 4, m * P:m * P + P], y[c][:, :, :],
                                            hi[:, 4 * c:4 * c + 4, m * P:m * P + P].bitcast(F32), ALU.subtract).then_inc(s_lo, 1)

            def out(i):
                for b in range(2):
                    if b == 0 or not (isinstance(i, int) and i == pairs - 1):
                        w.split_lo(dve, 1 - b, pairs + i + b)
                    dve.wait_ge(w.multiplied[b], pairs + i + 1)
                    for h in range(2):
                        last = nc.vector.tensor_copy(yo[:, bass.ds(2 * i + b, 1), h * HALF:h * HALF + HALF].rearrange("p a t -> p (a t)"),
                                                     z[b][h][:, :])
                    last.then_inc(s_down[b], 1)
            repeat(dve, pairs, out)


L2 = T + P
PIECE = L2 // 3


U_Z, U_HQ, U_HG, U_SQ, U_SK, U_SV, U_X, U_DT, U_HF, U_HI = 0, 4, 6, 8, 10, 12, 14, 22, 23, 25
N_SILU, N_UNITS = 8, 27


def second_projection(nc, hi, lo, w, proj):
    turns = N_UNITS // 3
    with Stage(nc, "ci") as st:
        out = [st.sb(f"out{b}", [P, L2]) for b in range(3)]
        th = [st.sb(f"th{j}", [P, PIECE]) for j in range(3)]
        z = [st.ps(f"z{j}", [P, HALF]) for j in range(3)]
        s_piece, s_th, s_out, s_left, s_c = st.sems("piece", 3), st.sems("th_s", 3), st.sems("out_s", 3), st.sems("left", 3), st.sem("chain")
        block = st.block()

        def schedule(eng, turn):
            full = N_SILU // 3
            turn(0, 3)
            for i in range(1, full):
                turn(i, 3)
            turn(full, N_SILU % 3)
            with eng.Fori(full + 1, turns - 1) as i:
                turn(i, 0)
            turn(turns - 1, 0)

        @block.sync
        def _(sp):
            def turn(i):
                for b in range(3):
                    w.load(sp, b, i, 3 * i + b)
            repeat(sp, turns, turn)

        @block.scalar
        def _(act):
            w.split_hi(act, 0, 0)

            def turn(i, silus):
                for b in range(3):
                    if b < 2:
                        w.split_hi(act, b + 1, i, free=(s_piece[2], 3 * i + b - 1))
                    elif not (isinstance(i, int) and i == turns - 1):
                        w.split_hi(act, 0, i + 1, free=(s_piece[2], 3 * i + 1))
                    wait(act, s_left[b], 16 * i)
                    for j in range(3):
                        act.wait_ge(s_piece[j], 3 * i + b + 1)
                        if b < silus:
                            wait(act, s_out[j], 3 * i + b)
                            nc.scalar.activation(th[j][:, :], z[j][:, 0:PIECE], ACT.Tanh, scale=0.5).then_inc(s_th[j], 1)
                        else:
                            nc.scalar.activation(out[b][:, j * PIECE:(j + 1) * PIECE], z[j][:, 0:PIECE], ACT.Copy).then_inc(s_out[j], 1)
                    for j in range(3):
                        act.wait_ge(s_out[j], 3 * i + b + 1)
                    act.dma_start(proj[bass.ds(3 * i + b, 1), :, :].rearrange("a p t -> p (a t)"), out[b][:, :]).then_inc(s_left[b], 16)
            schedule(act, turn)
            for b in range(3):
                act.wait_ge(s_left[b], 16 * turns)

        @block.tensor
        def _(pe):
            def turn(i):
                for b in range(3):
                    pe.wait_ge(w.lo_done[b], i + 1)
                    for j in range(3):
                        wait(pe, s_out[j], 3 * i + b)
                        last = w.products(z[j][:, 0:PIECE], b, hi, lo, slice(j * PIECE, (j + 1) * PIECE))
                        last.then_inc(s_piece[j], 1)
            repeat(pe, turns, turn)

        @block.vector
        def _(dve):
            chain = Chain(dve, s_c)
            w.split_lo(dve, 0, 0)

            def turn(i, silus):
                for b in range(3):
                    if b < 2:
                        w.split_lo(dve, b + 1, i)
                    elif not (isinstance(i, int) and i == turns - 1):
                        w.split_lo(dve, 0, i + 1)
                    if b < silus:
                        wait(dve, s_left[b], 16 * i)
                        for j in range(3):
                            dve.wait_ge(s_th[j], 3 * i + b + 1)
                            chain.link(nc.vector.tensor_scalar(th[j][:, :], th[j][:, :], 0.5, 0.5, ALU.mult, ALU.add))
                            nc.vector.tensor_tensor(out[b][:, j * PIECE:(j + 1) * PIECE], th[j][:, :], z[j][:, 0:PIECE],
                                                    ALU.mult).then_inc(s_out[j], 1)
            schedule(dve, turn)


SB_HEADS, HD = 4, 64
EXP_LN = "natural_log_exp_and_others"


TAPS = 4


def stick_breaking(nc, proj, q_gain, k_gain, out_gain, cst, o_cat, conv_w, conv_b, conv):
    steps = []
    for qb in range(2):
        t0 = 1 + 4 * qb
        for kt in range(t0 + 3, -1, -1):
            first = max(kt, t0)
            steps.append((qb, kt, (first - 1) * P, (t0 + 4 - first) * P, kt >= t0))
    NS = len(steps)
    tri, strict, neg, blocks, row, rowneg, ones, ident = (cst[x] for x in ("suffix", "before", "not_before", "block64", "row_ok", "row_neg", "ones", "ident"))
    with Stage(nc, "sb") as st:
        raw = st.sb("raw", [P, L2])
        vraw = st.sb("vraw", [HD, L2])
        sq = st.sb("sq", [P, L2])
        ms = st.sb("ms", [P, L2])
        nrm = st.sb("nrm", [P, L2])
        q = st.sb("q", [HD, T])
        k = st.sb("k", [HD, L2])
        v_new = st.sb("v_new", [P, 9 * HD])
        v = st.sb("v", [P, 9 * HD])
        gain = st.sb("gain", [P, 1])
        eps4 = st.sb("eps4", [P, 1])
        og = st.sb("og", [P, SB_HEADS * HD])
        a = [st.sb(f"a{b}", [P, HALF]) for b in range(2)]
        zs = [st.sb(f"zs{b}", [P, HALF]) for b in range(2)]
        l = [st.sb(f"l{b}", [P, HALF]) for b in range(2)]
        sp_ = [st.sb(f"sp{b}", [P, HALF]) for b in range(2)]
        acc = st.sb("acc", [P, HALF])
        lw = [st.sb(f"lw{b}", [P, HALF]) for b in range(2)]
        wt = [st.sb(f"wt{b}", [P, HALF]) for b in range(2)]
        o = [st.sb(f"o{b}", [P, 4, HD]) for b in range(2)]
        osq = st.sb("osq", [P, 4, HD])
        oss = st.sb("oss", [P, 4])
        oln = st.sb("oln", [P, 4])
        orr = st.sb("orr", [P, 4])
        cx = [st.sb(f"cx{b}", [P, TAPS - 1 + L2]) for b in range(2)]
        cy = [st.sb(f"cy{b}", [P, L2]) for b in range(2)]
        ce = [st.sb(f"ce{b}", [P, L2]) for b in range(2)]
        ct = st.sb("ct", [P, L2])
        taps = st.sb("taps", [P, 2 * SB_HEADS, TAPS])
        cbias = st.sb("cbias", [P, 2 * SB_HEADS])
        s_cpar, s_cc = st.sem("conv_par"), st.sem("conv_chain")
        s_cin, s_cy, s_cm, s_ce, s_cs, s_cout = (st.sems(v, 2) for v in ("conv_in", "conv_y", "conv_low", "conv_exp", "conv_silu", "conv_out"))
        zb = [st.ps(f"z{b}", [P, HALF]) for b in range(2)]
        sb_ = [st.ps(f"sum{b}", [P, HALF]) for b in range(2)]
        ob = [st.ps(f"ob{b}", [P, HALF]) for b in range(2)]
        pb = [st.ps(f"pb{b}", [P, HALF]) for b in range(2)]
        (s_par, s_gain, s_raw, s_sq, s_blk, s_ms, s_rt, s_nrm, s_vt, s_vnew, s_cur, s_vcur, s_z, s_a, s_e, s_l, s_sp, s_sum, s_lw, s_acc, s_w,
         s_pv, s_oc, s_oss, s_oln, s_orr, s_of, s_odma, s_c, s_cp, s_zs) = (
            st.sem(x) for x in ("par", "gain_s", "raw_s", "sq_s", "blk", "ms_s", "rt", "nrm_s", "vt", "vnew", "cur", "vcur", "z_s", "a_s", "e_s", "l_s",
                                "sp_s", "sum_s", "lw_s", "acc_s", "w_s", "pv", "oc", "oss_s", "oln_s", "orr_s", "of", "odma", "chain", "chain_prep", "zs_s"))
        block = st.block()

        def schedule(eng, turn):
            turn(0)
            turn(1)
            with eng.Fori(2, SB_HEADS) as i:
                turn(i)
            turn(SB_HEADS)

        prep_of = lambda n: not (isinstance(n, int) and n == SB_HEADS)
        main_of = lambda n: not (isinstance(n, int) and n == 0)
        flat = proj.rearrange("u f t -> (u f) t")

        @block.sync
        def _(sp):
            sp.dma_start(gain[0:HD, :], q_gain).then_inc(s_par, 16)
            sp.dma_start(gain[HD:P, :], k_gain).then_inc(s_par, 16)
            sp.dma_start(og[:, :], bass.AP(out_gain.tensor, 0, [[0, P], [1, SB_HEADS * HD]])).then_inc(s_par, 16)

            def turn(n):
                if prep_of(n):
                    wait(sp, s_nrm, n)
                    sp.dma_start(raw[0:HD, :], flat[bass.ds(U_SQ * P + n * HD, HD), :]).then_inc(s_raw, 16)
                    sp.dma_start(raw[HD:P, :], flat[bass.ds(U_SK * P + n * HD, HD), :]).then_inc(s_raw, 16)
                    wait(sp, s_vt, n)
                    sp.dma_start(vraw[:, :], flat[bass.ds(U_SV * P + n * HD, HD), :]).then_inc(s_raw, 16)
                if main_of(n):
                    for qb in range(2):
                        sp.wait_ge(s_of, 2 * (n - 1) + qb + 1)
                        for x in range(4):
                            sp.dma_start(o_cat[(4 * qb + x) * P:(4 * qb + x + 1) * P, bass.ds((n - 1) * HD, HD)], o[qb][:, x, :]).then_inc(s_odma, 16)
                if prep_of(n):
                    sp.wait_ge(s_nrm, n + 1)
                    sp.dma_start(q[:, :], nrm[0:HD, P:L2]).then_inc(s_cur, 16)
                    sp.dma_start(k[:, :], nrm[HD:P, :]).then_inc(s_cur, 16)
            schedule(sp, turn)
            sp.wait_ge(s_odma, 16 * 8 * SB_HEADS)

        @block.scalar
        def _(act):
            act.wait_ge(s_par, 49)
            nc.scalar.preload_act_table_set(EXP_LN)

            def turn(n):
                for s in range(NS + 3):
                    if prep_of(n):
                        if s == 1:
                            act.wait_ge(s_raw, 48 * n + 48)
                            wait(act, s_blk, 3 * n)
                            nc.scalar.activation(sq[:, :], raw[:, :], ACT.Square).then_inc(s_sq, 1)
                        if s == 6:
                            act.wait_ge(s_ms, 3 * n + 3)
                            nc.scalar.activation(ms[:, :], ms[:, :], ACT.Sqrt).then_inc(s_rt, 1)
                            nc.scalar.preload_act_table_set(EXP_LN)
                    if not main_of(n):
                        continue
                    if s in (5, 6, 7, 11, 12, 13):
                        u, j = int(s > 7), (s - 5) % 6
                        if j == 0:
                            act.wait_ge(s_cm[u], n)
                        else:
                            act.wait_ge(s_ce[u], 3 * (n - 1) + j)
                        func, scale, add = ((ACT.Exp, -1.0, 0.0), (ACT.Ln, 1.0, 1.0), (ACT.Exp, -1.0, 0.0))[j]
                        nc.scalar.activation(ce[u][:, :], ce[u][:, :], func, scale=scale, bias=add).then_inc(s_ce[u], 1)
                    c = NS * (n - 1) + s
                    if s < NS:
                        qb, kt, q0, N, diag = steps[s]
                        act.wait_ge(s_z, c + 1)
                        nc.scalar.activation(a[s % 2][:, 0:N], zb[s % 2][:, 0:N], ACT.Abs).then_inc(s_a, 1)
                        act.wait_ge(s_a, c + 1)
                        nc.scalar.activation(a[s % 2][:, 0:N], a[s % 2][:, 0:N], ACT.Exp, scale=-1.0).then_inc(s_e, 1)
                        act.wait_ge(s_e, c + 1)
                        wait(act, s_sp, c - 1)
                        nc.scalar.activation(l[s % 2][:, 0:N], a[s % 2][:, 0:N], ACT.Ln, bias=1.0).then_inc(s_l, 1)
                    if 1 <= s <= NS:
                        qb, kt, q0, N, diag = steps[s - 1]
                        b = (s - 1) % 2
                        act.wait_ge(s_lw, c)
                        wait(act, s_pv, c - 2)
                        nc.scalar.activation(wt[b][:, 0:N], lw[b][:, 0:N], ACT.Exp, bias=rowneg if kt == 0 else 0.0).then_inc(s_w, 1)
                    if s - 3 in (4, NS - 1):
                        qb = int(s - 3 != 4)
                        m = 2 * (n - 1) + qb
                        act.wait_ge(s_oss, m + 1)
                        nc.scalar.activation(oln[:, :], oss[:, :], ACT.Ln, scale=1.0 / HD, bias=eps4[:, :]).then_inc(s_oln, 1)
                        act.wait_ge(s_oln, m + 1)
                        nc.scalar.activation(orr[:, :], oln[:, :], ACT.Exp, scale=-0.5).then_inc(s_orr, 1)
            schedule(act, turn)

        @block.gpsimd
        def _(pool):
            units = 2 * SB_HEADS
            chain = Chain(pool, s_cc)
            pool.dma_start(taps[:, :, :], conv_w).then_inc(s_cpar, 16)
            pool.dma_start(cbias[:, :], conv_b).then_inc(s_cpar, 16)
            for u in range(2):
                pool.dma_start(cx[u][:, TAPS - 1:], proj[U_X + u]).then_inc(s_cin[u], 16)
                chain.link(nc.gpsimd.memset(cx[u][:, 0:TAPS - 1], 0.0))
            pool.wait_ge(s_cpar, 32)

            def convolve(unit):
                i, u = unit // 2, unit % 2
                pool.wait_ge(s_cin[u], 16 * i + 16)
                wait(pool, s_cout[u], 16 * i)
                chain.link(nc.gpsimd.tensor_scalar(cy[u][:, :], cx[u][:, 0:L2], taps[:, unit, 0:1], cbias[:, unit:unit + 1], ALU.mult, ALU.add))
                for j in range(1, TAPS):
                    chain.link(nc.gpsimd.tensor_scalar(ct[:, :], cx[u][:, j:j + L2], taps[:, unit, j:j + 1], None, ALU.mult))
                    last = nc.gpsimd.tensor_tensor(cy[u][:, :], cy[u][:, :], ct[:, :], ALU.add)
                    if j < TAPS - 1:
                        chain.link(last)
                last.then_inc(s_cy[u], 1)
                pool.wait_ge(s_cy[u], i + 1)
                if unit + 2 < units:
                    pool.dma_start(cx[u][:, TAPS - 1:], proj[U_X + unit + 2]).then_inc(s_cin[u], 16)
                nc.gpsimd.tensor_scalar(ce[u][:, :], cy[u][:, :], -44.0, None, ALU.max).then_inc(s_cm[u], 1)

            def silu(unit):
                i, u = unit // 2, unit % 2
                pool.wait_ge(s_ce[u], 3 * i + 3)
                nc.gpsimd.tensor_tensor(cy[u][:, :], cy[u][:, :], ce[u][:, :], ALU.mult).then_inc(s_cs[u], 1)
                pool.wait_ge(s_cs[u], i + 1)
                pool.dma_start(conv[unit], cy[u][:, :]).then_inc(s_cout[u], 16)
            convolve(0)
            for unit in range(units):
                if unit + 1 < units:
                    convolve(unit + 1)
                silu(unit)
            for u in range(2):
                pool.wait_ge(s_cout[u], 16 * units // 2)

        @block.tensor
        def _(pe):
            def z_of(n, s):
                qb, kt, q0, N, diag = steps[s]
                c = NS * (n - 1) + s
                if s == 0:
                    pe.wait_ge(s_cur, 32 * n)
                wait(pe, s_zs, c - 1)
                nc.tensor.matmul(zb[s % 2][:, 0:N], k[:, kt * P:kt * P + P], q[:, q0:q0 + N], start=True, stop=True).then_inc(s_z, 1)

            def turn(n):
                if main_of(n):
                    z_of(n, 0)
                for s in range(NS + 1):
                    if prep_of(n):
                        if s == 2:
                            pe.wait_ge(s_sq, n + 1)
                            wait(pe, s_vnew, n)
                            for j in range(2):
                                nc.tensor.matmul(pb[j][:, 0:PIECE], blocks, sq[:, j * PIECE:(j + 1) * PIECE], start=True, stop=True).then_inc(s_blk, 1)
                        if s == 4:
                            pe.wait_ge(s_ms, 3 * n + 1)
                            nc.tensor.matmul(pb[0][:, 0:PIECE], blocks, sq[:, 2 * PIECE:3 * PIECE], start=True, stop=True).then_inc(s_blk, 1)
                        if s == 8:
                            pe.wait_ge(s_raw, 48 * n + 48)
                            pe.wait_ge(s_ms, 3 * n + 3)
                            for m in range(9):
                                last = nc.tensor.matmul(pb[m // 8][:, (m % 8) * HD:(m % 8 + 1) * HD], vraw[:, m * P:m * P + P], ident[0:HD, 0:HD],
                                                        start=True, stop=True)
                            last.then_inc(s_vt, 1)
                    if not main_of(n):
                        continue
                    c = NS * (n - 1) + s
                    if s + 1 < NS:
                        z_of(n, s + 1)
                    if s < NS:
                        qb, kt, q0, N, diag = steps[s]
                        old = P if diag else 0
                        pe.wait_ge(s_sp, c + 1)
                        wait(pe, s_acc, c)
                        wait(pe, s_lw, c - 1)
                        more = N > old
                        if old:
                            last = nc.tensor.matmul(sb_[s % 2][:, 0:old], tri, sp_[s % 2][:, 0:old], start=True, stop=True)
                        if more:
                            nc.tensor.matmul(sb_[s % 2][:, old:N], tri, sp_[s % 2][:, old:N], start=True, stop=False)
                            last = nc.tensor.matmul(sb_[s % 2][:, old:N], ones, acc[:, HALF - N + old:HALF], start=False, stop=True)
                        last.then_inc(s_sum, 1)
                    if s >= 1:
                        qb, kt, q0, N, diag = steps[s - 1]
                        if s == 1:
                            pe.wait_ge(s_vcur, n)
                        pe.wait_ge(s_w, c)
                        first = kt == 4 + 4 * qb
                        if first:
                            wait(pe, s_oc, 2 * (n - 1) + qb - 1)
                        for x in range(N // P):
                            y0 = 4 - N // P + x
                            last = nc.tensor.matmul(ob[qb][:, y0 * HD:y0 * HD + HD], wt[(s - 1) % 2][:, x * P:x * P + P],
                                                    v[:, kt * HD:kt * HD + HD], start=first, stop=kt == 0, skip_group_check=True)
                        last.then_inc(s_pv, 1)
            schedule(pe, turn)

        @block.vector
        def _(dve):
            nc.vector.memset(eps4[:, :], EPS)
            dve.wait_ge(s_par, 48)
            nc.vector.tensor_scalar(gain[0:HD, :], gain[0:HD, :], HD ** -0.5, None, ALU.mult).then_inc(s_par, 1)
            dve.wait_ge(s_par, 49)
            prep_chain, chain = Chain(dve, s_cp), Chain(dve, s_c)
            ends = {4: 0, NS - 1: 1}

            def turn(n):
                if prep_of(n):
                    prep_chain.start(n, 1)
                if main_of(n):
                    chain.start(n - 1, 22)
                for s in range(NS + 3):
                    if prep_of(n):
                        if s in (3, 5):
                            for j in ((0, 1) if s == 3 else (2,)):
                                dve.wait_ge(s_blk, 3 * n + j + 1)
                                nc.vector.tensor_scalar(ms[:, j * PIECE:(j + 1) * PIECE], pb[j % 2][:, 0:PIECE], 1.0 / HD, EPS,
                                                        ALU.mult, ALU.add).then_inc(s_ms, 1)
                        if s == 7:
                            dve.wait_ge(s_rt, n + 1)
                            prep_chain.link(nc.vector.reciprocal(sq[:, :], ms[:, :]))
                            wait(dve, s_cur, 32 * n)
                            nc.vector.scalar_tensor_tensor(nrm[:, :], raw[:, :], gain[:, 0:1], sq[:, :], ALU.mult, ALU.mult).then_inc(s_nrm, 1)
                        if s == 9:
                            dve.wait_ge(s_vt, n + 1)
                            nc.vector.tensor_copy(v_new[:, 0:8 * HD], pb[0][:, 0:8 * HD])
                            nc.vector.tensor_copy(v_new[:, 8 * HD:9 * HD], pb[1][:, 0:HD]).then_inc(s_vnew, 1)
                    if not main_of(n):
                        continue
                    c = NS * (n - 1) + s
                    if s < NS:
                        qb, kt, q0, N, diag = steps[s]
                        dve.wait_ge(s_z, c + 1)
                        dve.wait_ge(s_a, c + 1)
                        nc.vector.tensor_copy(zs[s % 2][:, 0:N], zb[s % 2][:, 0:N]).then_inc(s_zs, 1)
                    if 1 <= s <= NS:
                        qb, kt, q0, N, diag = steps[s - 1]
                        b = (s - 1) % 2
                        dve.wait_ge(s_sum, c)
                        wait(dve, s_w, c - 2)
                        last = nc.vector.tensor_tensor(lw[b][:, 0:N], zs[b][:, 0:N], sb_[b][:, 0:N], ALU.subtract)
                        if diag:
                            chain.link(last)
                            last = nc.vector.tensor_tensor(lw[b][:, 0:P], lw[b][:, 0:P], neg, ALU.add)
                        last.then_inc(s_lw, 1)
                        new = P if diag else 0
                        c0 = HALF - N
                        dve.wait_ge(s_sp, c)
                        wait(dve, s_acc, c - 1)
                        if new:
                            last = nc.vector.tensor_copy(acc[:, c0:c0 + new], sp_[b][:, 0:new])
                        if N > new:
                            last = nc.vector.tensor_tensor(acc[:, c0 + new:HALF], acc[:, c0 + new:HALF], sp_[b][:, new:N], ALU.add)
                        last.then_inc(s_acc, 1)
                    if s < NS:
                        qb, kt, q0, N, diag = steps[s]
                        b = s % 2
                        dve.wait_ge(s_l, c + 1)
                        wait(dve, s_sum, c - 1)
                        dve.wait_ge(s_zs, c + 1)
                        last = nc.vector.scalar_tensor_tensor(sp_[b][:, 0:N], zs[b][:, 0:N], 0.0, l[b][:, 0:N], ALU.max, ALU.add)
                        if diag:
                            chain.link(last)
                            last = nc.vector.tensor_tensor(sp_[b][:, 0:P], sp_[b][:, 0:P], strict, ALU.mult)
                        if kt == 0:
                            chain.link(last)
                            last = nc.vector.tensor_scalar(sp_[b][:, 0:N], sp_[b][:, 0:N], row, None, ALU.mult)
                        last.then_inc(s_sp, 1)
                    if s - 3 in ends:
                        qb = ends[s - 3]
                        m = 2 * (n - 1) + qb
                        dve.wait_ge(s_pv, NS * (n - 1) + s - 2)
                        wait(dve, s_odma, 64 * (m - 1))
                        nc.vector.tensor_copy(o[qb][:, :, :], ob[qb][:, 0:4 * HD].rearrange("p (x c) -> p x c", x=4)).then_inc(s_oc, 1)
                        dve.wait_ge(s_oc, m + 1)
                        chain.link(nc.vector.tensor_tensor(osq[:, :, :], o[qb][:, :, :], o[qb][:, :, :], ALU.mult))
                        nc.vector.tensor_reduce(oss[:, :], osq[:, :, :], AX.X, ALU.add).then_inc(s_oss, 1)
                        dve.wait_ge(s_orr, m + 1)
                        chain.link(nc.vector.tensor_tensor(o[qb][:, :, :], o[qb][:, :, :],
                                                           orr[:, :].rearrange("p (x a) -> p x a", a=1).broadcast_to([P, 4, HD]), ALU.mult))
                        nc.vector.tensor_tensor(o[qb][:, :, :], o[qb][:, :, :],
                                                og[:, bass.ds((n - 1) * HD, HD)].rearrange("p (a c) -> p a c", a=1).broadcast_to([P, 4, HD]),
                                                ALU.mult).then_inc(s_of, 1)
                if prep_of(n):
                    dve.wait_ge(s_vnew, n + 1)
                    wait(dve, s_pv, NS * n)
                    nc.vector.tensor_copy(v[:, :], v_new[:, :]).then_inc(s_vcur, 1)
            schedule(dve, turn)


SSD_HEADS, GH = 8, 4
NCH = L2 // P

def ssd(nc, proj, conv, dt_bias, a_log, d_skip, gain, cst, o_cat):
    G = 2
    W = GH * HD
    with Stage(nc, "sd") as st:
        dtf = st.sb("dtf", [SSD_HEADS, L2])
        tmp = st.sb("tmp", [SSD_HEADS, L2])
        af = st.sb("af", [SSD_HEADS, L2])
        par = st.sb("par", [SSD_HEADS, 4])
        dt = st.sb("dt", [P, NCH, SSD_HEADS])
        a = st.sb("a", [P, NCH, SSD_HEADS])
        cum = st.sb("cum", [P, NCH, SSD_HEADS])
        ecum = st.sb("ecum", [P, NCH, SSD_HEADS])
        wend = st.sb("wend", [P, NCH, SSD_HEADS])
        elast = st.sb("elast", [P, NCH, SSD_HEADS])
        dsk = st.sb("dsk", [P, SSD_HEADS])
        gn = st.sb("gn", [P, G * W])
        xbc = [st.sb(f"xbc{b}", [P, 8, P]) for b in range(2)]
        zf = [st.sb(f"zf{b}", [P, 4, P]) for b in range(2)]
        x = st.sb("x", [P, SSD_HEADS, HD])
        xdt = st.sb("xdt", [P, SSD_HEADS, HD])
        xw = st.sb("xw", [P, SSD_HEADS, HD])
        ab = st.sb("ab", [P, SSD_HEADS, P])
        bt = st.sb("bt", [P, G, P])
        cbm = st.sb("cbm", [P, G, P])
        seg = [st.sb(f"seg{g}", [P, GH, P]) for g in range(G)]
        state = st.sb("state", [P, G, W])
        y = st.sb("y", [P, SSD_HEADS, HD])
        yd = st.sb("yd", [P, SSD_HEADS, HD])
        ysq = st.sb("ysq", [P, G, W])
        ss = st.sb("ss", [P, G])
        lnm = st.sb("lnm", [P, G])
        rms = st.sb("rms", [P, G])
        eps = st.sb("eps", [P, 1])
        pX = st.ps("pX", [P, HALF])
        pB = st.ps("pB", [P, HALF])
        pA = [st.ps(f"pA{g}", [P, HALF]) for g in range(G)]
        pD = st.ps("pD", [P, HALF])
        pO = st.ps("pO", [P, HALF])
        pS = st.ps("pS", [P, HALF])
        ident, upto, ones = cst["ident"], cst["upto"], cst["ones"]
        (s_in, s_par, s_v, s_e, s_c, s_tr, s_dt, s_cum, s_rl, s_sq, s_ln, s_yx, s_n) = (
            st.sem(v) for v in ("in", "par_s", "v", "e", "chain", "tr", "dt_s", "cum_s", "relu", "sq_s", "ln_s", "yx", "n_s"))
        s_xbc, s_zf = st.sems("xbc_s", 2), st.sems("zf_s", 2)
        (s_xt, s_bt, s_cb, s_ab, s_zt, s_x, s_btc, s_cbm, s_seg, s_es, s_m, s_yd, s_yo, s_st, s_state, s_y, s_z, s_rms, s_out,
         s_left, s_xw, s_yr, s_abc) = (
            st.sem(v) for v in ("xt", "bt_s", "cb", "ab", "zt", "x_s", "btc", "cbm_s", "seg_s", "es", "m", "yd_s", "yo", "st_s", "state_s", "y_s",
                                "z_s", "rms_s", "out", "left", "xw_s", "yr", "abc"))
        block = st.block()
        bc = lambda t2, n: t2.rearrange("p (h a) -> p h a", a=1).broadcast_to([P, t2.shape[1], n])
        row = lambda t, c: t[:, bass.ds(c, 1), :].rearrange("p a h -> p (a h)")

        def schedule(eng, chunk):
            chunk(0, 0)
            chunk(1, 1)
            with eng.Fori(1, NCH // 2) as i:
                chunk(2 * i, 0)
                chunk(2 * i + 1, 1)
            chunk(NCH - 1, 0)

        @block.sync
        def _(sp):
            sp.dma_start(dtf[:, :], proj[U_DT, 0:SSD_HEADS, :]).then_inc(s_in, 16)
            sp.dma_start(par[:, 0:1], dt_bias).then_inc(s_in, 16)
            sp.dma_start(par[:, 1:2], a_log).then_inc(s_in, 16)
            sp.dma_start(dsk[:, :], bass.AP(d_skip.tensor, 0, [[0, P], [1, SSD_HEADS]])).then_inc(s_par, 16)
            sp.dma_start(gn[:, :], bass.AP(gain.tensor, 0, [[0, P], [1, G * W]])).then_inc(s_par, 16)

            def chunk(c, b):
                wait(sp, s_yo, c - 1)
                sp.dma_start(xbc[b][:, :, :], conv[:, :, bass.ds(c * P, P)].rearrange("u p t -> p u t")).then_inc(s_xbc[b], 16)
                wait(sp, s_zt, c - 1)
                sp.dma_start(zf[b][:, :, :], proj[U_Z:U_Z + 4, :, bass.ds(c * P, P)].rearrange("u p t -> p u t")).then_inc(s_zf[b], 16)
                if not (isinstance(c, int) and c < 2):
                    sp.wait_ge(s_out, c)
                    sp.dma_start(o_cat[bass.ds((c - 2) * P, P), W:3 * W], y[:, :, :].rearrange("p h d -> p (h d)")).then_inc(s_left, 16)
            schedule(sp, chunk)
            sp.wait_ge(s_out, NCH)
            sp.dma_start(o_cat[(NCH - 2) * P:(NCH - 1) * P, W:3 * W], y[:, :, :].rearrange("p h d -> p (h d)")).then_inc(s_left, 16)
            sp.wait_ge(s_left, 16 * (NCH - 1))

        @block.scalar
        def _(act):
            act.wait_ge(s_in, 48)
            nc.scalar.preload_act_table_set(EXP_LN)
            nc.scalar.activation(par[:, 2:3], par[:, 1:2], ACT.Exp).then_inc(s_e, 1)
            act.wait_ge(s_v, 1)
            nc.scalar.activation(tmp[:, :], tmp[:, :], ACT.Exp, scale=-1.0).then_inc(s_e, 1)
            act.wait_ge(s_e, 2)
            nc.scalar.activation(tmp[:, :], tmp[:, :], ACT.Ln, bias=1.0).then_inc(s_e, 1)
            act.wait_ge(s_cum, 1)
            nc.scalar.activation(ecum[:, :, :], cum[:, :, :], ACT.Exp).then_inc(s_e, 1)
            nc.scalar.activation(wend[:, :, :], wend[:, :, :], ACT.Exp).then_inc(s_e, 1)
            nc.scalar.activation(elast[:, :, :], elast[:, :, :], ACT.Exp).then_inc(s_e, 1)

            def norm(c):
                wait(act, s_z, c + 1)
                for g in range(G):
                    last = nc.scalar.activation(ysq[:, g, :], y[:, g * GH:(g + 1) * GH, :].rearrange("p h d -> p (h d)"), ACT.Square,
                                                accum_out=ss[:, g:g + 1])
                last.then_inc(s_sq, 1)
                act.wait_ge(s_sq, c + 1)
                nc.scalar.activation(lnm[:, :], ss[:, :], ACT.Ln, scale=1.0 / W, bias=eps[:, :]).then_inc(s_ln, 1)
                act.wait_ge(s_ln, c + 1)
                wait(act, s_out, c)
                nc.scalar.activation(rms[:, :], lnm[:, :], ACT.Exp, scale=-0.5).then_inc(s_rms, 1)

            def chunk(c, b):
                act.wait_ge(s_xt, c + 1)
                wait(act, s_y, c)
                wait(act, s_yx, c)
                nc.scalar.activation(x[:, :, :], pX[:, :].rearrange("p (h d) -> p h d", h=SSD_HEADS), ACT.Copy).then_inc(s_x, 1)
                if not (isinstance(c, int) and c == 0):
                    norm(c - 1)
                for g in range(G):
                    act.wait_ge(s_seg, G * c + g + 1)
                    nc.scalar.activation(seg[g][:, :, :], seg[g][:, :, :], ACT.Relu, scale=-1.0).then_inc(s_rl, 1)
                for g in range(G):
                    act.wait_ge(s_rl, G * c + g + 1)
                    nc.scalar.activation(seg[g][:, :, :], seg[g][:, :, :], ACT.Exp, scale=-1.0).then_inc(s_es, 1)
            schedule(act, chunk)
            norm(NCH - 1)

        @block.gpsimd
        def _(pool):
            pool.wait_ge(s_par, 32)

            def chunk(c, b):
                pool.wait_ge(s_x, c + 1)
                wait(pool, s_state, c + 1)
                nc.gpsimd.tensor_tensor(yd[:, :, :], x[:, :, :], bc(dsk[:, :], HD), ALU.mult).then_inc(s_yx, 1)
            schedule(pool, chunk)

        @block.tensor
        def _(pe):
            for n, src in enumerate((dtf, af)):
                pe.wait_ge(s_v, 2 + n)
                for c in range(NCH):
                    last = nc.tensor.transpose(pA[n][:, c * SSD_HEADS:(c + 1) * SSD_HEADS], src[:, c * P:c * P + P], ident[0:SSD_HEADS, 0:SSD_HEADS])
                last.then_inc(s_tr, 1)
            pe.wait_ge(s_dt, 1)
            flat = a[:, :, :].rearrange("p c h -> p (c h)")
            nc.tensor.matmul(pD[:, 0:NCH * SSD_HEADS], upto, flat, start=True, stop=True)
            nc.tensor.matmul(pO[:, 0:NCH * SSD_HEADS], ones, flat, start=True, stop=True).then_inc(s_tr, 1)

            def chunk(c, b):
                pe.wait_ge(s_xbc[b], 8 * (c - b) + 16)
                wait(pe, s_cbm, G * c)
                for g in range(G):
                    last = nc.tensor.transpose(pB[:, g * P:g * P + P], xbc[b][:, 4 + g, :], ident)
                for g in range(G):
                    last = nc.tensor.matmul(pB[:, (2 + g) * P:(3 + g) * P], xbc[b][:, 4 + g, :], xbc[b][:, 6 + g, :], start=True, stop=True)
                last.then_inc(s_cb, 1)
                pe.wait_ge(s_abc, c + 1)
                for g in range(G):
                    wait(pe, s_seg, G * c - 1 + g)
                    for h in range(GH):
                        last = nc.tensor.matmul(pA[g][:, h * P:h * P + P], ab[:, g * GH + h, :], upto, start=True, stop=True)
                    last.then_inc(s_ab, 1)
                wait(pe, s_z, c)
                for u in range(4):
                    last = nc.tensor.transpose(pX[:, u * P:u * P + P], xbc[b][:, u, :], ident)
                last.then_inc(s_xt, 1)
                pe.wait_ge(s_x, c + 1)
                pe.wait_ge(s_zf[b], 8 * (c - b) + 16)
                for u in range(4):
                    last = nc.tensor.transpose(pX[:, u * P:u * P + P], zf[b][:, u, :], ident)
                last.then_inc(s_zt, 1)
                wait(pe, s_y, c)
                pe.wait_ge(s_state, c + 1)
                for g in range(G):
                    last = nc.tensor.matmul(pO[:, g * W:(g + 1) * W], xbc[b][:, 6 + g, :], state[:, g, :], start=True, stop=True)
                last.then_inc(s_yo, 1)
                pe.wait_ge(s_xw, c + 1)
                pe.wait_ge(s_btc, c + 1)
                for g in range(G):
                    last = nc.tensor.matmul(pS[:, g * W:(g + 1) * W], bt[:, g, :], xw[:, g * GH:(g + 1) * GH, :], start=True, stop=True)
                last.then_inc(s_st, 1)
                for g in range(G):
                    pe.wait_ge(s_m, G * c + g + 1)
                    for h in range(GH):
                        last = nc.tensor.matmul(pD[:, g * W + h * HD:g * W + (h + 1) * HD], seg[g][:, h, :], xdt[:, g * GH + h, :], start=True, stop=True)
                last.then_inc(s_yd, 1)
            schedule(pe, chunk)

        @block.vector
        def _(dve):
            chain = Chain(dve, s_c)
            pre = Chain(dve, s_yr)
            nc.vector.memset(eps[:, :], EPS)
            nc.vector.memset(state[:, :, :], 0.0).then_inc(s_state, 1)
            dve.wait_ge(s_in, 48)
            pre.link(nc.vector.tensor_scalar(dtf[:, :], dtf[:, :], par[:, 0:1], None, ALU.add))
            nc.vector.scalar_tensor_tensor(tmp[:, :], dtf[:, :], -1.0, dtf[:, :], ALU.mult, ALU.max).then_inc(s_v, 1)
            dve.wait_ge(s_e, 3)
            pre.link(nc.vector.scalar_tensor_tensor(dtf[:, :], dtf[:, :], 0.0, tmp[:, :], ALU.max, ALU.add))
            nc.vector.memset(dtf[:, 0:P - 16], 0.0).then_inc(s_v, 1)
            dve.wait_ge(s_v, 2)
            nc.vector.tensor_scalar(af[:, :], dtf[:, :], par[:, 2:3], -1.0, ALU.mult, ALU.mult).then_inc(s_v, 1)
            dve.wait_ge(s_tr, 2)
            nc.vector.tensor_copy(dt[:, :, :], pA[0][:, 0:NCH * SSD_HEADS].rearrange("p (c h) -> p c h", c=NCH))
            nc.vector.tensor_copy(a[:, :, :], pA[1][:, 0:NCH * SSD_HEADS].rearrange("p (c h) -> p c h", c=NCH)).then_inc(s_dt, 1)
            dve.wait_ge(s_tr, 3)
            pre.link(nc.vector.tensor_copy(cum[:, :, :], pD[:, 0:NCH * SSD_HEADS].rearrange("p (c h) -> p c h", c=NCH)))
            pre.link(nc.vector.tensor_copy(elast[:, :, :], pO[:, 0:NCH * SSD_HEADS].rearrange("p (c h) -> p c h", c=NCH)))
            nc.vector.tensor_tensor(wend[:, :, :], elast[:, :, :], cum[:, :, :], ALU.subtract).then_inc(s_cum, 1)
            dve.wait_ge(s_e, 6)
            dve.wait_ge(s_par, 32)

            def spread(c):
                wait(dve, s_ab, G * c)
                nc.vector.tensor_copy(ab[:, :, :], bc(row(a, c), P)).then_inc(s_abc, 1)

            def output(c):
                wait(dve, s_rms, c + 1)
                y3 = y[:, :, :].rearrange("p (g h) d -> p g (h d)", g=G)
                nc.vector.tensor_tensor(y3, y3, bc(rms[:, :], W), ALU.mult).then_inc(s_n, 1)
                dve.wait_ge(s_n, c + 1)
                nc.vector.tensor_tensor(y3, y3, gn[:, :].rearrange("p (g w) -> p g w", g=G), ALU.mult).then_inc(s_out, 1)

            def chunk(c, b):
                chain.start(c, 4)
                for g in range(G):
                    dve.wait_ge(s_ab, G * c + g + 1)
                    nc.vector.tensor_tensor(seg[g][:, :, :], pA[g][:, :].rearrange("p (h t) -> p h t", h=GH),
                                                       bc(row(cum, c)[:, g * GH:(g + 1) * GH], P), ALU.subtract).then_inc(s_seg, 1)
                if not (isinstance(c, int) and c == 0):
                    output(c - 1)
                dve.wait_ge(s_cb, c + 1)
                nc.vector.tensor_copy(bt[:, :, :], pB[:, 0:G * P].rearrange("p (g n) -> p g n", g=G)).then_inc(s_btc, 1)
                for g in range(G):
                    nc.vector.tensor_tensor(cbm[:, g, :], pB[:, (2 + g) * P:(3 + g) * P], upto, ALU.mult).then_inc(s_cbm, 1)
                dve.wait_ge(s_x, c + 1)
                wait(dve, s_st, c)
                wait(dve, s_yd, c)
                chain.link(nc.vector.tensor_tensor(xdt[:, :, :], x[:, :, :], bc(row(dt, c), HD), ALU.mult))
                nc.vector.tensor_tensor(xw[:, :, :], xdt[:, :, :], bc(row(wend, c), HD), ALU.mult).then_inc(s_xw, 1)
                for g in range(G):
                    dve.wait_ge(s_es, G * c + g + 1)
                    dve.wait_ge(s_cbm, G * c + g + 1)
                    nc.vector.tensor_tensor(seg[g][:, :, :], seg[g][:, :, :],
                                            cbm[:, g:g + 1, :].broadcast_to([P, GH, P]), ALU.mult).then_inc(s_m, 1)
                if not (isinstance(c, int) and c == NCH - 1):
                    spread(c + 1)
                dve.wait_ge(s_yo, c + 1)
                dve.wait_ge(s_yd, c + 1)
                wait(dve, s_left, 16 * (c - 1))
                chain.link(nc.vector.tensor_tensor(y[:, :, :], pO[:, :].rearrange("p (h d) -> p h d", h=SSD_HEADS), bc(row(ecum, c), HD), ALU.mult))
                nc.vector.tensor_tensor(y[:, :, :], y[:, :, :], pD[:, :].rearrange("p (h d) -> p h d", h=SSD_HEADS), ALU.add).then_inc(s_y, 1)
                dve.wait_ge(s_y, c + 1)
                dve.wait_ge(s_yx, c + 1)
                chain.link(nc.vector.tensor_tensor(y[:, :, :], y[:, :, :], yd[:, :, :], ALU.add))
                dve.wait_ge(s_st, c + 1)
                st3 = state[:, :, :].rearrange("p g (h d) -> p (g h) d", d=HD)
                chain.link(nc.vector.tensor_tensor(st3, st3, bc(row(elast, c), HD), ALU.mult))
                nc.vector.tensor_tensor(state[:, :, :], state[:, :, :], pS[:, :].rearrange("p (g w) -> p g w", g=G), ALU.add).then_inc(s_state, 1)
                dve.wait_ge(s_zt, c + 1)
                nc.vector.tensor_tensor(y[:, :, :], y[:, :, :], pX[:, :].rearrange("p (h d) -> p h d", h=SSD_HEADS), ALU.mult).then_inc(s_z, 1)
            spread(0)
            schedule(dve, chunk)
            output(NCH - 1)


LEVELS = 7
LN_TINY = float(np.log(1e-30))


def gated_recurrence(nc, proj, gain, cst, o_cat):
    NL = LEVELS + 1
    with Stage(nc, "hg") as st:
        raw = [st.sb(f"raw{b}", [P, 8, P]) for b in range(2)]
        mag = st.sb("mag", [P, 2, P])
        soft = st.sb("soft", [P, 2, P])
        logf = st.sb("logf", [P, 2, P])
        key = [st.sb(f"key{b}", [P, 2, P]) for b in range(2)]
        cum = st.sb("cum", [P, 2, P])
        ecum = [st.sb(f"ecum{b}", [P, 2, P]) for b in range(2)]
        kend = [st.sb(f"kend{b}", [P, 2, P]) for b in range(2)]
        qe = [st.sb(f"qe{b}", [P, 2, P]) for b in range(2)]
        dist = st.sb("dist", [P, LEVELS, 2, P])
        dq = [st.sb(f"dq{b}", [P, LEVELS, 2, P]) for b in range(2)]
        dk = [st.sb(f"dk{b}", [P, LEVELS, 2, P]) for b in range(2)]
        tm = st.sb("tm", [P, 4, P])
        masked = [st.sb(f"masked{h}", [P, NL, P]) for h in range(2)]
        prob = [[st.sb(f"prob{hp}{h}", [P, P]) for h in range(2)] for hp in range(2)]
        state = st.sb("state", [P, 2, P])
        add = st.sb("add", [P, 2, P])
        o = st.sb("o", [P, 4, HD])
        osq = st.sb("osq", [P, 4, HD])
        ss = st.sb("ss", [P, 4])
        ln = st.sb("ln", [P, 4])
        rr = st.sb("rr", [P, 4])
        gn = st.sb("gn", [P, 4 * HD])
        eps = st.sb("eps", [P, 1])
        one = st.sb("one", [P, P])
        sc = [st.ps(f"sc{h}", [P, NL * P]) for h in range(2)]
        pT = st.ps("pT", [P, HALF])
        pO = [st.ps(f"pO{hp}", [P, HALF]) for hp in range(2)]
        pSG = st.ps("pSG", [P, HALF])
        pS, pG = pSG[:, 0:2 * P], pSG[:, 2 * P:4 * P]
        ident, levels, block64 = cst["ident"], cst["levels"], cst["block64"]
        s_raw = st.sems("raw_s", 2)
        (s_par, s_mag, s_em, s_soft, s_logf, s_lk, s_key, s_cum, s_ecum, s_end, s_kend, s_qe, s_dist, s_ed, s_dq, s_dk, s_tr, s_tm,
         s_sc, s_masked, s_op, s_sp, s_state, s_o, s_ss, s_ln, s_rr, s_gt, s_out, s_left, s_c, s_one, s_kz, s_o2, s_lz, s_used, s_co, s_prob) = (
            st.sem(v) for v in ("par", "mag_s", "em", "soft_s", "logf_s", "lk", "key_s", "cum_s", "ecum_s", "end", "kend_s", "qe_s",
                                "dist_s", "ed", "dq_s", "dk_s", "tr", "tm_s", "sc_s", "masked_s", "op", "sp", "state_s", "o_s", "ss_s", "ln_s",
                                "rr_s", "gt", "out", "left", "chain", "one_s", "kz", "o2", "lz", "used", "chain_o", "prob_s"))
        block = st.block()

        def schedule(eng, turn):
            turn(0, 0)
            turn(1, 1)
            with eng.Fori(1, NCH // 2) as i:
                turn(2 * i, 0)
                turn(2 * i + 1, 1)
            turn(NCH - 1, 0)
            turn(NCH, 1)

        begins = lambda n: isinstance(n, int) and n == 0
        ends = lambda n: isinstance(n, int) and n == NCH
        wide = lambda t: t[:, :, :, :].rearrange("p l h t -> p l (h t)")
        over = lambda t: t.rearrange("p (a h) t -> p a (h t)", a=1).broadcast_to([P, LEVELS, 2 * P])

        @block.sync
        def _(sp):
            sp.dma_start(gn[:, :], bass.AP(gain.tensor, 0, [[0, P], [1, 4 * HD]])).then_inc(s_par, 16)

            def turn(n, b):
                if not ends(n):
                    wait(sp, s_sc, 2 * (n - 1))
                    wait(sp, s_gt, n - 1)
                    wait(sp, s_dq, n - 1)
                    cols = bass.ds(n * P, P)
                    sp.dma_start(raw[b][:, 0:4, :], proj[U_HQ:U_HQ + 4, :, cols].rearrange("u p t -> p u t")).then_inc(s_raw[b], 16)
                    sp.dma_start(raw[b][:, 4:8, :], proj[U_HF:U_HF + 4, :, cols].rearrange("u p t -> p u t")).then_inc(s_raw[b], 16)
                if not (isinstance(n, int) and n < 3):
                    sp.wait_ge(s_out, n - 1)
                    sp.dma_start(o_cat[bass.ds((n - 3) * P, P), 3 * 4 * HD:], o[:, :, :].rearrange("p h d -> p (h d)")).then_inc(s_left, 16)
            turn(0, 0)
            turn(1, 1)
            turn(2, 0)
            turn(3, 1)
            with sp.Fori(2, NCH // 2) as i:
                turn(2 * i, 0)
                turn(2 * i + 1, 1)
            turn(NCH - 1, 0)
            turn(NCH, 1)
            sp.wait_ge(s_out, NCH)
            sp.dma_start(o_cat[(NCH - 2) * P:(NCH - 1) * P, 3 * 4 * HD:], o[:, :, :].rearrange("p h d -> p (h d)")).then_inc(s_left, 16)
            sp.wait_ge(s_left, 16 * (NCH - 1))

        @block.scalar
        def _(act):
            nc.scalar.preload_act_table_set(EXP_LN)
            act.wait_ge(s_one, 1)

            def turn(n, b):
                if not ends(n):
                    act.wait_ge(s_raw[b], 16 * (n - b) + 32)
                    nc.scalar.activation(mag[:, :, :], raw[b][:, 4:6, :], ACT.Abs).then_inc(s_mag, 1)
                    act.wait_ge(s_mag, n + 1)
                    nc.scalar.activation(mag[:, :, :], mag[:, :, :], ACT.Exp, scale=-1.0).then_inc(s_em, 1)
                    act.wait_ge(s_em, n + 1)
                    wait(act, s_cum, n)
                    nc.scalar.activation(soft[:, :, :], mag[:, :, :], ACT.Ln, bias=1.0).then_inc(s_soft, 1)
                if not begins(n):
                    act.wait_ge(s_tr, n)
                    wait(act, s_op, 2 * (n - 1))
                    nc.scalar.activation(tm[:, :, :], pT[:, :].rearrange("p (u t) -> p u t", u=4), ACT.Copy).then_inc(s_tm, 1)
                if not ends(n):
                    act.wait_ge(s_lk, n + 1)
                    nc.scalar.activation(key[b][:, :, :], key[b][:, :, :], ACT.Exp, scale=-1.0).then_inc(s_key, 1)
                    act.wait_ge(s_cum, n + 1)
                    wait(act, s_state, n)
                    nc.scalar.activation(ecum[b][:, :, :], cum[:, :, :], ACT.Exp).then_inc(s_ecum, 1)
                    wait(act, s_tr, n - 1)
                    for hp in range(2):
                        last = nc.scalar.activation(kend[b][:, hp, :], cum[:, hp, :], ACT.Exp, scale=-1.0, bias=cum[:, hp, P - 1:P])
                    last.then_inc(s_end, 1)
                    act.wait_ge(s_dist, n + 1)
                    nc.scalar.activation(dist[:, :, :, :], dist[:, :, :, :], ACT.Exp).then_inc(s_ed, 1)
                if not begins(n):
                    act.wait_ge(s_ss, n)
                    nc.scalar.activation(ln[:, :], ss[:, :], ACT.Ln, scale=1.0 / HD, bias=eps[:, :]).then_inc(s_ln, 1)
                    act.wait_ge(s_ln, n)
                    nc.scalar.activation(rr[:, :], ln[:, :], ACT.Exp, scale=-0.5).then_inc(s_rr, 1)
            schedule(act, turn)

        @block.gpsimd
        def _(pool):
            def turn(n, b):
                if ends(n):
                    return
                pool.wait_ge(s_ed, n + 1)
                pool.wait_ge(s_key, n + 1)
                if begins(n):
                    pool.wait_ge(s_kz, 1)
                wait(pool, s_sc, 2 * (n - 1))
                nc.gpsimd.tensor_tensor(wide(dk[b]), wide(dist), over(key[b][:, :, :]), ALU.mult).then_inc(s_dk, 1)
            schedule(pool, turn)

        @block.tensor
        def _(pe):
            def scores(c, b, hp):
                wait(pe, s_masked, 4 * c + 2 * hp)
                for l in range(NL):
                    for h in range(2):
                        hs = slice(64 * h, 64 * h + 64)
                        k_l = dk[b][hs, l, hp, :] if l < LEVELS else key[b][hs, hp, :]
                        q_l = dq[b][hs, l, hp, :] if l < LEVELS else raw[b][hs, hp, :]
                        last = nc.tensor.matmul(sc[h][:, l * P:l * P + P], k_l, q_l, start=True, stop=True)
                last.then_inc(s_sc, 1)

            def values(c, hp):
                for h in range(2):
                    pe.wait_ge(s_prob, 4 * c + 2 * hp + h + 1)
                    last = nc.tensor.matmul(pO[hp][:, h * HD:(h + 1) * HD], prob[hp][h][:, :],
                                            tm[:, 2 + hp, h * HD:(h + 1) * HD], start=False, stop=True, skip_group_check=True)
                last.then_inc(s_op, 1)

            def turn(n, b):
                if begins(n):
                    return
                c, b = n - 1, 1 - b
                pe.wait_ge(s_dq, c + 1)
                pe.wait_ge(s_dk, c + 1)
                scores(c, b, 0)
                pe.wait_ge(s_kend, c + 1)
                wait(pe, s_tm, c)
                for u in range(2):
                    nc.tensor.transpose(pT[:, u * P:u * P + P], kend[b][:, u, :], ident)
                for u in range(2):
                    last = nc.tensor.transpose(pT[:, (2 + u) * P:(3 + u) * P], raw[b][:, 6 + u, :], ident)
                last.then_inc(s_tr, 1)
                wait(pe, s_o, c)
                pe.wait_ge(s_qe, c + 1)
                pe.wait_ge(s_state, c + 1)
                for hp in range(2):
                    last = nc.tensor.matmul(pO[hp][:, 0:P], qe[b][:, hp, :], state[:, hp, :], start=True, stop=False, skip_group_check=True)
                last.then_inc(s_used, 1)
                scores(c, b, 1)
                wait(pe, s_out, c)
                for u in range(2):
                    last = nc.tensor.transpose(pG[:, u * P:u * P + P], raw[b][:, 2 + u, :], ident)
                last.then_inc(s_gt, 1)
                pe.wait_ge(s_tm, c + 1)
                for hp in range(2):
                    last = nc.tensor.matmul(pS[:, hp * P:hp * P + P], tm[:, hp, :], tm[:, 2 + hp, :], start=True, stop=True)
                last.then_inc(s_sp, 1)
                values(c, 0)
                values(c, 1)
            schedule(pe, turn)

        @block.vector
        def _(dve):
            chain, chain_o = Chain(dve, s_c), Chain(dve, s_co)
            nc.vector.memset(eps[:, :], EPS)
            nc.vector.memset(state[:, :, :], 0.0).then_inc(s_state, 1)
            nc.vector.memset(one[:, :], 1.0).then_inc(s_one, 1)
            dve.wait_ge(s_one, 1)
            dve.wait_ge(s_par, 16)

            def sums(n, b):
                chain.start(n, 2)
                dve.wait_ge(s_soft, n + 1)
                wait(dve, s_sc, 2 * (n - 1))
                wait(dve, s_end, n)
                nc.vector.scalar_tensor_tensor(key[b][:, :, :], raw[b][:, 4:6, :], 0.0, soft[:, :, :], ALU.max, ALU.add).then_inc(s_lk, 1)
                chain.link(nc.vector.scalar_tensor_tensor(logf[:, :, :], raw[b][:, 4:6, :], 0.0, soft[:, :, :], ALU.min, ALU.subtract))
                chain.link(nc.vector.tensor_scalar(logf[:, :, :], logf[:, :, :], LN_TINY, None, ALU.max))
                if begins(n):
                    nc.vector.memset(logf[:, :, 0:P - 16], 0.0).then_inc(s_lz, 1)
                    dve.wait_ge(s_lz, 1)
                for hp in range(2):
                    last = nc.vector.tensor_tensor_scan(cum[:, hp, :], one[:, :], logf[:, hp, :], 0.0, ALU.mult, ALU.add)
                last.then_inc(s_cum, 1)

            def distances(n):
                dve.wait_ge(s_cum, n + 1)
                wait(dve, s_dk, n)
                flat = cum[:, :, :].rearrange("p h t -> p (h t)")
                for l in range(LEVELS):
                    B = 2 << l
                    half = B // 2
                    src = flat.rearrange("p (n b) -> p n b", b=B)
                    dst = dist[:, l, :, :].rearrange("p h t -> p (h t)").rearrange("p (n b) -> p n b", b=B)
                    ref = src[:, :, half - 1:half].broadcast_to([P, 2 * P // B, half])
                    nc.vector.tensor_tensor(dst[:, :, 0:half], ref, src[:, :, 0:half], ALU.subtract)
                    last = nc.vector.tensor_tensor(dst[:, :, half:B], src[:, :, half:B], ref, ALU.subtract)
                last.then_inc(s_dist, 1)

            def ends_of_keys(n, b):
                dve.wait_ge(s_key, n + 1)
                if begins(n):
                    nc.vector.memset(key[b][:, :, 0:P - 16], 0.0).then_inc(s_kz, 1)
                    dve.wait_ge(s_kz, 1)
                dve.wait_ge(s_end, n + 1)
                nc.vector.tensor_tensor(kend[b][:, :, :], kend[b][:, :, :], key[b][:, :, :], ALU.mult).then_inc(s_kend, 1)
                wait(dve, s_used, n - 1)
                nc.vector.tensor_tensor(qe[b][:, :, :], ecum[b][:, :, :], raw[b][:, 0:2, :], ALU.mult).then_inc(s_qe, 1)

            def queries(n, b):
                dve.wait_ge(s_ed, n + 1)
                nc.vector.tensor_tensor(wide(dq[b]), wide(dist), over(raw[b][:, 0:2, :]), ALU.mult).then_inc(s_dq, 1)

            def mask(c, hp):
                dve.wait_ge(s_sc, 2 * c + hp + 1)
                wait(dve, s_prob, 4 * c + 2 * hp)
                for h in range(2):
                    nc.vector.tensor_tensor(masked[h][:, :, :], sc[h][:, :].rearrange("p (l t) -> p l t", l=NL),
                                            levels.rearrange("p (l t) -> p l t", l=NL), ALU.mult).then_inc(s_masked, 1)
                wait(dve, s_op, 2 * c - 1 + hp)
                for h in range(2):
                    dve.wait_ge(s_masked, 4 * c + 2 * hp + h + 1)
                    nc.vector.tensor_reduce(prob[hp][h][:, :], masked[h][:, :, :].rearrange("p l t -> p t l"), AX.X, ALU.add).then_inc(s_prob, 1)

            def new_state(c, b):
                chain_o.start(c, 2)
                dve.wait_ge(s_sp, c + 1)
                dve.wait_ge(s_used, c + 1)
                chain_o.link(nc.vector.tensor_tensor(add[:, :, :], pS[:, 0:2 * P].rearrange("p (h t) -> p h t", h=2),
                                                     block64.rearrange("p (a t) -> p a t", a=1).broadcast_to([P, 2, P]), ALU.mult))
                for hp in range(2):
                    last = nc.vector.scalar_tensor_tensor(state[:, hp, :], state[:, hp, :], ecum[b][:, hp, P - 1:P], add[:, hp, :], ALU.mult, ALU.add)
                last.then_inc(s_state, 1)

            def squares(c):
                dve.wait_ge(s_op, 2 * c + 2)
                wait(dve, s_left, 16 * (c - 1))
                for hp in range(2):
                    last = nc.vector.tensor_copy(o[:, 2 * hp:2 * hp + 2, :], pO[hp][:, 0:P].rearrange("p (h d) -> p h d", d=HD))
                last.then_inc(s_o, 1)
                dve.wait_ge(s_o, c + 1)
                chain_o.link(nc.vector.tensor_tensor(osq[:, :, :], o[:, :, :], o[:, :, :], ALU.mult))
                nc.vector.tensor_reduce(ss[:, :], osq[:, :, :], AX.X, ALU.add).then_inc(s_ss, 1)

            def output(c):
                dve.wait_ge(s_rr, c + 1)
                nc.vector.tensor_tensor(o[:, :, :], o[:, :, :], rr[:, :].rearrange("p (h a) -> p h a", a=1).broadcast_to([P, 4, HD]), ALU.mult).then_inc(s_o2, 1)
                dve.wait_ge(s_o2, 2 * c + 1)
                nc.vector.tensor_tensor(o[:, :, :], o[:, :, :], gn[:, :].rearrange("p (h d) -> p h d", d=HD), ALU.mult).then_inc(s_o2, 1)
                dve.wait_ge(s_o2, 2 * c + 2)
                dve.wait_ge(s_gt, c + 1)
                nc.vector.tensor_tensor(o[:, :, :], o[:, :, :], pG[:, 0:2 * P].rearrange("p (h d) -> p h d", d=HD), ALU.mult).then_inc(s_out, 1)

            def turn(n, b):
                new, old, c = not ends(n), not begins(n), n - 1
                if new:
                    sums(n, b)
                if old:
                    mask(c, 0)
                if new:
                    distances(n)
                if old:
                    mask(c, 1)
                if new:
                    ends_of_keys(n, b)
                if old:
                    new_state(c, 1 - b)
                if new:
                    queries(n, b)
                if old:
                    squares(c)
                    output(c)
            schedule(dve, turn)

def mixers_output(nc, hi, lo, w_out, o_cat, ident, x):
    tiles = T // P
    pairs = KT // 2
    with Stage(nc, "mo") as st:
        w = Weights(st, w_out)
        o = [st.sb(f"o{b}", [P, D]) for b in range(2)]
        f = [st.sb(f"f{b}", [P, HALF]) for b in range(2)]
        z = [[st.ps(f"z{b}{h}", [P, HALF]) for h in range(2)] for b in range(2)]
        tr = [st.ps(f"tr{h}", [P, HALF]) for h in range(2)]
        s_o, s_added = st.sems("o_s", 2), st.sems("added", 2)
        s_tr, s_f, s_hi, s_lo = (st.sem(v) for v in ("tr_s", "f_s", "hi_s", "lo_s"))
        block = st.block()

        @block.sync
        def _(sp):
            for b in range(2):
                w.load(sp, b, 0, b)
            for m in range(tiles):
                wait(sp, s_tr, 2 * (m - 1))
                sp.dma_start(o[m % 2][:, :], o_cat[m * P:(m + 1) * P, :]).then_inc(s_o[m % 2], 16)

            def out(i):
                for b in range(2):
                    w.load(sp, b, i, 2 * i + b)
            with sp.Fori(1, pairs) as i:
                out(i)

        @block.scalar
        def _(act):
            w.split_hi(act, 0, 0)
            w.split_hi(act, 1, 0)
            for n in range(2 * tiles):
                m, c = n // 2, n % 2
                act.wait_ge(s_tr, n + 1)
                wait(act, s_lo, n - 1)
                nc.scalar.activation(f[c][:, :], tr[c][:, :], ACT.Copy).then_inc(s_f, 1)
                act.wait_ge(s_f, n + 1)
                nc.scalar.activation(hi[:, 4 * c:4 * c + 4, m * P:m * P + P], f[c][:, :].rearrange("p (k t) -> p k t", k=4), ACT.Copy).then_inc(s_hi, 1)
            with act.Fori(1, pairs) as i:
                for b in range(2):
                    w.split_hi(act, b, i)

        @block.tensor
        def _(pe):
            for n in range(2 * tiles):
                m, c = n // 2, n % 2
                pe.wait_ge(s_o[m % 2], 16 * (m // 2) + 16)
                wait(pe, s_f, n - 1)
                for k in range(4):
                    last = nc.tensor.transpose(tr[c][:, k * P:k * P + P], o[m % 2][:, (4 * c + k) * P:(4 * c + k + 1) * P], ident)
                last.then_inc(s_tr, 1)
            pe.wait_ge(s_lo, 2 * tiles)

            def out(i):
                for b in range(2):
                    pe.wait_ge(w.lo_done[b], i + 1)
                    wait(pe, s_added[b], i)
                    for h in range(2):
                        last = w.products(z[b][h][:, :], b, hi, lo, slice(h * HALF, h * HALF + HALF))
                    last.then_inc(w.multiplied[b], 1)
            repeat(pe, pairs, out)

        @block.vector
        def _(dve):
            w.split_lo(dve, 0, 0)
            w.split_lo(dve, 1, 0)
            for n in range(2 * tiles):
                m, c = n // 2, n % 2
                dve.wait_ge(s_hi, n + 1)
                at = (slice(None), slice(4 * c, 4 * c + 4), slice(m * P, m * P + P))
                nc.vector.tensor_tensor(lo[at], f[c][:, :].rearrange("p (k t) -> p k t", k=4), hi[at].bitcast(F32), ALU.subtract).then_inc(s_lo, 1)

            def out(i):
                for b in range(2):
                    dve.wait_ge(w.multiplied[b], i + 1)
                    for h in range(2):
                        dst = x[:, bass.ds(2 * i + b, 1), h * HALF:h * HALF + HALF].rearrange("p a t -> p (a t)")
                        last = nc.vector.tensor_tensor(dst, dst, z[b][h][:, :], ALU.add)
                    last.then_inc(s_added[b], 1)
                    if not (isinstance(i, int) and i == pairs - 1):
                        w.split_lo(dve, b, i + 1)
            repeat(dve, pairs, out)


def mlp(nc, hi, lo, w, x):
    quarters, pairs = 4, KT // 2
    with Stage(nc, "mlp") as st:
        h_hi = st.sb("h_hi", [P, KT, T], F32R)
        h_lo = st.sb("h_lo", [P, KT, T], F32R)
        r = [st.sb(f"r{b}", [P, T]) for b in range(2)]
        y = [st.sb(f"y{b}", [P, T]) for b in range(2)]
        z = [[st.ps(f"z{b}{h}", [P, HALF]) for h in range(2)] for b in range(2)]
        s_r, s_y, s_hi, s_lo, s_added = (st.sems(v, 2) for v in ("r_s", "y_s", "hi_s", "lo_s", "added"))
        block = st.block()
        total = 2 * quarters * pairs
        done = lambda i, qr, part: qr * 2 * pairs + part * pairs + i

        def schedule(eng, up, down):
            for qr in range(quarters):
                repeat(eng, pairs, lambda i: up(qr, i))
                repeat(eng, pairs, lambda i: down(qr, i))

        @block.sync
        def _(sp):
            def up(qr, i):
                for b in range(2):
                    w.load(sp, b, done(i, qr, 0), 2 * done(i, qr, 0) + b)

            def down(qr, i):
                for b in range(2):
                    w.load(sp, b, done(i, qr, 1), 2 * done(i, qr, 1) + b)
            schedule(sp, up, down)

        @block.scalar
        def _(act):
            w.split_hi(act, 0, 0)

            def ahead(n, b):
                if b == 0 or not (isinstance(n, int) and n == total - 1):
                    w.split_hi(act, 1 - b, n + b)

            def up(qr, i):
                n, j = done(i, qr, 0), qr * pairs + i
                for b in range(2):
                    ahead(n, b)
                    act.wait_ge(w.multiplied[b], n + 1)
                    wait(act, s_y[b], j)
                    for h in range(2):
                        hs = slice(h * HALF, h * HALF + HALF)
                        last = nc.scalar.activation(r[b][:, hs], z[b][h][:, :], ACT.Relu)
                    last.then_inc(s_r[b], 1)
                    act.wait_ge(s_y[b], j + 1)
                    nc.scalar.activation(h_hi[:, bass.ds(2 * i + b, 1), :].rearrange("p a t -> p (a t)"), y[b][:, :], ACT.Copy).then_inc(s_hi[b], 1)

            def down(qr, i):
                for b in range(2):
                    ahead(done(i, qr, 1), b)
            schedule(act, up, down)

        @block.tensor
        def _(pe):
            def unit(n, b, a_hi, a_lo):
                pe.wait_ge(w.lo_done[b], n + 1)
                for h in range(2):
                    last = w.products(z[b][h][:, :], b, a_hi, a_lo, slice(h * HALF, h * HALF + HALF))
                last.then_inc(w.multiplied[b], 1)

            def up(qr, i):
                for b in range(2):
                    wait(pe, s_y[b], qr * pairs + i)
                    wait(pe, s_added[b], qr * pairs)
                    unit(done(i, qr, 0), b, hi, lo)

            def down(qr, i):
                for b in range(2):
                    for c in range(2):
                        pe.wait_ge(s_lo[c], (qr + 1) * pairs)
                    wait(pe, s_added[b], qr * pairs + i)
                    unit(done(i, qr, 1), b, h_hi, h_lo)
            schedule(pe, up, down)

        @block.vector
        def _(dve):
            w.split_lo(dve, 0, 0)

            def ahead(n, b):
                if b == 0 or not (isinstance(n, int) and n == total - 1):
                    w.split_lo(dve, 1 - b, n + b)

            def up(qr, i):
                n, j = done(i, qr, 0), qr * pairs + i
                for b in range(2):
                    ahead(n, b)
                    dve.wait_ge(s_r[b], j + 1)
                    wait(dve, s_hi[b], j)
                    for h in range(2):
                        hs = slice(h * HALF, h * HALF + HALF)
                        last = nc.vector.tensor_tensor(y[b][:, hs], r[b][:, hs], z[b][h][:, :], ALU.mult)
                    last.then_inc(s_y[b], 1)
                    dve.wait_ge(s_hi[b], j + 1)
                    at = h_hi[:, bass.ds(2 * i + b, 1), :].rearrange("p a t -> p (a t)").bitcast(F32)
                    nc.vector.tensor_tensor(h_lo[:, bass.ds(2 * i + b, 1), :].rearrange("p a t -> p (a t)"), y[b][:, :], at,
                                            ALU.subtract).then_inc(s_lo[b], 1)

            def down(qr, i):
                n = done(i, qr, 1)
                for b in range(2):
                    ahead(n, b)
                    dve.wait_ge(w.multiplied[b], n + 1)
                    for h in range(2):
                        dst = x[:, bass.ds(2 * i + b, 1), h * HALF:h * HALF + HALF].rearrange("p a t -> p (a t)")
                        last = nc.vector.tensor_tensor(dst, dst, z[b][h][:, :], ALU.add)
                    last.then_inc(s_added[b], 1)
            schedule(dve, up, down)


def move(nc, name, pairs):
    with Stage(nc, name) as st:
        s = st.sem("moved")
        block = st.block()

        @block.sync
        def _(sp):
            for to, frm in pairs:
                sp.dma_start(to, frm).then_inc(s, 16)
            sp.wait_ge(s, 16 * len(pairs))


def constants():
    i, j = np.arange(P)[:, None], np.arange(P)[None, :]
    meta = P - 16
    parts = {
        "ident": i == j,
        "ones": (i >= 0) & (j >= 0),
        "suffix": i >= j,
        "before": i < j,
        "not_before": np.where(i < j, 0, -1e30),
        "block64": i // 64 == j // 64,
        "upto": i <= j,
        "row_ok": i >= meta,
        "row_neg": np.where(i >= meta, 0, -1e30),
        "levels": np.concatenate([(i // B == j // B) & (i % B < B // 2) & (j % B >= B // 2)
                                  for B in (2 << l for l in range(LEVELS))] + [i == j], 1),
    }
    where, at = {}, 0
    for name, m in parts.items():
        where[name] = (at, m.shape[1])
        at += m.shape[1]
    return np.concatenate([m.astype(np.float32) for m in parts.values()], 1), where


def bucket_tables():
    hot = np.zeros((REL_BUCKETS, len(GROUPS) * VEC), np.float32)
    far = np.full((B_HEADS, len(GROUPS) * VEC), FAR, np.float32)
    half, exact = REL_BUCKETS // 2, 8
    for g, (d, _) in enumerate(GROUPS):
        for e in range(VEC):
            rel = e - 191
            if abs(rel) > WINDOW:
                continue
            n = abs(rel * d)
            large = exact + int(np.float32(np.log(np.float32(max(n, 1)) / np.float32(exact))) / np.float32(np.log(1024 / exact)) * np.float32(half - exact))
            hot[(half if rel > 0 else 0) + (n if n < exact else min(large, half - 1)), g * VEC + e] = 1.0
            far[:, g * VEC + e] = 0.0
    return hot, far


def build(nc, a, out):
    vhat = nc.dram_tensor("vhat", [A_HEADS, P, KT, P], F32).ap()
    vecs = nc.dram_tensor("vecs", [len(GROUPS) * B_HEADS, VEC], F32).ap()
    tiles = nc.dram_tensor("bias_tiles", [len(GROUPS) * B_HEADS, P, 2 * P], F32).ap()
    o_dram = nc.dram_tensor("o_groups", [len(GROUPS), T, D], F32).ap()
    lse_dram = nc.dram_tensor("lse_groups", [len(GROUPS), T, B_HEADS], F32).ap()
    proj = nc.dram_tensor("proj", [N_UNITS, P, L2], F32).ap()
    conv = nc.dram_tensor("conv", [8, P, L2], F32).ap()
    o_cat = nc.dram_tensor("o_cat", [T, D], F32).ap()
    x_dram = nc.dram_tensor("x_kept", [2, P, KT, T], F32).ap()
    where = constants()[1]
    late = where["suffix"][0]
    total = sum(n for _, n in where.values())
    with Stage(nc, "all") as top:
        ident = top.sb("ident", [P, P])[:, :]
        ones = top.sb("ones", [P, P])[:, :]
        with Stage(nc, "ab") as ab:
            hi = ab.sb("hi", [P, KT, T], F32R)
            lo = ab.sb("lo", [P, KT, T], F32R)
            with Stage(nc, "wv") as ws:
                w = Weights(ws, a["w_v"], ahead=True)
                with Stage(nc, "x0") as st:
                    x = st.sb("x", [P, KT, T])
                    move(nc, "load0", [(x[:, :, :], a["x"]), (ident, a["cst"][:, 0:P]), (ones, a["cst"][:, P:2 * P])])
                    norm_stage(nc, "n0", x, a["pre0"], ones, hi, lo, T, w=w)
                gmlp_values(nc, hi, lo, w, vhat, ident)
            with Stage(nc, "r0") as st:
                yo = st.sb("yo", [P, KT, T])
                gmlp_gate(nc, hi, lo, a["w_ug"], vhat, a["ws_t"], a["b_s"], a["ln_g"], a["ln_b"], yo)
                x = st.sb("x", [P, KT, T])
                norm_stage(nc, "n1", x, a["pre1"], ones, hi, lo, T, post=yo, post_gain=a["post0"], x_from=a["x"], x_to=x_dram[0])
            bias_vectors(nc, a["rel_bias"], a["hot"], a["far"], vecs, tiles)
            dilated_attention(nc, hi, lo, a["w_qkv"], tiles, o_dram, lse_dram, ident)
            with Stage(nc, "r1") as st:
                yo = st.sb("yo", [P, KT, T])
                attention_output(nc, hi, lo, a["w_bo"], o_dram, lse_dram, ident, yo)
                x = st.sb("x", [P, KT, T])
                norm_stage(nc, "n2", x, None, ones, None, None, T, post=yo, post_gain=a["post1"], x_from=x_dram[0], x_to=x_dram[1])
        x = top.sb("x", [P, KT, T])
        with Stage(nc, "three") as st:
            hi = st.sb("hi", [P, KT, L2], F32R)
            lo = st.sb("lo", [P, KT, L2], F32R)
            with Stage(nc, "lead") as ld:
                lead = ld.sb("lead", [P, KT, P])
                move(nc, "load2", [(lead[:, :, :], a["lead"])])
                norm_stage(nc, "n3", lead, a["pre2"], ones, hi, lo, P, copies=[(x[:, :, :], x_dram[1])])
            w = Weights(st, a["w_in2"], buffers=3, ahead=True)
            norm_stage(nc, "n5", x, a["pre2"], ones, hi, lo, T, col0=P, w=w)
            second_projection(nc, hi, lo, w, proj)
        with Stage(nc, "mixers") as st:
            c = st.sb("cst", [P, total - late])
            cst = {name: c[:, at - late:at - late + n] for name, (at, n) in where.items() if at >= late}
            cst.update(ident=ident, ones=ones)
            move(nc, "load4", [(c[:, :], a["cst"][:, late:total])])
            stick_breaking(nc, proj, a["q_gain"], a["k_gain"], a["sb_gain"], cst, o_cat, a["conv_w"], a["conv_b"], conv)
            ssd(nc, proj, conv, a["dt_bias"], a["a_log"], a["d_skip"], a["ssd_gain"], cst, o_cat)
            gated_recurrence(nc, proj, a["hg_gain"], cst, o_cat)
        hi = top.sb("hi", [P, KT, T], F32R)
        lo = top.sb("lo", [P, KT, T], F32R)
        mixers_output(nc, hi, lo, a["w_out2"], o_cat, ident, x)
        with Stage(nc, "wm") as ws:
            w = Weights(ws, a["w_mlp"], ahead=True)
            norm_stage(nc, "n4", x, a["pre3"], ones, hi, lo, T, w=w)
            mlp(nc, hi, lo, w, x)
        move(nc, "store", [(out, x[:, :, :])])


def units(w):
    k, n = w.shape
    return w.reshape(k // P, P, n // P, P).transpose(2, 1, 0, 3).reshape(n // P, P, (k // P) * P)


def by_feature(x):
    return x.T.reshape(-1, P, x.shape[0]).transpose(1, 0, 2)


def vector(g):
    return g.reshape(-1, P).T


def layout(v):
    aw, bw, w2 = v["a_w_in"][0], v["b_w_in"][0], v["w_in_2"][0]
    u, g = units(aw[:, :2 * D]), units(aw[:, 4 * D:])
    ug = []
    for hf in range(2):
        for j in range(A_HEADS // 2):
            ug += [u[hf * 8 + j:hf * 8 + j + 1], g[hf * 8 + j:hf * 8 + j + 1]]
        ug.append(units(v["a_w_out"][0][hf * D:(hf + 1) * D]))
    qkv = []
    for gi in range(len(GROUPS)):
        three = [units(bw[:, (3 * gi + j) * D:(3 * gi + j + 1) * D]) for j in range(3)]
        for hp in range(B_PAIRS):
            qkv += [t[hp:hp + 1] for t in three]
    cut = np.cumsum([256, 256, 256, 512, 512, 256, 256, 8, 256, 256, 256])
    q, k, vv, z, xs, bm, cm, dt, hq, hf_, hi_, hg = np.split(w2, cut, axis=1)
    dt = np.concatenate([dt, np.zeros((D, P - 8), np.float32)], 1)
    in2 = units(np.concatenate([z, hq, hg, q, k, vv, xs, bm, cm, dt, hf_, hi_], 1))
    up = units(v["w_up_2"][0])
    mlp_w = []
    for qr in range(4):
        mlp_w += [up[8 * qr:8 * qr + 8], units(v["w_down_2"][0][qr * D:(qr + 1) * D])]
    lead = np.concatenate([np.zeros((P - 16, D), np.float32), v["meta_tokens_2"]], 0)
    hot, far = bucket_tables()
    return {
        "x": by_feature(v["x"][0]), "cst": constants()[0], "hot": hot, "far": far, "lead": by_feature(lead),
        "pre0": vector(v["norm_pre"][0]), "pre1": vector(v["norm_pre"][1]),
        "post0": vector(v["norm_post"][0]), "post1": vector(v["norm_post"][1]),
        "pre2": vector(v["norm_mix_w_2"][0]), "pre3": vector(v["norm_mlp_w_2"][0]),
        "w_v": units(aw[:, 2 * D:4 * D]), "w_ug": np.concatenate(ug), "ws_t": v["a_w_s"][0].transpose(0, 2, 1),
        "b_s": v["a_b_s"][0], "ln_g": v["a_vnorm_g"][0], "ln_b": v["a_vnorm_b"][0],
        "rel_bias": v["rel_bias"], "w_qkv": np.concatenate(qkv),
        "w_bo": np.concatenate([units(bw[:, 9 * D:]), units(v["b_w_out"][0])]),
        "w_in2": in2, "q_gain": v["sb_q_norm_2"].T, "k_gain": v["sb_k_norm_2"].T, "sb_gain": v["sb_out_norm_2"][0],
        "conv_w": v["ssd_conv_w_2"][0].reshape(TAPS, 8, P).transpose(2, 1, 0), "conv_b": vector(v["ssd_conv_b_2"][0]),
        "dt_bias": v["ssd_dt_bias_2"].T, "a_log": v["ssd_A_log_2"].T, "d_skip": v["ssd_D_2"][0],
        "ssd_gain": v["ssd_norm_w_2"][0], "hg_gain": v["hg_out_norm_2"][0],
        "w_out2": units(v["w_out_2"][0]), "w_mlp": np.concatenate(mlp_w),
    }


def kernel(**inputs):
    import numpy as _np
    import concourse.bacc as _bacc
    from concourse.bass_utils import run_bass_kernel_spmd as _run

    nc = _bacc.Bacc("TRN2", target_bir_lowering=False, num_devices=1)
    arrays, aps = {}, {}
    for name, a in layout({n: _np.asarray(v) for n, v in inputs.items()}).items():
        arrays[f"in_{name}"] = _np.ascontiguousarray(a)
        aps[name] = nc.dram_tensor(f"in_{name}", a.shape, F32, kind="ExternalInput").ap()
    out = nc.dram_tensor("out", [P, KT, T], F32, kind="ExternalOutput").ap()
    build(nc, aps, out)
    r = _run(nc, [arrays], core_ids=[0])
    y = r.results[0]["out"]
    return _np.ascontiguousarray(y.transpose(1, 0, 2).reshape(D, T).T).reshape(1, T, D)
```
